# Optimizing a Trainium2 kernel written in Bass

```python
import math
import jax, jax.numpy as jnp
from jax import lax
import numpy as np

D_MODEL = 2048
BATCH = 1
SEQ = 128
DEPTH = 1
DEC_BATCH = 1
DEC_SEQ = 512
PAST_LEN = 128

GRID_W = 64
NA_HEADS = 8
NA_HEAD_DIM = 64
NA_WIDTH = NA_HEADS * NA_HEAD_DIM
NA_WIN_ROWS = 8
NA_WIN_COLS = 16
SG_GROUPS = 4
SG_GROUP_DIM = 128
SG_WIDTH = SG_GROUPS * SG_GROUP_DIM
SG_CHUNK = 128
RW_HEADS = 16
RW_HEAD_DIM = 64
RW_WIDTH = RW_HEADS * RW_HEAD_DIM
DECAY_LORA = 64
AAA_LORA = 64
GATE_LORA = 128
N_EXPERTS = 16
D_EXPERT = 1024
CAPACITY_FACTOR = 2
N_MOD = 6
NORM_EPS = 1e-6
GN_EPS = 64e-5
IN_COLS = 3 * NA_WIDTH + 2 * SG_WIDTH + 3 * RW_WIDTH + DECAY_LORA + AAA_LORA + GATE_LORA

kernel_name = 'hybrid_diffusion_natten_sgu_rwkv7_ec_step'

def rms_norm(x, g):
    xf = x.astype(jnp.float32)
    y = xf * lax.rsqrt(jnp.mean(xf * xf, axis=-1, keepdims=True) + NORM_EPS)
    return (y * g.astype(jnp.float32)).astype(x.dtype)

def modulation(cond, w_ada, b_ada):
    m = jax.nn.silu(cond) @ w_ada + b_ada
    return jnp.split(m[..., None, :], N_MOD, axis=-1)

def split_proj(z):
    sizes = (NA_WIDTH, NA_WIDTH, NA_WIDTH, SG_WIDTH, SG_WIDTH, RW_WIDTH, RW_WIDTH, RW_WIDTH,
             DECAY_LORA, AAA_LORA, GATE_LORA)
    cuts, acc = [], 0
    for s in sizes[:-1]:
        acc += s
        cuts.append(acc)
    return jnp.split(z, cuts, axis=-1)

def na_context(q, k, v):
    s = jnp.einsum('bqhd,bkhd->bhqk', q * NA_HEAD_DIM ** -0.5, k).astype(jnp.float32)
    p = jax.nn.softmax(s, axis=-1).astype(v.dtype)
    return jnp.einsum('bhqk,bkhd->bqhd', p, v)

def na_latent(q, k, v, k_ctx, v_ctx, rpb):
    B, T, H, dh = q.shape
    rows = T // GRID_W
    kr = min(NA_WIN_ROWS, rows)
    kc = NA_WIN_COLS
    qg = (q * NA_HEAD_DIM ** -0.5).reshape(B, rows, GRID_W, H, dh)
    kg = k.reshape(B, rows, GRID_W, H, dh)
    vg = v.reshape(B, rows, GRID_W, H, dh)
    cols = jnp.arange(GRID_W)
    col_idx = jnp.clip(cols - kc // 2, 0, GRID_W - kc)[:, None] + jnp.arange(kc)
    col_off = col_idx - cols[:, None] + (NA_WIN_COLS - 1)
    rpb = rpb.astype(jnp.float32)

    def row_fn(r):
        r0 = jnp.clip(r - kr // 2, 0, rows - kr)
        q_r = lax.dynamic_index_in_dim(qg, r, axis=1, keepdims=False)
        k_win = lax.dynamic_slice_in_dim(kg, r0, kr, axis=1)[:, :, col_idx]
        v_win = lax.dynamic_slice_in_dim(vg, r0, kr, axis=1)[:, :, col_idx]
        row_off = r0 + jnp.arange(kr) - r + (NA_WIN_ROWS - 1)
        bias = rpb[:, row_off][:, :, col_off].transpose(0, 2, 1, 3)
        s_loc = jnp.einsum('bqhd,brqchd->bhqrc', q_r, k_win).astype(jnp.float32) + bias[None]
        s_loc = s_loc.reshape(B, H, GRID_W, kr * kc)
        s_ctx = jnp.einsum('bqhd,bkhd->bhqk', q_r, k_ctx).astype(jnp.float32)
        p = jax.nn.softmax(jnp.concatenate([s_loc, s_ctx], axis=-1), axis=-1).astype(v.dtype)
        p_loc = p[..., :kr * kc].reshape(B, H, GRID_W, kr, kc)
        p_ctx = p[..., kr * kc:]
        return (jnp.einsum('bhqrc,brqchd->bqhd', p_loc, v_win)
                + jnp.einsum('bhqk,bkhd->bqhd', p_ctx, v_ctx))

    out = lax.map(row_fn, jnp.arange(rows))
    return out.transpose(1, 0, 2, 3, 4).reshape(B, T, H * dh)

def spatial_gating(u, v, gain, w_s, b_s):
    B, T, _ = u.shape
    n = T // SG_CHUNK
    vn = rms_norm(v.reshape(B, T, SG_GROUPS, SG_GROUP_DIM), gain.reshape(SG_GROUPS, SG_GROUP_DIM))
    vn = vn.reshape(B, n, SG_CHUNK, SG_GROUPS, SG_GROUP_DIM)
    mixed = jnp.einsum('gpq,bnqgc->bnpgc', w_s, vn) + b_s.T[:, :, None]
    return u * mixed.reshape(B, T, SG_WIDTH)

def wkv_scan(r, w, k, v, a, b, s0, reverse):
    def step(S, xs):
        r_t, w_t, k_t, v_t, a_t, b_t = xs
        sa = jnp.einsum('bhvk,bhk->bhv', S, a_t)
        S = S * w_t[:, :, None, :] + sa[..., None] * b_t[:, :, None, :] + v_t[..., None] * k_t[:, :, None, :]
        return S, jnp.einsum('bhvk,bhk->bhv', S, r_t)
    xs = tuple(jnp.swapaxes(t, 0, 1) for t in (r, w, k, v, a, b))
    s_T, o = lax.scan(step, s0.astype(jnp.float32), xs, reverse=reverse)
    return jnp.swapaxes(o, 0, 1), s_T

def rwkv7_mix(r, k, v, x_w, x_a, x_g, s0_f, s0_b, lp):
    B, T, _ = r.shape
    f32 = jnp.float32
    shp = (B, T, RW_HEADS, RW_HEAD_DIM)
    rf, kf, vf = r.astype(f32), k.astype(f32), v.astype(f32)
    kk = (kf * lp['rw_kk']).reshape(shp)
    kk = kk * lax.rsqrt(jnp.sum(kk * kk, axis=-1, keepdims=True) + 1e-12)
    tw = jnp.tanh(x_w.astype(f32))
    xa = x_a.astype(f32)
    outs, finals = [], []
    for d, (s0, rev) in enumerate(((s0_f, False), (s0_b, True))):
        w_log = -jax.nn.softplus(-(lp['rw_w0'][d] + tw @ lp['rw_w2'][d])) - 0.5
        decay = jnp.exp(-jnp.exp(w_log))
        a_rate = jax.nn.sigmoid(lp['rw_a0'][d] + xa @ lp['rw_a2'][d])
        k_d = kf * (1.0 + (a_rate - 1.0) * lp['rw_ka'])
        a_h = a_rate.reshape(shp)
        o_d, s_d = wkv_scan(rf.reshape(shp), decay.reshape(shp), k_d.reshape(shp), vf.reshape(shp),
                            -kk, kk * a_h, s0, rev)
        outs.append(o_d)
        finals.append(s_d)
    o = outs[0] + outs[1]
    mu = jnp.mean(o, axis=-1, keepdims=True)
    var = jnp.mean(jnp.square(o - mu), axis=-1, keepdims=True)
    o = ((o - mu) * lax.rsqrt(var + GN_EPS)).reshape(B, T, RW_WIDTH) * lp['rw_ln_w'] + lp['rw_ln_b']
    bonus = jnp.sum(rf.reshape(shp) * kf.reshape(shp) * lp['rw_rk'], axis=-1, keepdims=True) * vf.reshape(shp)
    o = o + bonus.reshape(B, T, RW_WIDTH)
    gate = jax.nn.sigmoid(x_g.astype(f32)) @ lp['rw_g2']
    return (o * gate).astype(r.dtype), finals[0], finals[1]

def token_mixers(h, lp, k_ctx=None, v_ctx=None, s_ctx=None):
    B, T, _ = h.shape
    qa, ka, va, u_s, v_s, r_c, k_c, v_c, x_w, x_a, x_g = split_proj(h @ lp['w_in'])
    q = qa.reshape(B, T, NA_HEADS, NA_HEAD_DIM)
    k = ka.reshape(B, T, NA_HEADS, NA_HEAD_DIM)
    v = va.reshape(B, T, NA_HEADS, NA_HEAD_DIM)
    if k_ctx is None:
        o_a = na_context(q, k, v).reshape(B, T, NA_WIDTH)
        s0_f = jnp.zeros((B, RW_HEADS, RW_HEAD_DIM, RW_HEAD_DIM), jnp.float32)
        s0_b = s0_f
    else:
        o_a = na_latent(q, k, v, k_ctx, v_ctx, lp['na_rpb'])
        s0_f, s0_b = s_ctx[:, 0], s_ctx[:, 1]
    o_b = spatial_gating(u_s, v_s, lp['sg_gain'], lp['sg_w'], lp['sg_b'])
    o_c, s_f, s_b = rwkv7_mix(r_c, k_c, v_c, x_w, x_a, x_g, s0_f, s0_b, lp)
    mixed = jnp.concatenate([o_a, o_b, o_c], axis=-1) @ lp['w_out']
    return mixed, k, v, jnp.stack([s_f, s_b], axis=1)

def expert_choice_ffn(h, w_router, w_gate, w_up, w_down):
    B, T, D = h.shape
    cap = CAPACITY_FACTOR * T // N_EXPERTS
    aff = jax.nn.softmax((h @ w_router).astype(jnp.float32), axis=-1)
    g, idx = lax.top_k(jnp.swapaxes(aff, 1, 2), cap)
    xs = jax.vmap(lambda hb, ib: hb[ib])(h, idx)
    hid = jax.nn.silu(jnp.einsum('becd,edf->becf', xs, w_gate)) * jnp.einsum('becd,edf->becf', xs, w_up)
    y = jnp.einsum('becf,efd->becd', hid, w_down) * g[..., None].astype(h.dtype)
    return jax.vmap(lambda yb, ib: jnp.zeros((T, D), yb.dtype).at[ib.reshape(-1)].add(yb.reshape(-1, D)))(y, idx)

def trunk_layer(x, cond, lp, k_ctx=None, v_ctx=None, s_ctx=None):
    sh1, sc1, g1, sh2, sc2, g2 = modulation(cond, lp['w_ada'], lp['b_ada'])
    h = rms_norm(x, lp['g_pre_mix']) * (1 + sc1) + sh1
    mixed, k, v, s = token_mixers(h, lp, k_ctx, v_ctx, s_ctx)
    x = x + g1 * rms_norm(mixed, lp['g_post_mix'])
    h = rms_norm(x, lp['g_pre_ffn']) * (1 + sc2) + sh2
    ffn = expert_choice_ffn(h, lp['w_router'], lp['w_gate'], lp['w_up'], lp['w_down'])
    x = x + g2 * rms_norm(ffn, lp['g_post_ffn'])
    return x, k, v, s

def setup_inputs(seed: int = 0) -> dict:
    key = jax.random.key(seed)
    ks = iter(jax.random.split(key, 40))
    L, D = DEPTH, D_MODEL

    def nrm(shape, scale):
        return scale * jax.random.normal(next(ks), shape, jnp.float32)

    return {
        'x_prompt': nrm((BATCH, SEQ, D), 1.0),
        'x_sample': nrm((DEC_BATCH, DEC_SEQ, D), 1.0),
        'cache_k': nrm((DEC_BATCH, L, PAST_LEN, NA_HEADS, NA_HEAD_DIM), 1.0),
        'cache_v': nrm((DEC_BATCH, L, PAST_LEN, NA_HEADS, NA_HEAD_DIM), 1.0),
        'state_wkv': nrm((DEC_BATCH, L, 2, RW_HEADS, RW_HEAD_DIM, RW_HEAD_DIM), 1.0),
        'c': nrm((DEC_BATCH, D), 1.0),
        'c_ctx': nrm((D,), 1.0),
        'w_ada': nrm((L, D, N_MOD * D), 0.5 * D ** -0.5),
        'b_ada': nrm((L, N_MOD * D), 0.02),
        'g_pre_mix': 1.0 + nrm((L, D), 0.02),
        'g_post_mix': 1.0 + nrm((L, D), 0.02),
        'g_pre_ffn': 1.0 + nrm((L, D), 0.02),
        'g_post_ffn': 1.0 + nrm((L, D), 0.02),
        'w_in': nrm((L, D, IN_COLS), D ** -0.5),
        'na_rpb': nrm((L, NA_HEADS, 2 * NA_WIN_ROWS - 1, 2 * NA_WIN_COLS - 1), 0.1),
        'sg_gain': 1.0 + nrm((L, SG_WIDTH), 0.02),
        'sg_w': nrm((L, SG_GROUPS, SG_CHUNK, SG_CHUNK), SG_CHUNK ** -0.5),
        'sg_b': 1.0 + nrm((L, SG_GROUPS, SG_CHUNK), 0.02),
        'rw_w0': jax.random.uniform(next(ks), (L, 2, RW_WIDTH), jnp.float32, -5.0, 0.0),
        'rw_w2': nrm((L, 2, DECAY_LORA, RW_WIDTH), 0.1 * DECAY_LORA ** -0.5),
        'rw_a0': nrm((L, 2, RW_WIDTH), 0.1),
        'rw_a2': nrm((L, 2, AAA_LORA, RW_WIDTH), 0.5 * AAA_LORA ** -0.5),
        'rw_g2': nrm((L, GATE_LORA, RW_WIDTH), GATE_LORA ** -0.5),
        'rw_kk': 0.85 + nrm((L, RW_WIDTH), 0.02),
        'rw_ka': 1.0 + nrm((L, RW_WIDTH), 0.02),
        'rw_rk': nrm((L, RW_HEADS, RW_HEAD_DIM), 0.1),
        'rw_ln_w': 1.0 + nrm((L, RW_WIDTH), 0.02),
        'rw_ln_b': nrm((L, RW_WIDTH), 0.02),
        'w_out': nrm((L, D, D), D ** -0.5),
        'w_router': nrm((L, D, N_EXPERTS), D ** -0.5),
        'w_gate': nrm((L, N_EXPERTS, D, D_EXPERT), D ** -0.5),
        'w_up': nrm((L, N_EXPERTS, D, D_EXPERT), D ** -0.5),
        'w_down': nrm((L, N_EXPERTS, D_EXPERT, D), D_EXPERT ** -0.5),
    }

def reference(x_prompt, x_sample, cache_k, cache_v, state_wkv, c, c_ctx, w_ada, b_ada,
              g_pre_mix, g_post_mix, g_pre_ffn, g_post_ffn, w_in, na_rpb, sg_gain, sg_w, sg_b,
              rw_w0, rw_w2, rw_a0, rw_a2, rw_g2, rw_kk, rw_ka, rw_rk, rw_ln_w, rw_ln_b,
              w_out, w_router, w_gate, w_up, w_down):
    xp, xs = x_prompt, x_sample
    ks, vs, ss = [], [], []
    for l in range(DEPTH):
        lp = dict(w_ada=w_ada[l], b_ada=b_ada[l], g_pre_mix=g_pre_mix[l], g_post_mix=g_post_mix[l],
                  g_pre_ffn=g_pre_ffn[l], g_post_ffn=g_post_ffn[l], w_in=w_in[l], na_rpb=na_rpb[l],
                  sg_gain=sg_gain[l], sg_w=sg_w[l], sg_b=sg_b[l], rw_w0=rw_w0[l], rw_w2=rw_w2[l],
                  rw_a0=rw_a0[l], rw_a2=rw_a2[l], rw_g2=rw_g2[l], rw_kk=rw_kk[l], rw_ka=rw_ka[l],
                  rw_rk=rw_rk[l], rw_ln_w=rw_ln_w[l], rw_ln_b=rw_ln_b[l], w_out=w_out[l],
                  w_router=w_router[l], w_gate=w_gate[l], w_up=w_up[l], w_down=w_down[l])
        xp, k_l, v_l, s_l = trunk_layer(xp, c_ctx, lp)
        ks.append(k_l)
        vs.append(v_l)
        ss.append(s_l.astype(x_prompt.dtype))
        xs, _, _, _ = trunk_layer(xs, c, lp, cache_k[:, l], cache_v[:, l], state_wkv[:, l])
    new_cache_k = jnp.stack(ks, axis=1)
    new_cache_v = jnp.stack(vs, axis=1)
    new_state_wkv = jnp.stack(ss, axis=1)
    return (xp, xs, new_cache_k, new_cache_v, new_state_wkv)


_drawn_inputs = setup_inputs


def setup_inputs(seed=0):
    import zlib

    import numpy as np

    out = dict(_drawn_inputs(seed))
    spreads = {}
    factors = {'g_post_mix': 2.748,
     'g_post_ffn': 8.0,
     'na_rpb': 4.195,
     'sg_gain': 4.995,
     'sg_b': 3.567,
     'rw_w2': 6.546,
     'rw_kk': 3.505,
     'rw_ln_w': 4.347,
     'rw_ln_b': 8.0}
    for name, (base, spread) in spreads.items():
        noise = np.random.default_rng([zlib.crc32(name.encode()), seed]).standard_normal(out[name].shape)
        drawn = base * np.exp(spread * noise) if base else spread * noise
        out[name] = __import__('jax').numpy.asarray(drawn.astype(out[name].dtype))
    for name, factor in factors.items():
        out[name] = (out[name] * factor).astype(out[name].dtype)
    return out
```

```python
from contextlib import ExitStack

import numpy as np

import concourse.bass as bass
from concourse import mybir

F32 = mybir.dt.float32
ALU = mybir.AluOpType
ACT = mybir.ActivationFunctionType
AX_X = mybir.AxisListType.X

P = 128
D = 2048
KD = D // P
TP, TS = 128, 512
T = TP + TS
NT = T // P
GRID_W, NAH, DH = 64, 8, 64
NAW = NAH * DH
SGG = 4
RW = 1024
NPAIR = RW // P
CK = 64
NCK = T // CK
NCP = TP // CK
NE, DE = 16, 1024
CAPS, CAPP = 2 * TS // NE, 2 * TP // NE
NCOL = 3 * NAW + 2 * 512 + 3 * RW + 256
NAW_C = 16
NORM_EPS, GN_EPS = 1e-6, 64e-5
NEG = -1.0e30
ZQ, ZK, ZU, ZR, ZKC, ZV, ZX = 0, 4, 8, 12, 20, 28, 36
NZ = 38


class Chain:

    def __init__(self, eng, sem):
        self.eng, self.sem, self.n = eng, sem, 0

    def link(self, ins):
        self.n += 1
        ins.then_inc(self.sem, 1)
        self.eng.wait_ge(self.sem, self.n)


def dram_ap(ap, offset, dims):
    return bass.AP(tensor=ap.tensor, offset=ap.offset + offset, ap=[list(d) for d in dims])


def bcast_rows(ap, offset, n, rows=P):
    return dram_ap(ap, offset, [[0, rows], [1, n]])


def block_modulation(nc, c, c_ctx, w_ada, b_ada, mod_d, ident_d):
    G, NB = 3, 8
    GC = NB * 512
    RING = 4
    with ExitStack() as ctx:
        def sb(name, shape):
            return ctx.enter_context(nc.sbuf_tensor(name, shape, F32))

        def sem(name):
            return nc.alloc_semaphore(name)

        cond = sb("ada_cond", [2 * KD, P])
        cond_s = sb("ada_cond_silu", [2 * KD, P])
        ident = sb("ada_ident", [P, P])
        cond_t = sb("ada_cond_t", [P, 2, KD])
        ring = sb("ada_ring", [P, RING, GC])
        bias = sb("ada_bias", [2, GC])
        rows = sb("ada_rows", [2, GC])
        acc = ctx.enter_context(nc.psum_tensor("ada_acc", [P, NB, 512], F32))
        cond_in, bias_in, ident_made, ident_out = (sem(n) for n in ("ada_cond_in", "ada_bias_in", "ada_id", "ada_id_out"))
        silu_done, cond_turned, cond_ready = sem("ada_silu"), sem("ada_turned"), sem("ada_condready")
        w_in = [sem(f"ada_w{i}") for i in range(RING)]
        k_used, rows_ready, rows_out = (sem(n) for n in ("ada_kused", "ada_rows_rdy", "ada_out"))
        block = ctx.enter_context(nc.Block())

        @block.sync
        def _(sp):
            sp.dma_start(cond[0:KD, :], c_ctx.rearrange("(k p) -> k p", p=P)).then_inc(cond_in, 16)
            sp.dma_start(cond[KD:2 * KD, :], c.rearrange("o (k p) -> (o k) p", p=P)).then_inc(cond_in, 16)
            for n in range(G * KD):
                g, k = n // KD, n % KD
                if n >= RING:
                    sp.wait_ge(k_used, n - RING + 1)
                sp.dma_start(ring[:, n % RING, :], w_ada[0, k * P:(k + 1) * P, g * GC:(g + 1) * GC]).then_inc(w_in[n % RING], 16)

        @block.gpsimd
        def _(pool):
            nc.gpsimd.memset(ident[:], 0.0).then_inc(ident_made, 1)
            pool.wait_ge(ident_made, 1)
            nc.gpsimd.affine_select(out=ident[:], in_=ident[:], compare_op=ALU.not_equal, fill=1.0, base=0,
                                    pattern=[[-1, P]], channel_multiplier=1).then_inc(ident_made, 1)
            pool.wait_ge(ident_made, 2)
            pool.dma_start(ident_d, ident[:]).then_inc(ident_out, 16)
            pool.wait_ge(ident_out, 16)

        @block.scalar
        def _(act):
            for g in range(G):
                if g:
                    act.wait_ge(rows_ready, g)
                act.dma_start(bias[:], bcast_rows(b_ada, g * GC, GC, 2)).then_inc(bias_in, 16)
                if g == 0:
                    act.wait_ge(cond_in, 32)
                    nc.scalar.activation(cond_s[:], cond[:], ACT.Silu).then_inc(silu_done, 1)
                act.wait_ge(rows_ready, g + 1)
                act.dma_start(mod_d[:, g * GC:(g + 1) * GC], rows[:]).then_inc(rows_out, 16)
            act.wait_ge(rows_out, 16 * G)

        @block.tensor
        def _(pe):
            pe.wait_ge(silu_done, 1)
            pe.wait_ge(ident_made, 2)
            pe.transpose(acc[:, 0, 0:2 * KD], cond_s[:], ident[0:2 * KD, 0:2 * KD]).then_inc(cond_turned, 1)
            pe.wait_ge(cond_ready, 1)
            for n in range(G * KD):
                g, k = n // KD, n % KD
                pe.wait_ge(w_in[n % RING], 16 * (n // RING + 1))
                if k == 0 and g:
                    pe.wait_ge(rows_ready, g)
                for b in range(NB):
                    mm = pe.matmul(acc[0:2, b, :], cond_t[:, :, k], ring[:, n % RING, b * 512:(b + 1) * 512],
                                   start=(k == 0), stop=(k == KD - 1))
                mm.then_inc(k_used, 1)

        @block.vector
        def _(dve):
            dve.wait_ge(cond_turned, 1)
            nc.vector.tensor_copy(cond_t[:].rearrange("p c k -> p (c k)"), acc[:, 0, 0:2 * KD]).then_inc(cond_ready, 1)
            for g in range(G):
                dve.wait_ge(k_used, KD * (g + 1))
                dve.wait_ge(bias_in, 16 * (g + 1))
                if g:
                    dve.wait_ge(rows_out, 16 * g)
                for b in range(NB):
                    tt = nc.vector.tensor_tensor(rows[:, b * 512:(b + 1) * 512], acc[0:2, b, :],
                                                 bias[:, b * 512:(b + 1) * 512], ALU.add)
                tt.then_inc(rows_ready, 1)


def block_projection(nc, x_prompt, x_sample, g_pre, w_in, mod_d, ident_d, z_d, v_d, vs_d):
    WB = 256
    NBLK = NCOL // WB
    KINDS = "zzvzs" + "z" * 7
    H0 = 5
    ZROW = [ZQ, ZK, None, ZU, None]
    with ExitStack() as ctx:
        def sb(name, shape):
            return ctx.enter_context(nc.sbuf_tensor(name, shape, F32))

        def sem(name):
            return nc.alloc_semaphore(name)

        ident = sb("pj_ident", [P, P])
        xt = sb("pj_x", [P, 2, D])
        junk = sb("pj_junk", [P, D])
        ssq = sb("pj_ssq", [P, NT])
        rstd = sb("pj_rstd", [P, NT])
        rr = sb("pj_rr", [P, NT])
        modr = sb("pj_modr", [5 * KD, P])
        modt = sb("pj_modt", [P, 5, KD])
        gsc = sb("pj_gsc", [P, 2, KD])
        hT = sb("pj_hT", [P, KD, T])
        ring = sb("pj_ring", [P, 2, KD, WB])
        stage = sb("pj_stage", [P, 4, 768])
        ps = ctx.enter_context(nc.psum_tensor("pj_ps", [P, 8, 512], F32))
        const_in, x_in0, x_in1 = sem("pj_const_in"), sem("pj_x_in0"), sem("pj_x_in1")
        x_in = (x_in0, x_in1)
        x_free, ss_done, rs_done, xn_done = sem("pj_xfree"), sem("pj_ss"), sem("pj_rs"), sem("pj_xn")
        mod_turned, mod_ready, dchain = sem("pj_modturn"), sem("pj_modrdy"), sem("pj_dchain")
        turned, h_act, h_dve = sem("pj_turned"), sem("pj_hact"), sem("pj_hdve")
        w_got = [sem("pj_w0"), sem("pj_w1")]
        col_done, ev_act, ev_dve = sem("pj_col"), sem("pj_evact"), sem("pj_evdve")
        out_sem = [sem(f"pj_out{i}") for i in range(4)]
        block = ctx.enter_context(nc.Block())

        def x_rows(t):
            return x_prompt[0] if t == 0 else x_sample[0, (t - 1) * P:t * P, :]

        def w_cols(b):
            return w_in[0, :, bass.ds(b * WB, WB)].rearrange("(k p) n -> p k n", p=P)

        def over_blocks(eng, body, first=0):
            for h in range(first, H0):
                for half in range(2):
                    body(h, half, KINDS[h])
            with eng.Fori(H0, NBLK // 2) as h:
                for half in range(2):
                    body(h, half, "z")
            body(NBLK // 2, 0, "z")

        @block.sync
        def _(sp):
            for t in range(NT):
                if t >= 2:
                    sp.wait_ge(turned, 4 * (t - 1))
                sp.dma_start(xt[:, t % 2, :], x_rows(t)).then_inc(x_in[t % 2], 16)
                if t == 0:
                    sp.dma_start(ident[:], ident_d).then_inc(const_in, 16)
                    for i, (cond, part) in enumerate(((0, 0), (0, 1), (1, 0), (1, 1))):
                        sp.dma_start(modr[i * KD:(i + 1) * KD, :],
                                     mod_d[cond, part * D:(part + 1) * D].rearrange("(k p) -> k p", p=P)).then_inc(const_in, 16)
                    sp.dma_start(modr[4 * KD:5 * KD, :], g_pre.rearrange("o (k p) -> (o k) p", p=P)).then_inc(const_in, 16)
                if t == 1:
                    for b in range(2):
                        sp.dma_start(ring[:, b, :, :], w_cols(b)).then_inc(w_got[b], 16)

            def load(h, half, kind):
                sp.wait_ge(col_done, 4 * h + 2 * half - 2)
                sp.dma_start(ring[:, half, :, :], w_cols(2 * h + half)).then_inc(w_got[half], 16)
            over_blocks(sp, load, first=1)

        @block.gpsimd
        def _(pool):
            def store(h, half, kind):
                for j in range(2):
                    slot, n = 2 * half + j, 4 * h + 2 * half + j
                    pool.wait_ge(ev_act, n + 1)
                    pool.wait_ge(ev_dve, n + 1)
                    if kind == "z":
                        row = ZROW[h] if isinstance(h, int) and h < H0 else ZR + 4 * (h - H0)
                        pool.dma_start(z_d[bass.ds(row + 2 * half + j, 1)].rearrange("o p n -> p (o n)"),
                                       stage[:, slot, 0:T]).then_inc(out_sem[slot], 16)
                    else:
                        dst = v_d if kind == "v" else vs_d
                        t0, t1 = ((0, 2), (2, 5))[j]
                        pool.dma_start(dst[t0:t1, :, half * WB:(half + 1) * WB].rearrange("t p c -> p t c"),
                                       stage[:, slot, 0:WB * (t1 - t0)].rearrange("p (t c) -> p t c", c=WB)).then_inc(out_sem[slot], 16)
            over_blocks(pool, store)
            for s in range(4):
                pool.wait_ge(out_sem[s], 16 * len([n for n in range(2 * NBLK) if n % 4 == s]))

        @block.scalar
        def _(act):
            for t in range(NT):
                act.wait_ge(x_in[t % 2], 16 * (t // 2 + 1))
                nc.scalar.activation(junk[:], xt[:, t % 2, :], ACT.Square, accum_out=ssq[:, t:t + 1]).then_inc(ss_done, 1)
                act.wait_ge(rs_done, 3 * t + 1)
                nc.scalar.activation(rr[:, t:t + 1], rstd[:, t:t + 1], ACT.Sqrt).then_inc(ss_done, 1)
                for q in (0, 2):
                    act.wait_ge(turned, 4 * t + q + 1)
                    act.wait_ge(mod_ready, 1)
                    for j in range(4):
                        k, cnd = 4 * q + j, min(t, 1)
                        a = nc.scalar.activation(hT[:, k, t * P:(t + 1) * P], ps[:, (4 * t + q) % 4, j * P:(j + 1) * P],
                                                 ACT.Identity, scale=gsc[:, cnd, k:k + 1],
                                                 bias=modt[:, 2 * cnd, k:k + 1])
                    a.then_inc(h_act, 1)

            def evacuate(h, half, kind):
                for j in range(2):
                    n, slot, base = 4 * h + 2 * half + j, 2 * half + j, 4 * half
                    act.wait_ge(col_done, n + 1)
                    if not isinstance(h, int) or h:
                        act.wait_ge(out_sem[slot], 16 * h)
                    if kind == "z":
                        a = nc.scalar.copy(stage[:, slot, TP:T], ps[:, base + 2 * j, :])
                    elif j == 0:
                        a = nc.scalar.copy(stage[:, slot, 0:WB], ps[:, base, 0:WB])
                    else:
                        a = nc.scalar.copy(stage[:, slot, 0:2 * WB], ps[:, base + 2, :])
                    a.then_inc(ev_act, 1)
            over_blocks(act, evacuate)

        @block.vector
        def _(dve):
            ch = Chain(dve, dchain)
            dve.wait_ge(mod_turned, 1)
            ch.link(nc.vector.tensor_copy(modt[:].rearrange("p a k -> p (a k)"), ps[:, 4, 0:5 * KD]))
            for cnd in range(2):
                g2 = nc.vector.scalar_tensor_tensor(gsc[:, cnd, :], modt[:, 2 * cnd + 1, :], 1.0, modt[:, 4, :], ALU.add, ALU.mult)
            g2.then_inc(mod_ready, 1)

            for t in range(NT):
                dve.wait_ge(ss_done, 2 * t + 1)
                nc.vector.tensor_scalar(rstd[:, t:t + 1], ssq[:, t:t + 1], 1.0 / D, NORM_EPS, ALU.mult, ALU.add).then_inc(rs_done, 1)
                dve.wait_ge(ss_done, 2 * t + 2)
                nc.vector.reciprocal(rstd[:, t:t + 1], rr[:, t:t + 1]).then_inc(rs_done, 1)
                dve.wait_ge(rs_done, 3 * t + 2)
                nc.vector.tensor_scalar(xt[:, t % 2, :], xt[:, t % 2, :], rstd[:, t:t + 1], None, ALU.mult).then_inc(rs_done, 1)
                for q in (1, 3):
                    dve.wait_ge(turned, 4 * t + q + 1)
                    if t == 0 and q == 1:
                        dve.wait_ge(mod_ready, 1)
                    for j in range(4):
                        k, cnd = 4 * q + j, min(t, 1)
                        a = nc.vector.tensor_scalar(hT[:, k, t * P:(t + 1) * P], ps[:, (4 * t + q) % 4, j * P:(j + 1) * P],
                                                    gsc[:, cnd, k:k + 1], modt[:, 2 * cnd, k:k + 1], ALU.mult, ALU.add)
                    a.then_inc(h_dve, 1)

            def evacuate(h, half, kind):
                for j in range(2):
                    n, slot, base = 4 * h + 2 * half + j, 2 * half + j, 4 * half
                    dve.wait_ge(col_done, n + 1)
                    if not isinstance(h, int) or h:
                        dve.wait_ge(out_sem[slot], 16 * h)
                    if kind == "z":
                        a = nc.vector.tensor_copy(stage[:, slot, 0:TP], ps[:, base + 2 * j + 1, 0:TP])
                    elif j == 0:
                        a = nc.vector.tensor_copy(stage[:, slot, WB:2 * WB], ps[:, base + 1, 0:WB])
                    else:
                        a = nc.vector.tensor_copy(stage[:, slot, 2 * WB:3 * WB], ps[:, base + 3, 0:WB])
                    a.then_inc(ev_dve, 1)
            over_blocks(dve, evacuate)

        @block.tensor
        def _(pe):
            pe.wait_ge(const_in, 16 * 6)
            pe.transpose(ps[:, 4, 0:5 * KD], modr[:], ident[0:5 * KD, 0:5 * KD]).then_inc(mod_turned, 1)
            for t in range(NT):
                pe.wait_ge(rs_done, 3 * t + 3)
                for q in range(4):
                    if t:
                        pe.wait_ge(h_dve if q % 2 else h_act, 2 * (t - 1) + q // 2 + 1)
                    for j in range(4):
                        k = 4 * q + j
                        mm = pe.transpose(ps[:, (4 * t + q) % 4, j * P:(j + 1) * P], xt[:, t % 2, k * P:(k + 1) * P], ident[:])
                    mm.then_inc(turned, 1)
            pe.wait_ge(h_act, 2 * NT)
            pe.wait_ge(h_dve, 2 * NT)

            def multiply(h, half, kind):
                base = 4 * half
                pe.wait_ge(w_got[half], 16 * (h + 1))
                if not isinstance(h, int) or h:
                    pe.wait_ge(ev_act, 4 * h + 2 * half - 2)
                    pe.wait_ge(ev_dve, 4 * h + 2 * half - 2)
                for j in range(2):
                    if kind == "z":
                        for dst, t0, t1 in ((ps[:, base + 2 * j, :], TP, T), (ps[:, base + 2 * j + 1, 0:TP], 0, TP)):
                            for k in range(KD):
                                mm = pe.matmul(dst, ring[:, half, k, j * P:(j + 1) * P], hT[:, k, t0:t1],
                                               start=(k == 0), stop=(k == KD - 1))
                    else:
                        for t, bank, c0 in (((0, 0, 0), (1, 1, 0)), ((2, 2, 0), (3, 2, WB), (4, 3, 0)))[j]:
                            for k in range(KD):
                                mm = pe.matmul(ps[:, base + bank, c0:c0 + WB], hT[:, k, t * P:(t + 1) * P], ring[:, half, k, :],
                                               start=(k == 0), stop=(k == KD - 1))
                    mm.then_inc(col_done, 1)
            over_blocks(pe, multiply)


def block_gating_and_keys(nc, z_d, vs_d, sg_gain, sg_w, sg_b, vectors, ident_d, par_d, kk_d, o_d):
    NV = sum(v_rows for _, v_rows in vectors)
    with ExitStack() as ctx:
        def sb(name, shape):
            return ctx.enter_context(nc.sbuf_tensor(name, shape, F32))

        def sem(name):
            return nc.alloc_semaphore(name)

        ident = sb("gk_ident", [P, P])
        vs = sb("gk_vs", [P, NT, SGG, P])
        sq = sb("gk_sq", [P, NT, SGG, P])
        gain = sb("gk_gain", [P, SGG, P])
        ws = sb("gk_ws", [P, SGG, P])
        wst = sb("gk_wst", [P, SGG, P])
        brow = sb("gk_brow", [1, SGG, P])
        ones = sb("gk_ones", [1, P])
        ss, sr, rs = sb("gk_ss", [P, NT * SGG]), sb("gk_sr", [P, NT * SGG]), sb("gk_rs", [P, NT * SGG])
        eps = sb("gk_eps", [P, 2])
        ut = sb("gk_ut", [P, SGG, T])
        ob = sb("gk_ob", [P, SGG, T])
        vrow = sb("gk_vrow", [NV, P])
        par = sb("gk_par", [P, NV])
        blk = sb("gk_blk", [P, P])
        kt = sb("gk_kt", [P, NPAIR, T])
        k2 = sb("gk_k2", [P, 2, T])
        nrm = sb("gk_nrm", [P, 2, T])
        ps = ctx.enter_context(nc.psum_tensor("gk_ps", [P, 8, 512], F32))
        small_in, vs_in, ut_in, k_in = sem("gk_small"), sem("gk_vsin"), sem("gk_utin"), sem("gk_kin")
        made, made_eps = sem("gk_made"), sem("gk_mdeps")
        turned, copied, dch = sem("gk_turned"), sem("gk_copied"), sem("gk_dch")
        ssd, srd, vnd, mixd, gated = sem("gk_ssd"), sem("gk_srd"), sem("gk_vnd"), sem("gk_mix"), sem("gk_gated")
        kkd, sqd, sumd, sqrtd, kkn = sem("gk_kkd"), sem("gk_sqd"), sem("gk_sumd"), sem("gk_sqrtd"), sem("gk_kkn")
        out = sem("gk_out")
        block = ctx.enter_context(nc.Block())

        @block.sync
        def _(sp):
            sp.dma_start(ident[:], ident_d).then_inc(small_in, 16)
            r = 0
            for v, n in vectors:
                sp.dma_start(vrow[r:r + n, :], v).then_inc(small_in, 16)
                r += n
            sp.dma_start(ws[:], sg_w[0].rearrange("g p q -> p g q")).then_inc(small_in, 16)
            sp.dma_start(brow[:], sg_b).then_inc(small_in, 16)
            sp.dma_start(gain[:].rearrange("p g c -> p (g c)"), bcast_rows(sg_gain, 0, 512)).then_inc(small_in, 16)
            sp.dma_start(vs[:].rearrange("p t g c -> p t (g c)"), vs_d.rearrange("t p c -> p t c")).then_inc(vs_in, 16)
            sp.dma_start(ut[:], z_d[ZU:ZU + SGG].rearrange("g p t -> p g t")).then_inc(ut_in, 16)
            sp.dma_start(kt[:], z_d[ZKC:ZKC + NPAIR].rearrange("g p t -> p g t")).then_inc(k_in, 16)
            sp.wait_ge(copied, 1)
            sp.dma_start(par_d, par[:]).then_inc(out, 16)
            sp.wait_ge(gated, 2 * SGG)
            sp.dma_start(o_d[4:4 + SGG].rearrange("g p t -> p g t"), ob[:]).then_inc(out, 16)
            for p in range(NPAIR):
                sp.wait_ge(kkn, p + 1)
                sp.dma_start(kk_d[p], kt[:, p, :]).then_inc(out, 16)
            sp.wait_ge(out, 16 * (2 + NPAIR))

        @block.gpsimd
        def _(pool):
            nc.gpsimd.memset(ones[:], 1.0)
            nc.gpsimd.memset(eps[:, 0:1], NORM_EPS)
            nc.gpsimd.memset(eps[:, 1:2], 1e-12).then_inc(made, 1)
        @block.tensor
        def _(pe):
            pe.wait_ge(small_in, 16 * (4 + len(vectors)))
            pe.transpose(ps[:, 0, 0:NV], vrow[:], ident[0:NV, 0:NV]).then_inc(turned, 1)
            for g in range(SGG):
                tr = pe.transpose(ps[:, 1, g * P:(g + 1) * P], ws[:, g, :], ident[:])
            tr.then_inc(turned, 1)
            pe.wait_ge(made, 2)
            for p in range(NPAIR):
                pe.wait_ge(sqd, p + 1)
                b = 2 + 2 * (p % 3)
                if p >= 3:
                    pe.wait_ge(sqrtd, p - 2)
                pe.matmul(ps[:, b, :], blk[:], k2[:, p % 2, TP:T], start=True, stop=True)
                pe.matmul(ps[:, b + 1, 0:TP], blk[:], k2[:, p % 2, 0:TP], start=True, stop=True).then_inc(sumd, 1)
            pe.wait_ge(vnd, 1)
            pe.wait_ge(copied, 2)
            pe.wait_ge(sqrtd, NPAIR)
            for g in range(SGG):
                if g >= 4:
                    pe.wait_ge(gated, 2 * (g - 3))
                for t in range(NT):
                    dst = ps[:, 4 + g, 0:P] if t == 0 else ps[:, g, (t - 1) * P:t * P]
                    pe.matmul(dst, vs[:, t, g, :], wst[:, g, :], start=True, stop=False)
                    mm = pe.matmul(dst, ones[:], brow[:, g, :], start=False, stop=True)
                    if t == 0 or t == NT - 1:
                        mm.then_inc(mixd, 1)

        @block.scalar
        def _(act):
            act.wait_ge(ssd, 1)
            act.wait_ge(made, 2)
            nc.scalar.activation(sr[:], ss[:], ACT.Sqrt, scale=1.0 / P, bias=eps[:, 0:1]).then_inc(srd, 1)
            for p in range(NPAIR):
                act.wait_ge(kkd, p + 1)
                if p >= 2:
                    act.wait_ge(sumd, p - 1)
                nc.scalar.activation(k2[:, p % 2, :], kt[:, p, :], ACT.Square).then_inc(sqd, 1)
                act.wait_ge(sumd, p + 1)
                b = 2 + 2 * (p % 3)
                if p >= 2:
                    act.wait_ge(kkn, p - 1)
                nc.scalar.activation(nrm[:, p % 2, TP:T], ps[:, b, :], ACT.Sqrt, bias=eps[:, 1:2])
                nc.scalar.activation(nrm[:, p % 2, 0:TP], ps[:, b + 1, 0:TP], ACT.Sqrt, bias=eps[:, 1:2]).then_inc(sqrtd, 1)

        @block.vector
        def _(dve):
            ch = Chain(dve, dch)
            nc.vector.memset(blk[0:DH, 0:DH], 1.0)
            nc.vector.memset(blk[0:DH, DH:P], 0.0)
            nc.vector.memset(blk[DH:P, 0:DH], 0.0)
            nc.vector.memset(blk[DH:P, DH:P], 1.0).then_inc(made, 1)
            dve.wait_ge(turned, 1)
            nc.vector.tensor_copy(par[:], ps[:, 0, 0:NV]).then_inc(copied, 1)
            dve.wait_ge(turned, 2)
            nc.vector.tensor_copy(wst[:].rearrange("p g c -> p (g c)"), ps[:, 1, :]).then_inc(copied, 1)
            dve.wait_ge(copied, 1)
            dve.wait_ge(k_in, 16)
            for p in range(NPAIR):
                nc.vector.tensor_scalar(kt[:, p, :], kt[:, p, :], par[:, p:p + 1], None, ALU.mult).then_inc(kkd, 1)
            dve.wait_ge(vs_in, 16)
            ch.link(nc.vector.tensor_tensor(sq[:], vs[:], vs[:], ALU.mult))
            nc.vector.tensor_reduce(ss[:], sq[:].rearrange("p t g c -> p (t g) c"), AX_X, ALU.add).then_inc(ssd, 1)
            for p in range(NPAIR):
                dve.wait_ge(sqrtd, p + 1)
                ch.link(nc.vector.reciprocal(nrm[:, p % 2, :], nrm[:, p % 2, :]))
                dve.wait_ge(kkd, p + 1)
                nc.vector.tensor_tensor(kt[:, p, :], kt[:, p, :], nrm[:, p % 2, :], ALU.mult).then_inc(kkn, 1)
                if p == 1:
                    dve.wait_ge(srd, 1)
                    ch.link(nc.vector.reciprocal(rs[:], sr[:]))
                    v3 = vs[:].rearrange("p t g c -> p (t g) c")
                    ch.link(nc.vector.tensor_tensor(v3, v3, rs[:].unsqueeze(2).to_broadcast([P, NT * SGG, P]), ALU.mult))
                    dve.wait_ge(small_in, 16 * (4 + len(vectors)))
                    for t in range(NT):
                        vn = nc.vector.tensor_tensor(vs[:, t], vs[:, t], gain[:], ALU.mult)
                    vn.then_inc(vnd, 1)
            dve.wait_ge(ut_in, 16)
            for g in range(SGG):
                dve.wait_ge(mixd, 2 * g + 1)
                nc.vector.tensor_tensor(ob[:, g, 0:TP], ps[:, 4 + g, 0:TP], ut[:, g, 0:TP], ALU.mult).then_inc(gated, 1)
                dve.wait_ge(mixd, 2 * g + 2)
                nc.vector.tensor_tensor(ob[:, g, TP:T], ps[:, g, :], ut[:, g, TP:T], ALU.mult).then_inc(gated, 1)


def block_attention(nc, z_d, v_d, cache_k, cache_v, rpb, ident_d, bias_d, o_d, new_k, new_v):
    GR = TS // GRID_W
    W2 = 2 * GRID_W - 1
    NR = 2 * GR - 1
    QS = DH ** -0.5
    U = NT
    with ExitStack() as ctx:
        def sb(name, shape):
            return ctx.enter_context(nc.sbuf_tensor(name, shape, F32))

        def sem(name):
            return nc.alloc_semaphore(name)

        ident = sb("at_ident", [P, P])
        table = sb("at_table", [NAH * NR, W2])
        colmask = sb("at_colmask", [P, GRID_W])
        bias = sb("at_bias", [P, 2, TS + TP])
        qt = sb("at_qt", [P, T])
        ktile = sb("at_kt", [P, T])
        qpad = sb("at_qpad", [P, 2, T])
        vt = sb("at_vt", [P, NT, P])
        ck, cv = sb("at_ck", [P, P]), sb("at_cv", [P, P])
        kct = sb("at_kct", [P, P])
        nk = sb("at_nk", [P, P])
        sc = sb("at_sc", [P, 2, T])
        pr = sb("at_pr", [P, 2, T])
        pt = sb("at_pt", [P, 2, T])
        mx, nmx, sm, rc = (sb(f"at_{n}", [P, 2]) for n in ("mx", "nmx", "sm", "rc"))
        ot = sb("at_ot", [P, T])
        ps_s = ctx.enter_context(nc.psum_tensor("at_ps_s", [P, 2, 1024], F32))
        ps_t = ctx.enter_context(nc.psum_tensor("at_ps_t", [P, 1024], F32))
        ps_o = ctx.enter_context(nc.psum_tensor("at_ps_o", [P, 2, 512], F32))
        pre_in, rpb_in, table_out, made = sem("at_pre_in"), sem("at_rpb_in"), sem("at_tabout"), sem("at_made")
        pair_in, pair_used, bias_ready, bias_used = (sem(f"at_{n}") for n in ("pairin", "pairused", "biasrdy", "biasused"))
        bias_in = (sem("at_biasin0"), sem("at_biasin1"))
        kct_t, kct_r, q_ready = sem("at_kctt"), sem("at_kctr"), sem("at_qready")
        scored, maxed, negd, expd, rcd, normed, turned, ptd, pvd = (sem(f"at_{n}") for n in
            ("scored", "maxed", "negd", "expd", "rcd", "normed", "turned", "ptd", "pvd"))
        begun = sem("at_begun")
        o_ready, o_out, nk_out, nv_out, ch_s = (sem(f"at_{n}") for n in ("oready", "oout", "nkout", "nvout", "chs"))
        block = ctx.enter_context(nc.Block())
        UP = 2 * U

        toep = dram_ap(bias_d, GRID_W - 1, [[GRID_W * W2, NAH * NR], [W2 - 1, GRID_W], [1, GRID_W]])

        @block.sync
        def _(sp):
            sp.dma_start(ident[:], ident_d).then_inc(pre_in, 16)
            sp.wait_ge(made, 1)
            sp.dma_start(table[:, GRID_W - NAW_C:GRID_W + NAW_C - 1], rpb[0].rearrange("h r c -> (h r) c")).then_inc(rpb_in, 16)
            sp.wait_ge(rpb_in, 16)
            sp.dma_start(bias_d.rearrange("r (c w) -> r c w", w=W2),
                         table[:].unsqueeze(1).to_broadcast([NAH * NR, GRID_W, W2])).then_inc(table_out, 16)
            sp.wait_ge(table_out, 16)
            with sp.Fori(0, NAH // 2) as p:
                sp.wait_ge(pair_used, p + 1)
                cols = bass.ds(p * P, P)
                sp.dma_start(qt[:], z_d[bass.ds(ZQ + p, 1)].rearrange("o p t -> p (o t)")).then_inc(pair_in, 16)
                sp.dma_start(ktile[:], z_d[bass.ds(ZK + p, 1)].rearrange("o p t -> p (o t)")).then_inc(pair_in, 16)
                sp.dma_start(vt[:], v_d[:, :, cols].rearrange("t p c -> p t c")).then_inc(pair_in, 16)
                sp.dma_start(ck[:], cache_k[:, cols]).then_inc(pair_in, 16)
                sp.dma_start(cv[:], cache_v[:, cols]).then_inc(pair_in, 16)
                for hh in range(2):
                    for tile in range(4):
                        n = 4 * hh + tile
                        sp.wait_ge(bias_used, p * 8 + n + 1)
                        for r2 in range(2):
                            row = (2 * p + hh) * NR + (GR - 1) - 2 * tile - r2
                            sp.dma_start(bias[r2 * GRID_W:(r2 + 1) * GRID_W, n % 2, 0:TS].rearrange("c (r k) -> c r k", k=GRID_W),
                                         toep[bass.ds(row, GR)].rearrange("r c k -> c r k")).then_inc(bias_in[n % 2], 16)
            sp.wait_ge(nk_out, 16 * (NAH // 2))
            sp.wait_ge(nv_out, 16 * (NAH // 2))
            sp.wait_ge(o_out, 16 * (NAH // 2))

        @block.gpsimd
        def _(pool):
            nc.gpsimd.memset(table[:], NEG).then_inc(made, 1)
            nc.gpsimd.memset(bias[:, :, TS:], 0.0)
            pch = Chain(pool, ch_s)
            pch.link(nc.gpsimd.memset(qpad[:], 0.0))
            pch.link(nc.gpsimd.memset(colmask[:], 0.0))
            half = NAW_C // 2
            for r2 in range(2):
                rows = slice(r2 * GRID_W, (r2 + 1) * GRID_W)
                m = colmask[rows, 0:GRID_W - NAW_C]
                pch.link(nc.gpsimd.affine_select(out=m, in_=m, compare_op=ALU.is_ge, fill=NEG, base=half,
                                                 pattern=[[1, GRID_W - NAW_C]], channel_multiplier=-1))
                m = colmask[rows, NAW_C:GRID_W]
                pch.link(nc.gpsimd.affine_select(out=m, in_=m, compare_op=ALU.is_ge, fill=NEG, base=half - 1 - NAW_C,
                                                 pattern=[[-1, GRID_W - NAW_C]], channel_multiplier=1))
            pool.sem_inc(pair_used, 1)
            pool.sem_inc(bias_used, 2)
            with pool.Fori(0, NAH // 2) as p:
                for n in range(8):
                    pool.wait_ge(bias_in[n % 2], p * 128 + (n // 2 + 1) * 32)
                    b3 = bias[:, n % 2, 0:TS].rearrange("p (r k) -> p r k", k=GRID_W)
                    nc.gpsimd.tensor_tensor(b3, b3, colmask[:].unsqueeze(1).to_broadcast([P, GR, GRID_W]), ALU.add).then_inc(bias_ready, 1)
                    if n == 3:
                        pool.wait_ge(kct_r, p + 1)
                        pool.dma_start(new_k[:, bass.ds(p * P, P)], nk[:]).then_inc(nk_out, 16)
                        pool.dma_start(new_v[:, bass.ds(p * P, P)], vt[:, 0, :]).then_inc(nv_out, 16)
                        pool.wait_ge(nk_out, p * 16 + 16)
                        pool.wait_ge(nv_out, p * 16 + 16)
                pool.wait_ge(o_ready, 2 * p + 4)
                pool.dma_start(o_d[bass.ds(p, 1)].rearrange("o p t -> p (o t)"), ot[:]).then_inc(o_out, 16)
                pool.wait_ge(o_out, p * 16 + 16)
                pool.sem_inc(pair_used, 1)

        def unit(u):
            return u // U, u % U

        @block.tensor
        def _(pe):
            pe.wait_ge(pre_in, 16)
            with pe.Fori(0, NAH // 2) as p:
                pe.wait_ge(pair_in, p * 80 + 80)
                pe.wait_ge(ptd, p * UP + 1)
                pe.transpose(ps_t[:, 0:P], ck[:], ident[:])
                pe.transpose(ps_t[:, P:2 * P], ktile[:, 0:TP], ident[:]).then_inc(kct_t, 1)
                pe.wait_ge(kct_r, p + 1)
                pe.wait_ge(q_ready, p + 1)

                def scores(u):
                    hh, tile = unit(u)
                    s = u % 2
                    pe.wait_ge(maxed, p * UP + u + 1)
                    if tile == 0:
                        mm = pe.matmul(ps_s[:, s, 512:512 + TP], qpad[:, hh, 0:TP], ktile[:, 0:TP], start=True, stop=True)
                    else:
                        pe.matmul(ps_s[:, s, 0:512], qpad[:, hh, tile * P:(tile + 1) * P], ktile[:, TP:T], start=True, stop=True)
                        mm = pe.matmul(ps_s[:, s, 512:512 + P], qpad[:, hh, tile * P:(tile + 1) * P], kct[:], start=True, stop=True)
                    mm.then_inc(scored, 1)

                def values(u):
                    hh, tile = unit(u)
                    pe.wait_ge(normed, p * UP + u + 1)
                    pe.wait_ge(ptd, p * UP + u + 1)
                    first = 4 if tile == 0 else 0
                    for j in range(first, 5):
                        tr = pe.transpose(ps_t[:, j * P:(j + 1) * P], pr[:, u % 2, j * P:(j + 1) * P], ident[:])
                    tr.then_inc(turned, 1)
                    pe.wait_ge(ptd, p * UP + u + 2)
                    if u == 0:
                        pe.wait_ge(o_ready, 2 * p + 2)
                    dst = ps_o[hh * DH:(hh + 1) * DH, 1, 0:TP] if tile == 0 else ps_o[hh * DH:(hh + 1) * DH, 0, (tile - 1) * P:tile * P]
                    for j in range(first, 5):
                        if tile == 0:
                            vv = vt[:, 0, hh * DH:(hh + 1) * DH]
                        elif j < 4:
                            vv = vt[:, 1 + j, hh * DH:(hh + 1) * DH]
                        else:
                            vv = cv[:, hh * DH:(hh + 1) * DH]
                        mm = pe.matmul(dst, vv, pt[:, u % 2, j * P:(j + 1) * P], start=(j == first), stop=(j == 4))
                    mm.then_inc(pvd, 1)

                scores(0)
                for u in range(UP):
                    if u + 1 < UP:
                        scores(u + 1)
                    values(u)

        @block.vector
        def _(dve):
            dve.sem_inc(maxed, 2)
            dve.sem_inc(ptd, 1)
            dve.sem_inc(pvd, 1)
            dve.sem_inc(o_ready, 2)
            dve.sem_inc(turned, 2)
            with dve.Fori(0, NAH // 2) as p:
                dve.wait_ge(pair_in, p * 80 + 80)
                dve.wait_ge(kct_t, p + 1)
                nc.vector.tensor_copy(kct[:], ps_t[:, 0:P])
                nc.vector.tensor_copy(nk[:], ps_t[:, P:2 * P]).then_inc(kct_r, 1)
                nc.vector.tensor_scalar(qpad[0:DH, 0, :], qt[0:DH, :], QS, None, ALU.mult)
                nc.vector.tensor_scalar(qpad[DH:P, 1, :], qt[DH:P, :], QS, None, ALU.mult).then_inc(q_ready, 1)

                def maximum(u):
                    hh, tile = unit(u)
                    s = u % 2
                    dve.wait_ge(scored, p * UP + u + 1)
                    if tile == 0:
                        nc.vector.tensor_copy(sc[:, s, 512:T], ps_s[:, s, 512:T])
                        nc.vector.tensor_reduce(mx[:, s:s + 1], ps_s[:, s, 512:T], AX_X, ALU.max).then_inc(maxed, 1)
                    else:
                        n = 4 * hh + tile - 1
                        dve.wait_ge(bias_ready, p * 8 + n + 1)
                        dve.sem_inc(begun, 1)
                        nc.vector.tensor_tensor_reduce(sc[:, s, :], ps_s[:, s, 0:T], bias[:, n % 2, :], 1.0, NEG,
                                                       ALU.add, ALU.max, mx[:, s:s + 1]).then_inc(maxed, 1)
                    dve.wait_ge(maxed, p * UP + u + 3)
                    if tile:
                        dve.sem_inc(bias_used, 1)
                    nc.vector.tensor_scalar(nmx[:, s:s + 1], mx[:, s:s + 1], -1.0, None, ALU.mult).then_inc(negd, 1)

                def normalise(u):
                    _, tile = unit(u)
                    s = u % 2
                    c0 = 512 if tile == 0 else 0
                    dve.wait_ge(expd, p * UP + u + 1)
                    nc.vector.reciprocal(rc[:, s:s + 1], sm[:, s:s + 1]).then_inc(rcd, 1)
                    dve.wait_ge(rcd, p * UP + u + 1)
                    nc.vector.tensor_scalar(pr[:, s, c0:T], pr[:, s, c0:T], rc[:, s:s + 1], None, ALU.mult).then_inc(normed, 1)

                maximum(0)
                for u in range(UP):
                    if u + 1 < UP:
                        maximum(u + 1)
                    normalise(u)

        @block.scalar
        def _(act):
            with act.Fori(0, NAH // 2) as p:
                def exponent(u):
                    _, tile = unit(u)
                    s = u % 2
                    c0 = 512 if tile == 0 else 0
                    act.wait_ge(negd, p * UP + u + 1)
                    act.wait_ge(turned, p * UP + u + 1)
                    nc.scalar.activation(pr[:, s, c0:T], sc[:, s, c0:T], ACT.Exp, bias=nmx[:, s:s + 1],
                                         accum_out=sm[:, s:s + 1]).then_inc(expd, 1)

                def copy_turned(u):
                    _, tile = unit(u)
                    c0 = 512 if tile == 0 else 0
                    act.wait_ge(turned, p * UP + u + 3)
                    nc.scalar.copy(pt[:, u % 2, c0:T], ps_t[:, c0:T]).then_inc(ptd, 1)

                exponent(0)
                for u in range(UP):
                    if u + 1 < UP:
                        exponent(u + 1)
                    copy_turned(u)
                act.wait_ge(pvd, p * UP + UP + 1)
                act.wait_ge(pair_used, p + 1)
                nc.scalar.copy(ot[:, TP:T], ps_o[:, 0, :]).then_inc(o_ready, 1)
                nc.scalar.copy(ot[:, 0:TP], ps_o[:, 1, 0:TP]).then_inc(o_ready, 1)


def block_rwkv(nc, z_d, kk_d, par_d, w2, a2, state, ident_d, o_raw_d, state_out):
    LAM = float(np.exp(-0.5))
    LEVELS = [2, 4, 8, 16, 32]
    BATCH = [(0, 4), (4, 8), (8, 10)]
    R = 4
    ORDER = [list(range(NCK)), list(range(NCP))[::-1] + list(range(NCP, NCK))[::-1]]

    plan = [("w", 0, 0), ("a", 0, 0), ("wa", 0, 0)]
    plan += [("vt", 0, b) for b in range(3)] + [("bk", 0, b) for b in range(5)] + [("sc", 0, c) for c in range(NCK)]
    plan += [("w", 1, 0), ("a", 1, 0), ("wa", 1, 0), ("s0", 0, 0), ("s0", 1, 0)]

    def inverse(d):
        jobs = [("ti", d, b) for b in range(3)]
        for lv in range(len(LEVELS)):
            jobs += [("x", d, b, lv) for b in range(3)]
            for b in range(3):
                jobs += [("dt", d, b, lv)] if lv < len(LEVELS) - 1 else []
                jobs += [("dtt", d, b, lv)]
        return jobs

    plan += inverse(0) + [("bk", 1, b) for b in range(5)] + [("sc", 1, c) for c in range(NCK)] + inverse(1)
    plan += [("so", 0, 0)]
    NJ = len(plan)
    assert NJ % R == 0, NJ
    on_act = [j[0] in ("w", "a", "wa", "vt", "bk", "ti", "s0", "so") for j in plan]
    NA, ND = sum(on_act), NJ - sum(on_act)
    index = {j: n for n, j in enumerate(plan)}

    with ExitStack() as ctx:
        def sb(name, shape):
            return ctx.enter_context(nc.sbuf_tensor("rw_" + name, shape, F32))

        def sem(name):
            return nc.alloc_semaphore("rw_" + name)

        ident, par, pp = sb("ident", [P, P]), sb("par", [P, 72]), sb("pp", [P, 10])
        mask = sb("mask", [P, 2, 192])
        join = sb("join", [P, 7, P])
        reset = sb("reset", [P, T])
        xwa = sb("xwa", [P, T])
        w2p, a2p = sb("w2p", [P, 2, P]), sb("a2p", [P, 2, P])
        rt, kt, vt, kk = sb("rt", [P, T]), sb("kt", [P, T]), sb("vt", [P, T]), sb("kk", [P, T])
        sg, ar, cs, pq, qq = sb("sg", [P, T]), sb("ar", [P, T]), sb("cs", [P, T]), sb("pq", [P, T]), sb("qq", [P, T])
        e_in, e_ex, e_inv = sb("e_in", [P, T]), sb("e_ex", [P, T]), sb("e_inv", [P, T])
        bb, kd, hc = sb("bb", [P, T]), sb("kd", [P, T]), sb("hc", [P, NCK])
        halves = sb("halves", [P, NCK])
        ec = sb("ec", [P, 2, NCK])
        bkpad = sb("bkpad", [P, 2, NCK, 2, CK])
        vpad = sb("vpad", [P, NCK, 2, CK])
        apad = sb("apad", [P, 2, NCK, 2, CK])
        rbar = sb("rbar", [P, 2, T])
        bktok = sb("bktok", [P, 2, 2 * NCK, P])
        vtok = sb("vtok", [P, NCK, P])
        sc = sb("sc", [P, 2, NCK, 2, 192])
        tm, xm = sb("tm", [P, NCK, P]), sb("xm", [P, NCK, P])
        tt = sb("tt", [P, 2, NCK, P])
        sin, s0, st, tmp, fs, fo = (sb(n, [P, 2, P]) for n in ("sin", "s0", "st", "tmp", "fs", "fo"))
        wsb, usb = sb("wsb", [P, 2, P]), sb("usb", [P, 2, P])
        of = sb("of", [P, 2, T])
        osum = sb("osum", [P, T])
        rot = ctx.enter_context(nc.psum_tensor("rw_rot", [P, R, 512], F32))
        wu = ctx.enter_context(nc.psum_tensor("rw_wu", [P, 2, 512], F32))
        zo = ctx.enter_context(nc.psum_tensor("rw_zo", [P, 2, 512], F32))

        once_in, loads, loads_free, made = sem("once"), sem("loads"), sem("loadsfree"), sem("made")
        job, act_ev, dve_ev = sem("job"), sem("actev"), sem("dveev")
        par_ready, xwa_ready = sem("parrdy"), sem("xwardy")
        cs_done, pq_done, bk_done, ex_done, rb_done, pad_done, vpad_done = (sem(n) for n in ("cs", "pq", "bk", "ex", "rb", "pad", "vpad"))
        tinit, seq_done, gch, dch = sem("tinit"), sem("seq"), sem("gch"), sem("dch")
        w_done, w_ev, u_done, u_ev, z_done, z_ev, o_ev, s_ready = ([sem(n + "0"), sem(n + "1")] for n in
            ("wd", "we", "ud", "ue", "zd", "ze", "oe", "sr"))
        fs_done, fo_out, osum_done, o_out = sem("fs"), sem("foout"), sem("osum"), sem("oout")
        block = ctx.enter_context(nc.Block())

        @block.sync
        def _(sp):
            sp.dma_start(ident[:], ident_d).then_inc(once_in, 16)
            sp.dma_start(par[:], par_d).then_inc(once_in, 16)
            sp.dma_start(xwa[:], z_d[ZX]).then_inc(once_in, 16)
            sp.wait_ge(made, 1)
            with sp.Fori(0, NPAIR) as p:
                sp.wait_ge(loads_free, p + 1)
                for dst, row in ((rt, ZR), (kt, ZKC), (vt, ZV)):
                    sp.dma_start(dst[:], z_d[bass.ds(row + p, 1)].rearrange("o p t -> p (o t)")).then_inc(loads, 16)
                sp.dma_start(kk[:], kk_d[bass.ds(p, 1)].rearrange("o p t -> p (o t)")).then_inc(loads, 16)
                for d in range(2):
                    sp.dma_start(w2p[0:64, d, :], w2[0, d, :, bass.ds(p * P, P)]).then_inc(loads, 16)
                    sp.dma_start(a2p[64:P, d, :], a2[0, d, :, bass.ds(p * P, P)]).then_inc(loads, 16)
                    for hh in range(2):
                        sp.dma_start(sin[hh * DH:(hh + 1) * DH, d, hh * DH:(hh + 1) * DH],
                                     state[d, bass.ds(2 * p + hh, 1)].rearrange("o v k -> (o v) k")).then_inc(loads, 16)
            sp.wait_ge(o_out, 16 * NPAIR)
            sp.wait_ge(fo_out, 16 * 4 * NPAIR)
        NLOAD = 12 * 16

        @block.gpsimd
        def _(pool):
            ch = Chain(pool, gch)
            for t in (w2p, a2p, sin, bkpad, vpad, apad):
                last = nc.gpsimd.memset(t[:], 0.0)
            last.then_inc(made, 1)
            ch.link(nc.gpsimd.memset(mask[:], 1.0))
            for d in range(2):
                sgn = 1 if d == 0 else -1
                m = mask[:, d, 0:P]
                ch.link(nc.gpsimd.affine_select(out=m, in_=m, compare_op=ALU.is_gt, fill=0.0, base=0,
                                                pattern=[[sgn, P]], channel_multiplier=-sgn))
                for hh in range(2):
                    m = mask[hh * CK:(hh + 1) * CK, d, P:P + CK]
                    ch.link(nc.gpsimd.affine_select(out=m, in_=m, compare_op=ALU.is_ge, fill=0.0, base=0,
                                                    pattern=[[sgn, CK]], channel_multiplier=-sgn))
            ch.link(nc.gpsimd.memset(join[:], 1.0))
            for i in range(7):
                n = 2 ** i
                m = join[:, i, :].rearrange("p (b n) -> p b n", n=n)
                ch.link(nc.gpsimd.affine_select(out=m, in_=m, compare_op=ALU.is_ge, fill=0.0, base=0,
                                                pattern=[[-n, P // n], [0, n]], channel_multiplier=1))
                ch.link(nc.gpsimd.affine_select(out=m, in_=m, compare_op=ALU.is_ge, fill=0.0, base=n - 1,
                                                pattern=[[n, P // n], [0, n]], channel_multiplier=-1))
            for i in range(6):
                ch.link(nc.gpsimd.tensor_tensor(join[:, i, :], join[:, i + 1, :], join[:, i, :], ALU.subtract))
            ch.link(nc.gpsimd.memset(halves[:], 0.5))
            ch.link(nc.gpsimd.memset(reset[:], 1.0))
            ch.link(nc.gpsimd.memset(reset[:].rearrange("p (c t) -> p c t", t=CK)[:, :, 0:1], 0.0))
            pool.sem_inc(made, 1)
            pool.sem_inc(loads_free, 1)
            pool.sem_inc(act_ev, NA)
            pool.sem_inc(dve_ev, ND)
            pool.sem_inc(seq_done, 1)
            pool.sem_inc(pad_done, 1)
            pool.sem_inc(rb_done, 1)
            for d in range(2):
                pool.sem_inc(o_ev[d], NCK)
                pool.sem_inc(z_ev[d], NCK)
                pool.sem_inc(u_ev[d], NCK)
            pool.sem_inc(osum_done, 1)

            def c3(t):
                return t.rearrange("p (c t) -> p c t", t=CK)

            with pool.Fori(0, NPAIR) as p:
                for d in range(2):
                    g = 2 * p + d
                    pool.wait_ge(cs_done, g + 1)
                    nc.gpsimd.tensor_tensor(hc[:], c3(cs[:])[:, :, CK - 1], halves[:], ALU.mult).then_inc(pq_done, 1)
                    pool.wait_ge(pq_done, 3 * g + 1)
                    nc.gpsimd.tensor_tensor(c3(pq[:]), c3(cs[:]), hc[:].unsqueeze(2).to_broadcast([P, NCK, CK]), ALU.subtract).then_inc(pq_done, 1)
                    pool.wait_ge(pq_done, 3 * g + 2)
                    nc.gpsimd.tensor_tensor(qq[:], pq[:], sg[:], ALU.subtract).then_inc(pq_done, 1)
                    nc.gpsimd.tensor_tensor(bb[:], kk[:], ar[:], ALU.mult)
                    nc.gpsimd.tensor_scalar(kd[:], ar[:], pp[:, 1:2], pp[:, 9:10], ALU.mult, ALU.add).then_inc(bk_done, 1)
                    pool.wait_ge(bk_done, 2 * g + 1)
                    nc.gpsimd.tensor_tensor(kd[:], kd[:], kt[:], ALU.mult).then_inc(bk_done, 1)
                    pool.wait_ge(seq_done, p + 1)
                    pool.wait_ge(ex_done, g + 1)
                    nc.gpsimd.tensor_tensor(rbar[:, d, :], rt[:], e_in[:], ALU.mult).then_inc(rb_done, 1)
                    pool.wait_ge(dve_ev, (p + 1) * ND + sum(not on_act[n] for n in range(index[("sc", d, NCK - 1)] + 1)))
                    nc.gpsimd.tensor_tensor(tt[:, d], sc[:, d, :, 0, 0:P], join[:, 0:1, :].to_broadcast([P, NCK, P]), ALU.mult).then_inc(tinit, 1)
                    pool.wait_ge(tinit, 2 * g + 1)
                    nc.gpsimd.tensor_tensor(tt[:, d], tt[:, d], ident[:].unsqueeze(1).to_broadcast([P, NCK, P]), ALU.add).then_inc(tinit, 1)
                    if d == 1:
                        pool.wait_ge(vpad_done, p + 1)
                        pool.wait_ge(pad_done, 2 * p + 3)
                        pool.wait_ge(act_ev, (p + 1) * NA + sum(on_act[n] for n in range(index[("s0", 1, 0)] + 1)))
                        pool.wait_ge(rb_done, 2 * p + 3)
                        pool.sem_inc(loads_free, 1)
                for d in range(2):
                    pool.wait_ge(o_ev[d], (p + 2) * NCK)
                nc.gpsimd.tensor_tensor(osum[:], of[:, 0, :], of[:, 1, :], ALU.add).then_inc(osum_done, 1)
                pool.wait_ge(osum_done, p + 2)
                pool.dma_start(o_raw_d[bass.ds(p, 1)].rearrange("o p t -> p (o t)"), osum[:]).then_inc(o_out, 16)
                for d in range(2):
                    for hh in range(2):
                        pool.dma_start(state_out[d, bass.ds(2 * p + hh, 1)].rearrange("o v k -> (o v) k"),
                                       fo[hh * DH:(hh + 1) * DH, d, hh * DH:(hh + 1) * DH]).then_inc(fo_out, 16)
                pool.wait_ge(o_out, p * 16 + 16)
                pool.wait_ge(fo_out, p * 64 + 64)

        def evacuated(n):
            return on_act[n], sum(on_act[m] == on_act[n] for m in range(n))

        @block.tensor
        def _(pe):
            pe.wait_ge(once_in, 48)
            pe.wait_ge(made, 2)
            pe.wait_ge(xwa_ready, 1)
            with pe.Fori(0, NPAIR) as p:
                def run_job(n):
                    kind, d, b = plan[n][0:3]
                    bank = rot[:, n % R]
                    reads = []
                    if kind in ("x", "dt", "dtt"):
                        lv = plan[n][3]
                        if kind == "x":
                            reads = [("ti", d, b) if lv == 0 else ("dt", d, b, lv - 1)]
                        elif kind == "dt" or lv == len(LEVELS) - 1:
                            reads = [("x", d, b, lv)]
                    for a, sem_, per in ((True, act_ev, NA), (False, dve_ev, ND)):
                        counts = [evacuated(m)[1] + 1 for m in [index[r] for r in reads] + ([n - R] if n >= R else []) if on_act[m] == a]
                        if counts:
                            pe.wait_ge(sem_, (p + 1) * per + max(counts))
                        elif n < R and on_act[n - R + NJ] == a:
                            pe.wait_ge(sem_, p * per + evacuated(n - R + NJ)[1] + 1)
                    if kind in ("w", "a"):
                        if n == 0:
                            pe.wait_ge(loads, p * NLOAD + NLOAD)
                        mm = pe.matmul(bank, (w2p if kind == "w" else a2p)[:, d, :], xwa[:, TP:T], start=True, stop=True)
                    elif kind == "wa":
                        pe.matmul(bank[:, 0:TP], w2p[:, d, :], xwa[:, 0:TP], start=True, stop=True)
                        mm = pe.matmul(bank[:, TP:2 * TP], a2p[:, d, :], xwa[:, 0:TP], start=True, stop=True)
                    elif kind == "s0":
                        mm = pe.transpose(bank[:, 0:P], sin[:, d, :], ident[:])
                    elif kind == "vt":
                        pe.wait_ge(vpad_done, p + 1)
                        for i, c in enumerate(range(*BATCH[b])):
                            mm = pe.transpose(bank[:, i * P:(i + 1) * P], vpad[:, c].rearrange("p h t -> p (h t)"), ident[:])
                    elif kind == "bk":
                        pe.wait_ge(pad_done, 2 * p + d + 2)
                        for i in range(4):
                            m = 4 * b + i
                            mm = pe.transpose(bank[:, i * P:(i + 1) * P], bkpad[:, m // NCK, m % NCK].rearrange("p h t -> p (h t)"), ident[:])
                    elif kind == "sc":
                        pe.wait_ge(rb_done, 2 * p + d + 2)
                        c = b
                        for i in range(2):
                            lhs = bkpad[:, i, c].rearrange("p h t -> p (h t)")
                            pe.matmul(bank[:, i * 192:i * 192 + P], lhs, apad[:, d, c].rearrange("p h t -> p (h t)"), start=True, stop=True)
                            mm = pe.matmul(bank[:, i * 192 + P:(i + 1) * 192], lhs, rbar[:, d, c * CK:(c + 1) * CK], start=True, stop=True)
                    elif kind == "ti":
                        pe.wait_ge(tinit, 4 * p + 2 * d + 2)
                        for i, c in enumerate(range(*BATCH[b])):
                            mm = pe.transpose(bank[:, i * P:(i + 1) * P], tt[:, d, c, :], ident[:])
                    else:
                        for i, c in enumerate(range(*BATCH[b])):
                            lhs, rhs = {"x": (sc[:, d, c, 0, 0:P], tm[:, c, :]), "dt": (tt[:, d, c, :], xm[:, c, :]),
                                        "dtt": (xm[:, c, :], tt[:, d, c, :])}[kind]
                            mm = pe.matmul(bank[:, i * P:(i + 1) * P], lhs, rhs, start=True, stop=True)
                    mm.then_inc(job, 1)

                for n in range(NJ - 1):
                    run_job(n)
                pe.wait_ge(dve_ev, (p + 2) * ND)
                for i in range(NCK):
                    for d in range(2):
                        c = ORDER[d][i]
                        q = p * NCK + i
                        pe.wait_ge(z_ev[d], q + NCK)
                        pe.wait_ge(o_ev[d], q + NCK)
                        pe.wait_ge(u_ev[d], q + NCK)
                        pe.matmul(zo[:, d, 0:P], bktok[:, d, NCK + c, :], vtok[:, c, :], start=True, stop=False, skip_group_check=True)
                        pe.matmul(zo[:, d, P:P + CK], vtok[:, c, :], sc[:, d, c, 1, P:192], start=False, stop=False, skip_group_check=True)
                        pe.matmul(wu[:, d, 0:P], sc[:, d, c, 1, 0:P], vtok[:, c, :], start=True, stop=False)
                    for d in range(2):
                        c = ORDER[d][i]
                        q = p * NCK + i
                        pe.wait_ge(s_ready[d], q + 1)
                        pe.matmul(wu[:, d, 0:P], apad[:, d, c].rearrange("p h t -> p (h t)"), st[:, d, :], start=False, stop=True).then_inc(w_done[d], 1)
                        pe.matmul(zo[:, d, P:P + CK], st[:, d, :], rbar[:, d, c * CK:(c + 1) * CK], start=False, stop=False, skip_group_check=True)
                    for d in range(2):
                        c = ORDER[d][i]
                        pe.wait_ge(w_ev[d], p * NCK + i + 1)
                        pe.matmul(wu[:, d, P:2 * P], tt[:, d, c, :], wsb[:, d, :], start=True, stop=True).then_inc(u_done[d], 1)
                    for d in range(2):
                        c = ORDER[d][i]
                        pe.wait_ge(u_ev[d], p * NCK + i + 1 + NCK)
                        pe.matmul(zo[:, d, 0:P], bktok[:, d, c, :], usb[:, d, :], start=False, stop=True, skip_group_check=True)
                        mm = pe.matmul(zo[:, d, P:P + CK], usb[:, d, :], sc[:, d, c, 0, P:192], start=False, stop=True, skip_group_check=True)
                        mm.then_inc(z_done[d], 1)
                    if i == NCP:
                        a, o = evacuated(NJ - 1 - R)
                        pe.wait_ge(act_ev if a else dve_ev, (p + 1) * (NA if a else ND) + o + 1)
                        pe.wait_ge(fs_done, 2 * p + 2)
                        pe.transpose(rot[:, (NJ - 1) % R, 0:P], fs[:, 0, :], ident[:])
                        pe.transpose(rot[:, (NJ - 1) % R, P:2 * P], fs[:, 1, :], ident[:]).then_inc(job, 1)
                for d in range(2):
                    pe.wait_ge(z_ev[d], (p + 2) * NCK)
                pe.sem_inc(seq_done, 1)

        @block.scalar
        def _(act):
            act.wait_ge(once_in, 48)
            nc.scalar.activation(xwa[0:64, :], xwa[0:64, :], ACT.Tanh).then_inc(xwa_ready, 1)
            with act.Fori(0, NPAIR) as p:
                def empty(n):
                    kind, d, b = plan[n][0:3]
                    bank = rot[:, n % R]
                    act.wait_ge(job, p * NJ + n + 1)
                    if kind == "w":
                        act.wait_ge(par_ready, 2 * p + 2)
                        act.wait_ge(rb_done, 2 * p + d + 1)
                        act.wait_ge(pad_done, 2 * p + d + 1)
                        a = nc.scalar.activation(sg[:, TP:T], bank, ACT.Sigmoid, bias=pp[:, 5 + d:6 + d])
                    elif kind == "a":
                        a = nc.scalar.activation(ar[:, TP:T], bank, ACT.Sigmoid, bias=pp[:, 7 + d:8 + d])
                    elif kind == "wa":
                        nc.scalar.activation(sg[:, 0:TP], bank[:, 0:TP], ACT.Sigmoid, bias=pp[:, 5 + d:6 + d])
                        a = nc.scalar.activation(ar[:, 0:TP], bank[:, TP:2 * TP], ACT.Sigmoid, bias=pp[:, 7 + d:8 + d])
                    elif kind == "s0":
                        a = nc.scalar.copy(s0[:, d, :], bank[:, 0:P])
                    elif kind == "so":
                        a = nc.scalar.copy(fo[:].rearrange("p d k -> p (d k)"), bank[:, 0:2 * P])
                    elif kind == "vt":
                        c0, c1 = BATCH[b]
                        a = nc.scalar.copy(vtok[:, c0:c1, :].rearrange("p c k -> p (c k)"), bank[:, 0:(c1 - c0) * P])
                    elif kind == "bk":
                        a = nc.scalar.copy(bktok[:, d, 4 * b:4 * b + 4, :].rearrange("p c k -> p (c k)"), bank)
                    elif kind == "ti":
                        c0, c1 = BATCH[b]
                        a = nc.scalar.copy(tm[:, c0:c1, :].rearrange("p c k -> p (c k)"), bank[:, 0:(c1 - c0) * P])
                    a.then_inc(act_ev, 1)

                def exponentials(d):
                    act.wait_ge(pq_done, 6 * p + 3 * d + 3)
                    s = LAM if d else -LAM
                    nc.scalar.activation(e_in[:], (qq if d else pq)[:], ACT.Exp, scale=s)
                    nc.scalar.activation(e_ex[:], (pq if d else qq)[:], ACT.Exp, scale=s)
                    nc.scalar.activation(e_inv[:], (qq if d else pq)[:], ACT.Exp, scale=-s)
                    nc.scalar.activation(ec[:, d, :], hc[:], ACT.Exp, scale=-LAM).then_inc(ex_done, 1)

                act.wait_ge(loads, p * NLOAD + NLOAD)
                act.wait_ge(seq_done, p + 1)
                nc.scalar.copy(vpad[0:64, :, 0, :], vt[0:64, :].rearrange("p (c t) -> p c t", t=CK))
                nc.scalar.copy(vpad[64:P, :, 1, :], vt[64:P, :].rearrange("p (c t) -> p c t", t=CK)).then_inc(vpad_done, 1)
                for n in range(NJ - 1):
                    if on_act[n]:
                        empty(n)
                    if plan[n][0] == "wa":
                        if plan[n][1] == 0:
                            exponentials(0)
                    if plan[n] == ("ti", 0, 2):
                        exponentials(1)
                for i in range(NCK):
                    for d in range(2):
                        act.wait_ge(w_done[d], p * NCK + i + 1)
                        nc.scalar.copy(wsb[:, d, :], wu[:, d, 0:P]).then_inc(w_ev[d], 1)
                    for d in range(2):
                        act.wait_ge(u_done[d], p * NCK + i + 1)
                        nc.scalar.copy(usb[:, d, :], wu[:, d, P:2 * P]).then_inc(u_ev[d], 1)
                    for d in range(2):
                        c = ORDER[d][i]
                        act.wait_ge(z_done[d], p * NCK + i + 1)
                        act.wait_ge(z_ev[d], p * NCK + i + 1 + NCK)
                        if i == 0:
                            act.wait_ge(osum_done, p + 1)
                        nc.scalar.copy(of[:, d, c * CK:(c + 1) * CK], zo[:, d, P:P + CK]).then_inc(o_ev[d], 1)
                    if i == NCP:
                        empty(NJ - 1)

        @block.vector
        def _(dve):
            dve.wait_ge(once_in, 48)
            dve.wait_ge(made, 2)
            p9 = par[:].rearrange("p (v k) -> p v k", k=NPAIR)
            with dve.Fori(0, NPAIR) as p:
                def empty(n):
                    kind, d, b = plan[n][0:3]
                    bank = rot[:, n % R]
                    dve.wait_ge(job, p * NJ + n + 1)
                    if kind == "sc":
                        a = nc.vector.tensor_tensor(sc[:, d, b], bank[:, 0:384].rearrange("p (i n) -> p i n", i=2),
                                                    mask[:, d:d + 1, :].to_broadcast([P, 2, 192]), ALU.mult)
                    else:
                        lv = plan[n][3]
                        c0, c1 = BATCH[b]
                        src = bank[:, 0:(c1 - c0) * P].rearrange("p (c k) -> p c k", k=P)
                        if kind == "x":
                            a = nc.vector.tensor_tensor(xm[:, c0:c1, :], src, join[:, lv + 1:lv + 2, :].to_broadcast([P, c1 - c0, P]), ALU.mult)
                        else:
                            t = tm[:, c0:c1, :] if kind == "dt" else tt[:, d, c0:c1, :]
                            a = nc.vector.tensor_tensor(t, src, t, ALU.add)
                    a.then_inc(dve_ev, 1)

                def scan(d):
                    dve.wait_ge(act_ev, (p + 1) * NA + sum(on_act[n] for n in range(index[("wa", d, 0)] + 1)))
                    nc.vector.tensor_tensor_scan(cs[:], reset[:], sg[:], 0.0, ALU.mult, ALU.add).then_inc(cs_done, 1)

                def padded(d):
                    dve.wait_ge(ex_done, 2 * p + d + 1)
                    dve.wait_ge(bk_done, 4 * p + 2 * d + 2)
                    dve.wait_ge(seq_done, p + 1)
                    if d == 1:
                        dve.wait_ge(job, p * NJ + index[("sc", 0, NCK - 1)] + 1)
                    for hh in range(2):
                        rows = slice(hh * DH, (hh + 1) * DH)

                        def c3(t):
                            return t[rows, :].rearrange("p (c t) -> p c t", t=CK)
                        nc.vector.scalar_tensor_tensor(apad[rows, d, :, hh, :], c3(kk), -1.0, c3(e_ex), ALU.mult, ALU.mult)
                        nc.vector.tensor_tensor(bkpad[rows, 0, :, hh, :], c3(bb), c3(e_inv), ALU.mult)
                        a = nc.vector.tensor_tensor(bkpad[rows, 1, :, hh, :], c3(kd), c3(e_inv), ALU.mult)
                    a.then_inc(pad_done, 1)

                dve.wait_ge(pad_done, 2 * p + 1)
                nc.vector.tensor_copy(pp[:, 0:9], p9[:, :, bass.ds(p, 1)].rearrange("p v o -> p (v o)")).then_inc(par_ready, 1)
                dve.wait_ge(par_ready, 2 * p + 1)
                nc.vector.tensor_scalar(pp[:, 9:10], pp[:, 1:2], -1.0, 1.0, ALU.mult, ALU.add).then_inc(par_ready, 1)
                scan(0)
                padded(0)
                for n in range(NJ - 1):
                    if not on_act[n]:
                        empty(n)
                    if plan[n] == ("x", 0, 2, 0):
                        scan(1)
                    if plan[n] == ("dtt", 0, 2, 2):
                        padded(1)
                for d in range(2):
                    nc.vector.memset(st[:, d, :], 0.0).then_inc(s_ready[d], 1)
                for i in range(NCK):
                    for d in range(2):
                        c = ORDER[d][i]
                        nx = ORDER[d][i + 1] if i + 1 < NCK else None
                        dve.wait_ge(z_done[d], p * NCK + i + 1)
                        nc.vector.tensor_tensor(tmp[:, d, :], zo[:, d, 0:P], st[:, d, :], ALU.add).then_inc(z_ev[d], 1)
                        dve.wait_ge(z_ev[d], p * NCK + i + 1 + NCK)
                        if i == NCP - 1:
                            nc.vector.tensor_scalar(fs[:, d, :], tmp[:, d, :], ec[:, d, c:c + 1], None, ALU.mult).then_inc(fs_done, 1)
                            nc.vector.tensor_scalar(st[:, d, :], s0[:, d, :], ec[:, d, nx:nx + 1], None, ALU.mult).then_inc(s_ready[d], 1)
                        elif nx is not None:
                            nc.vector.tensor_scalar(st[:, d, :], tmp[:, d, :], ec[:, d, c:c + 1], ec[:, d, nx:nx + 1],
                                                    ALU.mult, ALU.mult).then_inc(s_ready[d], 1)


def block_rwkv_output(nc, z_d, o_raw_d, par_d, g2, ident_d, o_d):
    with ExitStack() as ctx:
        def sb(name, shape):
            return ctx.enter_context(nc.sbuf_tensor("ro_" + name, shape, F32))

        def sem(name):
            return nc.alloc_semaphore("ro_" + name)

        par, g2s, sx = sb("par", [P, 72]), sb("g2s", [P, RW]), sb("sx", [P, T])
        mean_w, sum_w, eps = sb("mean_w", [P, P]), sb("sum_w", [P, P]), sb("eps", [P, 1])
        o, rt, kt, vt = (sb(n, [P, 2, T]) for n in ("o", "r", "k", "v"))
        sq, rs, bo = (sb(n, [P, 2, T]) for n in ("sq", "rs", "bo"))
        ps = [ctx.enter_context(nc.psum_tensor(f"ro_{n}", [P, 1024], F32)) for n in ("mean", "var", "bonus", "gate")]
        once, made, sx_done, ch = sem("once"), sem("made"), sem("sx"), sem("ch")
        loads = (sem("load0"), sem("load1"))
        meaned, centred, squared, vard, rsd, rk_done, bonused, done, out = (sem(n) for n in
            ("meaned", "centred", "squared", "vard", "rsd", "rk", "bonused", "done", "out"))
        block = ctx.enter_context(nc.Block())

        @block.sync
        def _(sp):
            sp.dma_start(par[:], par_d).then_inc(once, 16)
            sp.dma_start(g2s[:], g2[0]).then_inc(once, 16)
            sp.dma_start(sx[:], z_d[ZX + 1]).then_inc(once, 16)
            for p in range(NPAIR):
                if p >= 2:
                    sp.wait_ge(out, 16 * (p - 1))
                sp.dma_start(o[:, p % 2, :], o_raw_d[p]).then_inc(loads[p % 2], 16)
                for dst, row in ((rt, ZR), (kt, ZKC), (vt, ZV)):
                    sp.dma_start(dst[:, p % 2, :], z_d[row + p]).then_inc(loads[p % 2], 16)
                if p >= 1:
                    sp.wait_ge(done, p)
                    sp.dma_start(o_d[8 + p - 1], o[:, (p - 1) % 2, :]).then_inc(out, 16)
            sp.wait_ge(done, NPAIR)
            sp.dma_start(o_d[8 + NPAIR - 1], o[:, (NPAIR - 1) % 2, :]).then_inc(out, 16)
            sp.wait_ge(out, 16 * NPAIR)

        @block.tensor
        def _(pe):
            pe.wait_ge(made, 1)
            pe.wait_ge(sx_done, 1)

            def both(dst, lhs, rhs):
                pe.matmul(dst[:, 0:512], lhs, rhs[:, 0:512], start=True, stop=True)
                return pe.matmul(dst[:, 512:T], lhs, rhs[:, 512:T], start=True, stop=True)

            for p in range(NPAIR):
                s = p % 2
                pe.wait_ge(loads[s], 64 * (p // 2 + 1))
                if p:
                    pe.wait_ge(done, p)
                both(ps[0], mean_w[:], o[:, s, :]).then_inc(meaned, 1)
                pe.wait_ge(rk_done, p + 1)
                both(ps[2], sum_w[:], bo[:, s, :])
                both(ps[3], g2s[:, p * P:(p + 1) * P], sx[:]).then_inc(bonused, 1)
                pe.wait_ge(squared, p + 1)
                both(ps[1], mean_w[:], sq[:, s, :]).then_inc(vard, 1)

        @block.scalar
        def _(act):
            act.wait_ge(once, 48)
            nc.scalar.activation(sx[:], sx[:], ACT.Sigmoid).then_inc(sx_done, 1)
            act.wait_ge(made, 1)
            for p in range(NPAIR):
                s = p % 2
                act.wait_ge(centred, p + 1)
                nc.scalar.activation(sq[:, s, :], o[:, s, :], ACT.Square).then_inc(squared, 1)
                act.wait_ge(vard, p + 1)
                nc.scalar.activation(rs[:, s, :], ps[1][:, 0:T], ACT.Ln, bias=eps[:]).then_inc(ch, 1)
                act.wait_ge(ch, p + 1)
                nc.scalar.activation(rs[:, s, :], rs[:, s, :], ACT.Exp, scale=-0.5).then_inc(rsd, 1)

        @block.vector
        def _(dve):
            nc.vector.memset(eps[:], GN_EPS)
            for w, v in ((mean_w, 1.0 / DH), (sum_w, 1.0)):
                nc.vector.memset(w[0:DH, DH:P], 0.0)
                nc.vector.memset(w[DH:P, 0:DH], 0.0)
                nc.vector.memset(w[0:DH, 0:DH], v)
                last = nc.vector.memset(w[DH:P, DH:P], v)
            last.then_inc(made, 1)
            dve.wait_ge(once, 48)
            link = Chain(dve, nc.alloc_semaphore("ro_dch")).link
            for p in range(NPAIR):
                s = p % 2
                dve.wait_ge(loads[s], 64 * (p // 2 + 1))
                nc.vector.scalar_tensor_tensor(bo[:, s, :], rt[:, s, :], par[:, 16 + p:17 + p], kt[:, s, :], ALU.mult, ALU.mult).then_inc(rk_done, 1)
                dve.wait_ge(meaned, p + 1)
                nc.vector.tensor_tensor(o[:, s, :], o[:, s, :], ps[0][:, 0:T], ALU.subtract).then_inc(centred, 1)
                dve.wait_ge(bonused, p + 1)
                link(nc.vector.tensor_tensor(vt[:, s, :], ps[2][:, 0:T], vt[:, s, :], ALU.mult))
                dve.wait_ge(rsd, p + 1)
                link(nc.vector.tensor_tensor(o[:, s, :], o[:, s, :], rs[:, s, :], ALU.mult))
                link(nc.vector.tensor_scalar(o[:, s, :], o[:, s, :], par[:, 24 + p:25 + p], par[:, 32 + p:33 + p], ALU.mult, ALU.add))
                link(nc.vector.tensor_tensor(o[:, s, :], o[:, s, :], vt[:, s, :], ALU.add))
                nc.vector.tensor_tensor(o[:, s, :], o[:, s, :], ps[3][:, 0:T], ALU.mult).then_inc(done, 1)


def block_output_projection(nc, o_d, w_out, mixed_d):
    WB = 512
    with ExitStack() as ctx:
        def sb(name, shape):
            return ctx.enter_context(nc.sbuf_tensor("op_" + name, shape, F32))

        def sem(name):
            return nc.alloc_semaphore("op_" + name)

        ot, ring, stage = sb("ot", [P, KD, T]), sb("ring", [P, 2, KD, WB]), sb("stage", [P, 2, NT, WB])
        ps = ctx.enter_context(nc.psum_tensor("op_ps", [P, 8, 512], F32))
        o_in, mm_done, evd, used = sem("oin"), sem("mm"), sem("ev"), sem("used")
        w_got, out = (sem("w0"), sem("w1")), (sem("out0"), sem("out1"))
        block = ctx.enter_context(nc.Block())

        @block.sync
        def _(sp):
            for b in range(D // WB):
                if b >= 2:
                    sp.wait_ge(mm_done, NT * (b - 1))
                sp.dma_start(ring[:, b % 2], w_out[0, :, b * WB:(b + 1) * WB].rearrange("(k p) n -> p k n", p=P)).then_inc(w_got[b % 2], 16)
                if b == 0:
                    sp.dma_start(ot[:], o_d.rearrange("k p t -> p k t")).then_inc(o_in, 16)
            for b in range(D // WB):
                sp.wait_ge(evd, NT * (b + 1))
                sp.dma_start(mixed_d[:, :, b * WB:(b + 1) * WB].rearrange("t p n -> p t n"), stage[:, b % 2]).then_inc(out[b % 2], 16)
            sp.wait_ge(out[0], 32)
            sp.wait_ge(out[1], 32)

        @block.tensor
        def _(pe):
            pe.wait_ge(o_in, 16)
            for b in range(D // WB):
                pe.wait_ge(w_got[b % 2], 16 * (b // 2 + 1))
                for t in range(NT):
                    n = b * NT + t
                    if n >= 8:
                        pe.wait_ge(evd, n - 7)
                    for k in range(KD):
                        mm = pe.matmul(ps[:, n % 8, :], ot[:, k, t * P:(t + 1) * P], ring[:, b % 2, k, :], start=(k == 0), stop=(k == KD - 1))
                    mm.then_inc(mm_done, 1)

        @block.scalar
        def _(act):
            for b in range(D // WB):
                for t in range(NT):
                    n = b * NT + t
                    act.wait_ge(mm_done, n + 1)
                    if b >= 2 and t == 0:
                        act.wait_ge(out[b % 2], 16)
                    nc.scalar.copy(stage[:, b % 2, t, :], ps[:, n % 8, :]).then_inc(evd, 1)


def block_middle(nc, x_prompt, x_sample, mixed_d, mod_d, g_post_mix, g_pre_ffn, w_router, ident_d, x1_d, h2_d, aff_d, afft_d):
    with ExitStack() as ctx:
        def sb(name, shape):
            return ctx.enter_context(nc.sbuf_tensor("mi_" + name, shape, F32))

        def sem(name):
            return nc.alloc_semaphore("mi_" + name)

        ident, wr, eps = sb("ident", [P, P]), sb("wr", [P, KD, NE]), sb("eps", [P, 1])
        g1, a2, sh2 = (sb(n, [P, 2, D]) for n in ("g1", "a2", "sh2"))
        gp, gf = sb("gp", [P, D]), sb("gf", [P, D])
        x, mx = sb("x", [P, 2, D]), sb("mx", [P, 2, D])
        junk, h2t = sb("junk", [P, D]), sb("h2t", [P, KD, P])
        st = sb("st", [P, NT, 6])
        af, afs = sb("af", [P, NT, NE]), sb("afs", [P, NT, 4])
        aft = sb("aft", [NE, T])
        ps = ctx.enter_context(nc.psum_tensor("mi_ps", [P, 8, 512], F32))
        once, made, rows_ready = sem("once"), sem("made"), sem("rows")
        loads = (sem("load0"), sem("load1"))
        ss1, sd1, x1r, ss2, sd2, h2r, turned, h2te, routed, mxd, expd, affd, atd, ate = (sem(n) for n in
            ("ss1", "sd1", "x1", "ss2", "sd2", "h2", "turned", "h2te", "routed", "mxd", "expd", "affd", "atd", "ate"))
        x1_out, h2_out, out = sem("x1out"), sem("h2out"), sem("out")
        block = ctx.enter_context(nc.Block())

        def store(sp, t):
            sp.wait_ge(x1r, t + 1)
            sp.dma_start(x1_d[t], x[:, t % 2, :]).then_inc(x1_out, 16)
            sp.wait_ge(h2r, t + 1)
            sp.dma_start(h2_d[t], mx[:, t % 2, :]).then_inc(h2_out, 16)

        @block.sync
        def _(sp):
            sp.dma_start(ident[:], ident_d).then_inc(once, 16)
            sp.dma_start(wr[:], w_router[0].rearrange("(k p) e -> p k e", p=P)).then_inc(once, 16)
            sp.dma_start(gp[:], bcast_rows(g_post_mix, 0, D)).then_inc(once, 16)
            sp.dma_start(gf[:], bcast_rows(g_pre_ffn, 0, D)).then_inc(once, 16)
            for cnd in range(2):
                for dst, part in ((g1, 2), (a2, 4), (sh2, 3)):
                    sp.dma_start(dst[:, cnd, :], bcast_rows(mod_d, cnd * 6 * D + part * D, D)).then_inc(once, 16)
            for t in range(NT):
                s = t % 2
                if t >= 2:
                    sp.wait_ge(x1_out, 16 * (t - 1))
                    sp.wait_ge(h2_out, 16 * (t - 1))
                    sp.wait_ge(turned, 4 * (t - 1))
                sp.dma_start(x[:, s, :], x_prompt[0] if t == 0 else x_sample[0, (t - 1) * P:t * P, :]).then_inc(loads[s], 16)
                sp.dma_start(mx[:, s, :], mixed_d[t]).then_inc(loads[s], 16)
                if t >= 1:
                    store(sp, t - 1)
            store(sp, NT - 1)
            sp.wait_ge(affd, NT)
            sp.dma_start(aff_d, af[:]).then_inc(out, 16)
            sp.wait_ge(ate, 2)
            sp.dma_start(afft_d, aft[:]).then_inc(out, 16)
            sp.wait_ge(x1_out, 16 * NT)
            sp.wait_ge(h2_out, 16 * NT)
            sp.wait_ge(out, 32)

        @block.tensor
        def _(pe):
            pe.wait_ge(once, 160)
            for t in range(NT):
                pe.wait_ge(h2r, t + 1)
                for q in range(4):
                    if t:
                        pe.wait_ge(h2te, 4 * (t - 1) + q + 1)
                    for j in range(4):
                        k = 4 * q + j
                        tr = pe.transpose(ps[:, q, j * P:(j + 1) * P], mx[:, t % 2, k * P:(k + 1) * P], ident[:])
                    tr.then_inc(turned, 1)
                pe.wait_ge(h2te, 4 * t + 4)
                if t >= 2:
                    pe.wait_ge(expd, t - 1)
                for k in range(KD):
                    mm = pe.matmul(ps[:, 4 + t % 2, 0:NE], h2t[:, k, :], wr[:, k, :], start=(k == 0), stop=(k == KD - 1))
                mm.then_inc(routed, 1)
            for t in range(NT):
                pe.wait_ge(affd, t + 1)
                dst = ps[0:NE, 6, (t - 1) * P:t * P] if t else ps[0:NE, 7, 0:P]
                pe.transpose(dst, af[:, t, :], ident[:]).then_inc(atd, 1)

        @block.scalar
        def _(act):
            act.wait_ge(made, 1)
            for t in range(NT):
                s = t % 2
                act.wait_ge(loads[s], 32 * (t // 2 + 1))
                nc.scalar.activation(junk[:], mx[:, s, :], ACT.Square, accum_out=st[:, t, 0:1]).then_inc(ss1, 1)
                act.wait_ge(ss1, 2 * t + 1)
                nc.scalar.activation(st[:, t, 1:2], st[:, t, 0:1], ACT.Sqrt, scale=1.0 / D, bias=eps[:]).then_inc(ss1, 1)
                act.wait_ge(x1r, t + 1)
                nc.scalar.activation(junk[:], x[:, s, :], ACT.Square, accum_out=st[:, t, 3:4]).then_inc(ss2, 1)
                act.wait_ge(ss2, 2 * t + 1)
                nc.scalar.activation(st[:, t, 4:5], st[:, t, 3:4], ACT.Sqrt, scale=1.0 / D, bias=eps[:]).then_inc(ss2, 1)
                for q in range(4):
                    act.wait_ge(turned, 4 * t + q + 1)
                    if t:
                        act.wait_ge(routed, t)
                    nc.scalar.copy(h2t[:, 4 * q:4 * q + 4, :].rearrange("p k t -> p (k t)"), ps[:, q, :]).then_inc(h2te, 1)
                act.wait_ge(mxd, t + 1)
                nc.scalar.activation(af[:, t, :], ps[:, 4 + t % 2, 0:NE], ACT.Exp, bias=afs[:, t, 1:2], accum_out=afs[:, t, 2:3]).then_inc(expd, 1)

        @block.vector
        def _(dve):
            link = Chain(dve, nc.alloc_semaphore("mi_dch")).link
            nc.vector.memset(eps[:], NORM_EPS).then_inc(made, 1)
            dve.wait_ge(once, 160)
            for cnd in range(2):
                nc.vector.tensor_tensor(g1[:, cnd, :], g1[:, cnd, :], gp[:], ALU.mult)
                last = nc.vector.scalar_tensor_tensor(a2[:, cnd, :], a2[:, cnd, :], 1.0, gf[:], ALU.add, ALU.mult)
            link(last)

            def router(t):
                dve.wait_ge(routed, t + 1)
                link(nc.vector.tensor_reduce(afs[:, t, 0:1], ps[:, 4 + t % 2, 0:NE], AX_X, ALU.max))
                nc.vector.tensor_scalar(afs[:, t, 1:2], afs[:, t, 0:1], -1.0, None, ALU.mult).then_inc(mxd, 1)
                dve.wait_ge(expd, t + 1)
                link(nc.vector.reciprocal(afs[:, t, 3:4], afs[:, t, 2:3]))
                nc.vector.tensor_scalar(af[:, t, :], af[:, t, :], afs[:, t, 3:4], None, ALU.mult).then_inc(affd, 1)

            for t in range(NT):
                s, cnd = t % 2, min(t, 1)
                dve.wait_ge(ss1, 2 * t + 2)
                link(nc.vector.reciprocal(st[:, t, 2:3], st[:, t, 1:2]))
                link(nc.vector.scalar_tensor_tensor(mx[:, s, :], mx[:, s, :], st[:, t, 2:3], g1[:, cnd, :], ALU.mult, ALU.mult))
                nc.vector.tensor_tensor(x[:, s, :], x[:, s, :], mx[:, s, :], ALU.add).then_inc(x1r, 1)
                dve.wait_ge(ss2, 2 * t + 2)
                link(nc.vector.reciprocal(st[:, t, 5:6], st[:, t, 4:5]))
                link(nc.vector.scalar_tensor_tensor(mx[:, s, :], x[:, s, :], st[:, t, 5:6], a2[:, cnd, :], ALU.mult, ALU.mult))
                nc.vector.tensor_tensor(mx[:, s, :], mx[:, s, :], sh2[:, cnd, :], ALU.add).then_inc(h2r, 1)
                router(t)
            dve.wait_ge(atd, 1)
            nc.vector.tensor_copy(aft[:, 0:TP], ps[0:NE, 7, 0:P]).then_inc(ate, 1)
            dve.wait_ge(atd, NT)
            nc.vector.tensor_copy(aft[:, TP:T], ps[0:NE, 6, :]).then_inc(ate, 1)


def block_select(nc, afft_d, ident_d, slot_d):
    with ExitStack() as ctx:
        def sb(name, shape):
            return ctx.enter_context(nc.sbuf_tensor("se_" + name, shape, F32))

        ident, wk, sel, cum = sb("ident", [P, P]), sb("wk", [NE, T]), sb("sel", [NE, T]), sb("cum", [NE, T])
        zero, top = sb("zero", [NE, T]), sb("top", [NE, 8])
        slot = sb("slot", [P, NT, NE])
        ps = ctx.enter_context(nc.psum_tensor("se_ps", [P, 512], F32))
        once, cumd, turned, done, out = (nc.alloc_semaphore("se_" + n) for n in ("once", "cumd", "turned", "done", "out"))
        block = ctx.enter_context(nc.Block())

        @block.sync
        def _(sp):
            sp.dma_start(ident[:], ident_d).then_inc(once, 16)
            sp.dma_start(wk[:], afft_d).then_inc(once, 16)
            sp.wait_ge(done, 1)
            sp.dma_start(slot_d, slot[:]).then_inc(out, 16)
            sp.wait_ge(out, 16)

        @block.vector
        def _(dve):
            link = Chain(dve, nc.alloc_semaphore("se_ch")).link
            link(nc.vector.memset(zero[:], 1.0))
            dve.wait_ge(once, 32)
            for t0, t1, cap in ((0, TP, CAPP), (TP, T, CAPS)):
                for _ in range(cap // 8):
                    link(nc.vector.max(top[:], wk[:, t0:t1]))
                    link(nc.vector.match_replace(wk[:, t0:t1], top[:], wk[:, t0:t1], -1.0))
                link(nc.vector.tensor_scalar(sel[:, t0:t1], wk[:, t0:t1], 0.0, None, ALU.is_lt))
                link(nc.vector.tensor_tensor_scan(cum[:, t0:t1], zero[:, t0:t1], sel[:, t0:t1], 0.0, ALU.mult, ALU.add))
            nc.vector.tensor_tensor(cum[:], cum[:], sel[:], ALU.mult).then_inc(cumd, 1)
            dve.wait_ge(turned, 1)
            nc.vector.tensor_copy(slot[:].rearrange("p t e -> p (t e)"), ps[:, 0:NT * NE]).then_inc(done, 1)

        @block.tensor
        def _(pe):
            pe.wait_ge(once, 32)
            pe.wait_ge(cumd, 1)
            for t in range(NT):
                tr = pe.transpose(ps[:, t * NE:(t + 1) * NE], cum[:, t * P:(t + 1) * P], ident[0:NE, 0:NE])
            tr.then_inc(turned, 1)


def block_experts(nc, h2_d, aff_d, slot_d, ident_d, w_gate, w_up, w_down, ffn_d):
    NG, EG = NE // 4, 4
    RING = 6
    PER = 24
    NL = EG * PER
    with ExitStack() as ctx:
        def sb(name, shape):
            return ctx.enter_context(nc.sbuf_tensor("ex_" + name, shape, F32))

        def sem(name):
            return nc.alloc_semaphore("ex_" + name)

        ident = sb("ident", [P, P])
        h2 = sb("h2", [P, NT, D])
        aff, slot, iota = sb("aff", [P, NT, NE]), sb("slot", [P, NT, NE]), sb("iota", [P, 64])
        xsp = sb("xsp", [P, KD, NE * CAPP])
        ring = sb("ring", [P, RING, 2048])
        xe0, xe1 = sb("xe0", [P, KD, 80]), sb("xe1", [P, KD, P])
        oh = sb("oh", [P, 4, 2, CAPS])
        cg, cgp = sb("cg", [P, 4, EG, CAPS]), sb("cgp", [P, EG, 32])
        cc, ccp = sb("cc", [P, 2, 4, P]), sb("ccp", [P, P])
        hid = sb("hid", [P, DE])
        hidt = sb("hidt", [P, 8, P])
        y, yp = sb("y", [P, 2, D]), sb("yp", [P, D])
        f = sb("f", [P, NT, D])
        ps = ctx.enter_context(nc.psum_tensor("ex_ps", [P, 8, 512], F32))

        once, made, ohp_ready, pg, pg_ev = sem("once"), sem("made"), sem("ohp"), sem("pg"), sem("pgev")
        slot_in = [sem(f"in{i}") for i in range(RING)]
        slot_used = sem("used")
        oh_ready, gathered, xe_act, xe_dve, xe_pool = (sem(n) for n in ("oh", "gath", "xea", "xev", "xep"))
        silu_done, hid_done, turned, ht_act, ht_dve, y_act, y_dve = (sem(n) for n in
            ("silu", "hid", "turned", "hta", "htv", "ya", "yv"))
        cg_ready, cc_turned, cc_ready, comb, added, out = (sem(n) for n in ("cg", "cct", "cc", "comb", "added", "out"))
        block = ctx.enter_context(nc.Block())
        rows = [80, P]

        @block.sync
        def _(sp):
            sp.dma_start(ident[:], ident_d).then_inc(once, 16)
            sp.dma_start(aff[:], aff_d).then_inc(once, 16)
            sp.dma_start(slot[:], slot_d).then_inc(once, 16)
            sp.dma_start(h2[:], h2_d.rearrange("t p d -> p t d")).then_inc(once, 16)
            with sp.Fori(0, NG) as g:
                for n in range(NL):
                    j, r = n // PER, n % PER
                    sp.wait_ge(slot_used, g * NL + n + 1)
                    e = bass.ds(4 * g + j, 1)
                    if r < 16:
                        w = w_gate if r % 2 == 0 else w_up
                        src = w[0, e, (r // 2) * 256:(r // 2 + 1) * 256, :].rearrange("o (k p) f -> p (o k) f", p=P)
                        dst = ring[:, n % RING, :].rearrange("p (k f) -> p k f", k=2)
                    else:
                        src = w_down[0, e, (r - 16) * P:(r - 15) * P, :].rearrange("o p f -> p (o f)")
                        dst = ring[:, n % RING, :]
                    sp.dma_start(dst, src).then_inc(slot_in[n % RING], 16)
            sp.wait_ge(added, 36 * NG)
            sp.dma_start(ffn_d.rearrange("t p d -> p t d"), f[:]).then_inc(out, 16)
            sp.wait_ge(out, 16)

        @block.gpsimd
        def _(pool):
            pool.sem_inc(slot_used, RING)
            nc.gpsimd.memset(xe1[:], 0.0)
            nc.gpsimd.memset(yp[:], 0.0)
            nc.gpsimd.memset(f[:], 0.0)
            nc.gpsimd.iota(iota[:], pattern=[[1, 64]], base=1, channel_multiplier=0, allow_small_or_imprecise_dtypes=True).then_inc(made, 1)
            pool.wait_ge(made, 1)
            pool.wait_ge(pg_ev, 16)
            with pool.Fori(0, NG) as g:
                for q in range(2):
                    pool.wait_ge(gathered, g * 8 + 4 * q + 4)
                    nc.gpsimd.tensor_copy(xe0[:, :, 64:80], xsp[:, :, bass.ds(g * 64 + 32 * q, CAPP)])
                    nc.gpsimd.tensor_copy(xe1[:, :, 0:16], xsp[:, :, bass.ds(g * 64 + 32 * q + 16, CAPP)]).then_inc(xe_pool, 1)

        @block.tensor
        def _(pe):
            pe.wait_ge(once, 64)
            pe.wait_ge(ohp_ready, 1)
            for k in range(KD):
                if k >= 8:
                    pe.wait_ge(pg_ev, k - 7)
                pe.matmul(ps[:, k % 8, 0:256], h2[:, 0, k * P:(k + 1) * P], cg[:, 0].rearrange("p e c -> p (e c)"), start=True, stop=True).then_inc(pg, 1)
            pe.wait_ge(pg_ev, 16)
            with pe.Fori(0, NG) as g:
                def slot_ready(n):
                    pe.wait_ge(slot_in[n % RING], g * (16 * NL // RING) + 16 * (n // RING + 1))

                def gather(q):
                    pe.wait_ge(oh_ready, 2 * g + q + 1)
                    for b in range(4):
                        for i in range(4):
                            k = 4 * b + i
                            for t in range(4):
                                mm = pe.matmul(ps[:, 4 + b, i * P:(i + 1) * P], h2[:, 1 + t, k * P:(k + 1) * P],
                                               oh[:, t].rearrange("p e c -> p (e c)"), start=(t == 0), stop=(t == 3))
                        mm.then_inc(gathered, 1)

                def gate_up(j):
                    m = rows[j % 2]
                    xe = (xe0, xe1)[j % 2]
                    if j % 2 == 0:
                        pe.wait_ge(xe_act, 4 * g + j + 2)
                        pe.wait_ge(xe_dve, 4 * g + j + 2)
                        pe.wait_ge(xe_pool, 2 * g + j // 2 + 1)
                    for r in range(16):
                        n = j * PER + r
                        slot_ready(n)
                        for kk in range(2):
                            k = 2 * (r // 2) + kk
                            for h in range(2):
                                mm = pe.matmul(ps[0:m, 2 * (r % 2) + h, :], xe[:, k, 0:m],
                                               ring[:, n % RING, kk * DE + h * 512:kk * DE + (h + 1) * 512],
                                               start=(k == 0), stop=(k == KD - 1))
                        mm.then_inc(slot_used, 1)

                def turn_hidden(j):
                    m = rows[j % 2]
                    for h in range(2):
                        pe.wait_ge(hid_done, 8 * g + 2 * j + h + 1)
                        for i in range(4):
                            tr = pe.transpose(ps[:, h, i * P:i * P + m], hid[0:m, (4 * h + i) * P:(4 * h + i + 1) * P], ident[0:m, 0:m])
                        tr.then_inc(turned, 1)

                def down(j):
                    m = rows[j % 2]
                    for k in range(8):
                        n = j * PER + 16 + k
                        slot_ready(n)
                        if k == 0:
                            pe.wait_ge(ht_act, 4 * g + j + 1)
                        if k == 4:
                            pe.wait_ge(ht_dve, 4 * g + j + 1)
                        for h in range(4):
                            mm = pe.matmul(ps[0:m, 4 + h, :], hidt[:, k, 0:m], ring[:, n % RING, h * 512:(h + 1) * 512],
                                           start=(k == 0), stop=(k == 7))
                        mm.then_inc(slot_used, 1)

                def combine(q):
                    outs = [(1 + t, h) for t in range(4) for h in range(4)] + ([(0, h) for h in range(4)] if q else [])
                    pe.wait_ge(y_act, 4 * g + 2 * q + 2)
                    pe.wait_ge(y_dve, 4 * g + 2 * q + 2)
                    for o, (t, h) in enumerate(outs):
                        if o >= 4:
                            pe.wait_ge(added, 36 * g + 16 * q + o - 3)
                        lhs, rhs = (cc[:, q, t - 1, :], y[:, q, h * 512:(h + 1) * 512]) if t else (ccp[:], yp[:, h * 512:(h + 1) * 512])
                        pe.matmul(ps[:, 4 + o % 4, :], lhs, rhs, start=True, stop=True).then_inc(comb, 1)
                    pe.wait_ge(added, 36 * g + 16 + 20 * q)

                gather(0)
                gate_up(0)
                pe.wait_ge(cg_ready, 2 * g + 2)
                for q in range(2):
                    for t in range(4):
                        pe.transpose(ps[:, 4 + q, t * P:(t + 1) * P], cg[:, t, 2 * q:2 * q + 2].rearrange("p e c -> p (e c)"), ident[:])
                pe.transpose(ps[:, 6, 0:P], cgp[:].rearrange("p e c -> p (e c)"), ident[:]).then_inc(cc_turned, 1)
                turn_hidden(0)
                pe.wait_ge(cc_ready, g + 1)
                down(0)
                gate_up(1)
                pe.wait_ge(y_act, 4 * g + 1)
                pe.wait_ge(y_dve, 4 * g + 1)
                gather(1)
                turn_hidden(1)
                pe.wait_ge(xe_act, 4 * g + 4)
                pe.wait_ge(xe_dve, 4 * g + 4)
                down(1)
                gate_up(2)
                combine(0)
                turn_hidden(2)
                down(2)
                gate_up(3)
                turn_hidden(3)
                pe.wait_ge(y_act, 4 * g + 3)
                pe.wait_ge(y_dve, 4 * g + 3)
                down(3)
                combine(1)

        def rows_of(j):
            if j % 2 == 0:
                return slice(0, 64), slice(64, 80), slice(32 * j, 32 * j + CAPP)
            return slice(64, P), slice(0, 16), slice(32 * j, 32 * j + CAPP)

        def store_rows(copy, j, banks):
            s, pr, dst = rows_of(j)
            for h in banks:
                copy(y[s, j // 2, h * 512:(h + 1) * 512], ps[s, 4 + h, :])
                last = copy(yp[dst, h * 512:(h + 1) * 512], ps[pr, 4 + h, :])
            return last

        @block.scalar
        def _(act):
            act.wait_ge(made, 1)
            for k in range(0, KD, 2):
                act.wait_ge(pg, k + 1)
                if k:
                    act.wait_ge(pg_ev, k)
                nc.scalar.copy(xsp[:, k, :], ps[:, k % 8, 0:256]).then_inc(pg_ev, 1)
            with act.Fori(0, NG) as g:
                def take_gathered(q):
                    for b in (0, 2):
                        act.wait_ge(gathered, 8 * g + 4 * q + b + 1)
                        src = ps[:, 4 + b, :].rearrange("p (k c) -> p k c", c=P)
                        nc.scalar.copy(xe0[:, 4 * b:4 * b + 4, 0:64], src[:, :, 0:64])
                        nc.scalar.copy(xe1[:, 4 * b:4 * b + 4, 64:P], src[:, :, 64:P]).then_inc(xe_act, 1)

                def expert(j):
                    m = rows[j % 2]
                    act.wait_ge(slot_used, g * NL + j * PER + 16 + RING)
                    for h in range(2):
                        nc.scalar.activation(hid[0:m, h * 512:(h + 1) * 512], ps[0:m, h, :], ACT.Silu).then_inc(silu_done, 1)
                    if j == 0:
                        act.wait_ge(cc_turned, g + 1)
                        for q in range(2):
                            nc.scalar.copy(cc[:, q].rearrange("p t c -> p (t c)"), ps[:, 4 + q, :])
                        nc.scalar.copy(ccp[:], ps[:, 6, 0:P]).then_inc(cc_ready, 1)
                    if j == 1:
                        take_gathered(1)
                    act.wait_ge(turned, 8 * g + 2 * j + 1)
                    nc.scalar.copy(hidt[:, 0:4, 0:m], ps[:, 0, :].rearrange("p (i c) -> p i c", c=P)[:, :, 0:m]).then_inc(ht_act, 1)
                    act.wait_ge(slot_used, g * NL + (j + 1) * PER + RING)
                    store_rows(nc.scalar.copy, j, (0, 1)).then_inc(y_act, 1)

                take_gathered(0)
                for j in range(EG):
                    expert(j)

        @block.vector
        def _(dve):
            link = Chain(dve, nc.alloc_semaphore("ex_dch")).link
            dve.wait_ge(made, 1)
            dve.wait_ge(once, 64)

            def one_hot(dst, tiles, experts, n):
                nt, ne = dst.shape[1], dst.shape[2]
                for t in range(nt):
                    last = nc.vector.tensor_tensor(dst[:, t], iota[:, 0:n].unsqueeze(1).to_broadcast([P, ne, n]),
                                                   slot[:, tiles + t, experts].unsqueeze(2).to_broadcast([P, ne, n]), ALU.is_equal)
                return last

            one_hot(cg[:, 0].rearrange("p e c -> p (e c)").rearrange("p (o e c) -> p o e c", o=1, c=CAPP), 0, slice(0, NE), CAPP).then_inc(ohp_ready, 1)
            for k in range(1, KD, 2):
                dve.wait_ge(pg, k + 1)
                dve.wait_ge(pg_ev, k)
                nc.vector.tensor_copy(xsp[:, k, :], ps[:, k % 8, 0:256]).then_inc(pg_ev, 1)
            with dve.Fori(0, NG) as g:
                def pair(q):
                    one_hot(oh[:], 1, bass.ds(4 * g + 2 * q, 2), CAPS).then_inc(oh_ready, 1)

                def take_gathered(q):
                    for b in (1, 3):
                        dve.wait_ge(gathered, 8 * g + 4 * q + b + 1)
                        src = ps[:, 4 + b, :].rearrange("p (k c) -> p k c", c=P)
                        nc.vector.tensor_copy(xe0[:, 4 * b:4 * b + 4, 0:64], src[:, :, 0:64])
                        nc.vector.tensor_copy(xe1[:, 4 * b:4 * b + 4, 64:P], src[:, :, 64:P]).then_inc(xe_dve, 1)

                def scatter_matrices():
                    for t in range(4):
                        nc.vector.tensor_tensor(cg[:, t], iota[:].unsqueeze(1).to_broadcast([P, EG, CAPS]),
                                                slot[:, 1 + t, bass.ds(4 * g, EG)].unsqueeze(2).to_broadcast([P, EG, CAPS]), ALU.is_equal)
                    nc.vector.tensor_tensor(cgp[:], iota[:, 0:32].unsqueeze(1).to_broadcast([P, EG, 32]),
                                            slot[:, 0, bass.ds(4 * g, EG)].unsqueeze(2).to_broadcast([P, EG, 32]), ALU.is_equal).then_inc(cg_ready, 1)
                    dve.wait_ge(cg_ready, 2 * g + 1)
                    for t in range(4):
                        nc.vector.tensor_tensor(cg[:, t], cg[:, t], aff[:, 1 + t, bass.ds(4 * g, EG)].unsqueeze(2).to_broadcast([P, EG, CAPS]), ALU.mult)
                    nc.vector.tensor_tensor(cgp[:], cgp[:], aff[:, 0, bass.ds(4 * g, EG)].unsqueeze(2).to_broadcast([P, EG, 32]), ALU.mult).then_inc(cg_ready, 1)

                def hidden(j):
                    m = rows[j % 2]
                    for h in range(2):
                        dve.wait_ge(silu_done, 8 * g + 2 * j + h + 1)
                        cols = slice(h * 512, (h + 1) * 512)
                        nc.vector.tensor_tensor(hid[0:m, cols], ps[0:m, 2 + h, :], hid[0:m, cols], ALU.mult).then_inc(hid_done, 1)

                def outputs(j):
                    m = rows[j % 2]
                    dve.wait_ge(turned, 8 * g + 2 * j + 2)
                    nc.vector.tensor_copy(hidt[:, 4:8, 0:m], ps[:, 1, :].rearrange("p (i c) -> p i c", c=P)[:, :, 0:m]).then_inc(ht_dve, 1)
                    dve.wait_ge(slot_used, g * NL + (j + 1) * PER + RING)
                    store_rows(nc.vector.tensor_copy, j, (2, 3)).then_inc(y_dve, 1)

                def add(q):
                    outs = [(1 + t, h) for t in range(4) for h in range(4)] + ([(0, h) for h in range(4)] if q else [])
                    for o, (t, h) in enumerate(outs):
                        dve.wait_ge(comb, 36 * g + 16 * q + o + 1)
                        cols = slice(h * 512, (h + 1) * 512)
                        nc.vector.tensor_tensor(f[:, t, cols], ps[:, 4 + o % 4, :], f[:, t, cols], ALU.add).then_inc(added, 1)

                pair(0)
                take_gathered(0)
                scatter_matrices()
                hidden(0)
                outputs(0)
                pair(1)
                hidden(1)
                take_gathered(1)
                outputs(1)
                hidden(2)
                add(0)
                outputs(2)
                hidden(3)
                outputs(3)
                add(1)


def block_final(nc, x1_d, ffn_d, mod_d, g_post_ffn, y_prompt, y_sample):
    with ExitStack() as ctx:
        def sb(name, shape):
            return ctx.enter_context(nc.sbuf_tensor("fi_" + name, shape, F32))

        def sem(name):
            return nc.alloc_semaphore("fi_" + name)

        g2, gp = sb("g2", [P, 2, D]), sb("gp", [P, D])
        x, f, junk, st, eps = sb("x", [P, NT, D]), sb("f", [P, NT, D]), sb("junk", [P, D]), sb("st", [P, NT, 3]), sb("eps", [P, 1])
        once, made, ss, done, out = (sem(n) for n in ("once", "made", "ss", "done", "out"))
        loads = [sem(f"load{t}") for t in range(NT)]
        block = ctx.enter_context(nc.Block())

        @block.sync
        def _(sp):
            for t in range(NT):
                sp.dma_start(f[:, t, :], ffn_d[t]).then_inc(loads[t], 16)
                sp.dma_start(x[:, t, :], x1_d[t]).then_inc(loads[t], 16)
            for t in range(NT):
                sp.wait_ge(done, t + 1)
                sp.dma_start(y_prompt[0] if t == 0 else y_sample[0, (t - 1) * P:t * P, :], x[:, t, :]).then_inc(out, 16)
            sp.wait_ge(out, 16 * NT)

        @block.gpsimd
        def _(pool):
            pool.dma_start(gp[:], bcast_rows(g_post_ffn, 0, D)).then_inc(once, 16)
            for cnd in range(2):
                pool.dma_start(g2[:, cnd, :], bcast_rows(mod_d, cnd * 6 * D + 5 * D, D)).then_inc(once, 16)

        @block.scalar
        def _(act):
            act.wait_ge(made, 1)
            for t in range(NT):
                act.wait_ge(loads[t], 32)
                nc.scalar.activation(junk[:], f[:, t, :], ACT.Square, accum_out=st[:, t, 0:1]).then_inc(ss, 1)
                act.wait_ge(ss, 2 * t + 1)
                nc.scalar.activation(st[:, t, 1:2], st[:, t, 0:1], ACT.Sqrt, scale=1.0 / D, bias=eps[:]).then_inc(ss, 1)

        @block.vector
        def _(dve):
            link = Chain(dve, nc.alloc_semaphore("fi_ch")).link
            nc.vector.memset(eps[:], NORM_EPS).then_inc(made, 1)
            dve.wait_ge(once, 48)
            for cnd in range(2):
                last = nc.vector.tensor_tensor(g2[:, cnd, :], g2[:, cnd, :], gp[:], ALU.mult)
            link(last)
            for t in range(NT):
                dve.wait_ge(ss, 2 * t + 2)
                link(nc.vector.reciprocal(st[:, t, 2:3], st[:, t, 1:2]))
                link(nc.vector.scalar_tensor_tensor(f[:, t, :], f[:, t, :], st[:, t, 2:3], g2[:, min(t, 1), :], ALU.mult, ALU.mult))
                nc.vector.tensor_tensor(x[:, t, :], x[:, t, :], f[:, t, :], ALU.add).then_inc(done, 1)


def trunk(nc, a, s):
    with nc.cleanup_on_exit():
        trunk_mixers(nc, a, s)
    trunk_experts(nc, a, s)


def trunk_mixers(nc, a, s):
    block_modulation(nc, a["c"], a["c_ctx"], a["w_ada"], a["b_ada"], s["mod"], s["ident"])
    block_projection(nc, a["x_prompt"], a["x_sample"], a["g_pre_mix"], a["w_in"], s["mod"], s["ident"], s["z"], s["v"], s["vs"])

    def channel_rows(ap):
        if ap.shape[-1] == DH:
            return ap.rearrange("a (k two) d -> (a k) (two d)", two=2)
        return ap.rearrange("a (k p) -> (a k) p" if len(ap.shape) == 2 else "a b (k p) -> (a b k) p", p=P)

    vectors = [(channel_rows(a[n]), NPAIR * (2 if n in ("rw_w0", "rw_a0") else 1))
               for n in ("rw_kk", "rw_ka", "rw_rk", "rw_ln_w", "rw_ln_b", "rw_w0", "rw_a0")]
    block_gating_and_keys(nc, s["z"], s["vs"], a["sg_gain"], a["sg_w"], a["sg_b"], vectors, s["ident"], s["par"], s["kk"], s["o"])
    flat = "a b c h d -> (a b c) (h d)"
    block_attention(nc, s["z"], s["v"], a["cache_k"].rearrange(flat), a["cache_v"].rearrange(flat), a["na_rpb"], s["ident"],
                    s["bias"], s["o"], a["new_cache_k"].rearrange(flat), a["new_cache_v"].rearrange(flat))
    states = "a b d h v k -> (a b d) h v k"
    block_rwkv(nc, s["z"], s["kk"], s["par"], a["rw_w2"], a["rw_a2"], a["state_wkv"].rearrange(states), s["ident"],
               s["o_raw"], a["new_state_wkv"].rearrange(states))


def trunk_experts(nc, a, s):
    block_rwkv_output(nc, s["z"], s["o_raw"], s["par"], a["rw_g2"], s["ident"], s["o"])
    block_output_projection(nc, s["o"], a["w_out"], s["mixed"])
    block_middle(nc, a["x_prompt"], a["x_sample"], s["mixed"], s["mod"], a["g_post_mix"], a["g_pre_ffn"], a["w_router"],
                 s["ident"], s["x1"], s["h2"], s["aff"], s["afft"])
    block_select(nc, s["afft"], s["ident"], s["slot"])
    block_experts(nc, s["h2"], s["aff"], s["slot"], s["ident"], a["w_gate"], a["w_up"], a["w_down"], s["ffn"])
    block_final(nc, s["x1"], s["ffn"], s["mod"], a["g_post_ffn"], a["y_prompt"], a["y_sample"])


_INS = ["x_prompt", "x_sample", "cache_k", "cache_v", "state_wkv", "c", "c_ctx", "w_ada", "b_ada", "g_pre_mix", "g_post_mix",
        "g_pre_ffn", "g_post_ffn", "w_in", "na_rpb", "sg_gain", "sg_w", "sg_b", "rw_w0", "rw_w2", "rw_a0", "rw_a2", "rw_g2",
        "rw_kk", "rw_ka", "rw_rk", "rw_ln_w", "rw_ln_b", "w_out", "w_router", "w_gate", "w_up", "w_down"]
_OUTS = [("y_prompt", (1, TP, D)), ("y_sample", (1, TS, D)), ("new_cache_k", (1, 1, TP, NAH, DH)),
         ("new_cache_v", (1, 1, TP, NAH, DH)), ("new_state_wkv", (1, 1, 2, 16, DH, DH))]
_SCRATCH = [("mod", (2, 6 * D)), ("ident", (P, P)), ("z", (NZ, P, T)), ("v", (NT, P, NAW)), ("vs", (NT, P, 512)),
            ("bias", (NAH * 15, GRID_W * (2 * GRID_W - 1))), ("par", (P, 72)), ("kk", (NPAIR, P, T)), ("o", (KD, P, T)),
            ("o_raw", (NPAIR, P, T)), ("mixed", (NT, P, D)), ("x1", (NT, P, D)), ("h2", (NT, P, D)), ("aff", (P, NT, NE)),
            ("afft", (NE, T)), ("slot", (P, NT, NE)), ("ffn", (NT, P, D))]


def kernel(**inputs):
    import concourse.bacc as bacc
    from concourse.bass_utils import run_bass_kernel_spmd

    nc = bacc.Bacc("TRN2", target_bir_lowering=False, num_devices=1)
    arrays, aps = {}, {}
    for name in _INS:
        x = np.ascontiguousarray(inputs[name])
        arrays[f"in_{name}"] = x
        aps[name] = nc.dram_tensor(f"in_{name}", x.shape, mybir.dt.from_np(x.dtype), kind="ExternalInput").ap()
    for name, shape in _OUTS:
        aps[name] = nc.dram_tensor(f"out_{name}", shape, F32, kind="ExternalOutput").ap()
    scratch = {name: nc.dram_tensor(f"scratch_{name}", shape, F32).ap() for name, shape in _SCRATCH}
    trunk(nc, aps, scratch)
    r = run_bass_kernel_spmd(nc, [arrays], core_ids=[0])
    return tuple(r.results[0][f"out_{name}"] for name, _ in _OUTS)
```

```python
from contextlib import ExitStack

import numpy as np

import concourse.bass as bass
from concourse import mybir

F32 = mybir.dt.float32
ALU = mybir.AluOpType
ACT = mybir.ActivationFunctionType
AX_X = mybir.AxisListType.X

P = 128
D = 2048
KD = D // P
TP, TS = 128, 512
T = TP + TS
NT = T // P
GRID_W, NAH, DH = 64, 8, 64
NAW = NAH * DH
SGG = 4
RW = 1024
NPAIR = RW // P
CK = 64
NCK = T // CK
NCP = TP // CK
NE, DE = 16, 1024
CAPS, CAPP = 2 * TS // NE, 2 * TP // NE
NCOL = 3 * NAW + 2 * 512 + 3 * RW + 256
NAW_C = 16
NORM_EPS, GN_EPS = 1e-6, 64e-5
NEG = -1.0e30
W2 = 2 * GRID_W - 1
NR = 2 * (TS // GRID_W) - 1
ZQ, ZK, ZU, ZR, ZKC, ZV, ZX = 0, 4, 8, 12, 20, 28, 36
NZ = 38


class Chain:

    def __init__(self, eng, sem):
        self.eng, self.sem, self.n = eng, sem, 0

    def link(self, ins):
        self.n += 1
        ins.then_inc(self.sem, 1)
        self.eng.wait_ge(self.sem, self.n)


def dram_ap(ap, offset, dims):
    return bass.AP(tensor=ap.tensor, offset=ap.offset + offset, ap=[list(d) for d in dims])


def bcast_rows(ap, offset, n, rows=P):
    return dram_ap(ap, offset, [[0, rows], [1, n]])


def block_modulation(nc, c, c_ctx, w_ada, b_ada, mod_d, cond_d, ident_d):
    G, NB = 1, 8
    GC = NB * 512
    RING = 4
    with ExitStack() as ctx:
        def sb(name, shape):
            return ctx.enter_context(nc.sbuf_tensor(name, shape, F32))

        def sem(name):
            return nc.alloc_semaphore(name)

        cond = sb("ada_cond", [2 * KD, P])
        cond_s = sb("ada_cond_silu", [2 * KD, P])
        ident = sb("ada_ident", [P, P])
        cond_t = sb("ada_cond_t", [P, 2, KD])
        ring = sb("ada_ring", [P, RING, GC])
        bias = sb("ada_bias", [2, GC])
        rows = sb("ada_rows", [2, GC])
        acc = ctx.enter_context(nc.psum_tensor("ada_acc", [P, NB, 512], F32))
        cond_in, bias_in, ident_made, ident_out = (sem(n) for n in ("ada_cond_in", "ada_bias_in", "ada_id", "ada_id_out"))
        silu_done, cond_turned, cond_ready = sem("ada_silu"), sem("ada_turned"), sem("ada_condready")
        w_in = [sem(f"ada_w{i}") for i in range(RING)]
        k_used, rows_ready, rows_out = (sem(n) for n in ("ada_kused", "ada_rows_rdy", "ada_out"))
        block = ctx.enter_context(nc.Block())

        @block.sync
        def _(sp):
            sp.dma_start(cond[0:KD, :], c_ctx.rearrange("(k p) -> k p", p=P)).then_inc(cond_in, 16)
            sp.dma_start(cond[KD:2 * KD, :], c.rearrange("o (k p) -> (o k) p", p=P)).then_inc(cond_in, 16)
            for n in range(G * KD):
                g, k = n // KD, n % KD
                if n >= RING:
                    sp.wait_ge(k_used, n - RING + 1)
                sp.dma_start(ring[:, n % RING, :], w_ada[0, k * P:(k + 1) * P, g * GC:(g + 1) * GC]).then_inc(w_in[n % RING], 16)

        @block.gpsimd
        def _(pool):
            nc.gpsimd.memset(ident[:], 0.0).then_inc(ident_made, 1)
            pool.wait_ge(ident_made, 1)
            nc.gpsimd.affine_select(out=ident[:], in_=ident[:], compare_op=ALU.not_equal, fill=1.0, base=0,
                                    pattern=[[-1, P]], channel_multiplier=1).then_inc(ident_made, 1)
            pool.wait_ge(ident_made, 2)
            pool.dma_start(ident_d, ident[:]).then_inc(ident_out, 16)
            pool.wait_ge(ident_out, 16)

        @block.scalar
        def _(act):
            for g in range(G):
                if g:
                    act.wait_ge(rows_ready, g)
                act.dma_start(bias[:], bcast_rows(b_ada, g * GC, GC, 2)).then_inc(bias_in, 16)
                if g == 0:
                    act.wait_ge(cond_in, 32)
                    nc.scalar.activation(cond_s[:], cond[:], ACT.Silu).then_inc(silu_done, 1)
                act.wait_ge(rows_ready, g + 1)
                act.dma_start(mod_d[:, g * GC:(g + 1) * GC], rows[:]).then_inc(rows_out, 16)
            act.wait_ge(cond_ready, 1)
            act.dma_start(cond_d, cond_t[:].rearrange("p c k -> p (c k)")).then_inc(rows_out, 16)
            act.wait_ge(rows_out, 16 * (G + 1))

        @block.tensor
        def _(pe):
            pe.wait_ge(silu_done, 1)
            pe.wait_ge(ident_made, 2)
            pe.transpose(acc[:, 0, 0:2 * KD], cond_s[:], ident[0:2 * KD, 0:2 * KD]).then_inc(cond_turned, 1)
            pe.wait_ge(cond_ready, 1)
            for n in range(G * KD):
                g, k = n // KD, n % KD
                pe.wait_ge(w_in[n % RING], 16 * (n // RING + 1))
                if k == 0 and g:
                    pe.wait_ge(rows_ready, g)
                for b in range(NB):
                    mm = pe.matmul(acc[0:2, b, :], cond_t[:, :, k], ring[:, n % RING, b * 512:(b + 1) * 512],
                                   start=(k == 0), stop=(k == KD - 1))
                mm.then_inc(k_used, 1)

        @block.vector
        def _(dve):
            dve.wait_ge(cond_turned, 1)
            nc.vector.tensor_copy(cond_t[:].rearrange("p c k -> p (c k)"), acc[:, 0, 0:2 * KD]).then_inc(cond_ready, 1)
            for g in range(G):
                dve.wait_ge(k_used, KD * (g + 1))
                dve.wait_ge(bias_in, 16 * (g + 1))
                if g:
                    dve.wait_ge(rows_out, 16 * g)
                for b in range(NB):
                    tt = nc.vector.tensor_tensor(rows[:, b * 512:(b + 1) * 512], acc[0:2, b, :],
                                                 bias[:, b * 512:(b + 1) * 512], ALU.add)
                tt.then_inc(rows_ready, 1)


def block_projection(nc, x_prompt, x_sample, g_pre, w_in, w_ada, b_ada, cond_d, mod_d, ident_d, z_d, v_d, vs_d):
    MC, MG0 = 1024, 3
    NMG = 4 * D // MC
    MR = 4
    WB = 256
    NBLK = NCOL // WB
    KINDS = "zzvzs" + "z" * 7
    H0 = 5
    ZROW = [ZQ, ZK, None, ZU, None]
    with ExitStack() as ctx:
        def sb(name, shape):
            return ctx.enter_context(nc.sbuf_tensor(name, shape, F32))

        def sem(name):
            return nc.alloc_semaphore(name)

        ident = sb("pj_ident", [P, P])
        xt = sb("pj_x", [P, 2, D])
        junk = sb("pj_junk", [P, D])
        ssq = sb("pj_ssq", [P, NT])
        rstd = sb("pj_rstd", [P, NT])
        rr = sb("pj_rr", [P, NT])
        modr = sb("pj_modr", [5 * KD, P])
        modt = sb("pj_modt", [P, 5, KD])
        gsc = sb("pj_gsc", [P, 2, KD])
        hT = sb("pj_hT", [P, KD, T])
        ring = sb("pj_ring", [P, 2, KD, WB])
        stage = sb("pj_stage", [P, 4, 768])
        cond = sb("pj_cond", [P, 2 * KD])
        m_ring = sb("pj_mring", [P, MR, 2, MC])
        m_acc = sb("pj_macc", [P, NMG, 2, MC])
        pick = sb("pj_pick", [P, 2, 2])
        ps = ctx.enter_context(nc.psum_tensor("pj_ps", [P, 8, 512], F32))
        const_in, x_in0, x_in1 = sem("pj_const_in"), sem("pj_x_in0"), sem("pj_x_in1")
        x_in = (x_in0, x_in1)
        x_free, ss_done, rs_done, xn_done = sem("pj_xfree"), sem("pj_ss"), sem("pj_rs"), sem("pj_xn")
        mod_turned, mod_ready, dchain = sem("pj_modturn"), sem("pj_modrdy"), sem("pj_dchain")
        turned, h_act, h_dve = sem("pj_turned"), sem("pj_hact"), sem("pj_hdve")
        w_got = [sem("pj_w0"), sem("pj_w1")]
        col_done, ev_act, ev_dve = sem("pj_col"), sem("pj_evact"), sem("pj_evdve")
        out_sem = [sem(f"pj_out{i}") for i in range(4)]
        m_got = [sem(f"pj_mgot{i}") for i in range(MR)]
        mac, m_bias, picked, m_summed, m_rows, m_out = (sem("pj_" + n) for n in ("mac", "mbias", "picked", "msum", "mrows", "mout"))
        block = ctx.enter_context(nc.Block())

        def x_rows(t):
            return x_prompt[0] if t == 0 else x_sample[0, (t - 1) * P:t * P, :]

        def w_cols(b):
            return w_in[0, :, bass.ds(b * WB, WB)].rearrange("(k p) n -> p k n", p=P)

        def group_of(h):
            return h - MG0 if not isinstance(h, int) or MG0 <= h < MG0 + NMG else None

        m_tiles = [xt[0:2, 0, :], xt[0:2, 1, :]] + [ring[0:2, 1].rearrange("p k n -> p (k n)")[:, i * D:(i + 1) * D] for i in range(2)]

        def over_blocks(eng, body, first=0):
            for h in range(first, H0):
                for half in range(2):
                    body(h, half, KINDS[h])
            with eng.Fori(H0, NBLK // 2) as h:
                for half in range(2):
                    body(h, half, "z")
            body(NBLK // 2, 0, "z")

        @block.sync
        def _(sp):
            for t in range(NT):
                if t >= 2:
                    sp.wait_ge(turned, 4 * (t - 1))
                sp.dma_start(xt[:, t % 2, :], x_rows(t)).then_inc(x_in[t % 2], 16)
                if t == 0:
                    sp.dma_start(ident[:], ident_d).then_inc(const_in, 16)
                    for i, (cnd, part) in enumerate(((0, 0), (0, 1), (1, 0), (1, 1))):
                        sp.dma_start(modr[i * KD:(i + 1) * KD, :],
                                     mod_d[cnd, part * D:(part + 1) * D].rearrange("(k p) -> k p", p=P)).then_inc(const_in, 16)
                    sp.dma_start(modr[4 * KD:5 * KD, :], g_pre.rearrange("o (k p) -> (o k) p", p=P)).then_inc(const_in, 16)
                    sp.dma_start(cond[:], cond_d).then_inc(const_in, 16)
                if t == 1:
                    for b in range(2):
                        sp.dma_start(ring[:, b, :, :], w_cols(b)).then_inc(w_got[b], 16)

            def load(h, half, kind):
                sp.wait_ge(col_done, 4 * h + 2 * half - 2)
                sp.dma_start(ring[:, half, :, :], w_cols(2 * h + half)).then_inc(w_got[half], 16)
                g = group_of(h)
                if g is not None:
                    for i in range(4 * half, 4 * half + 4):
                        if not isinstance(g, int) or 8 * g + i >= MR:
                            sp.wait_ge(mac, 4 * (8 * g + i - MR + 1))
                        src = w_ada[0, 2 * i * P:(2 * i + 2) * P, bass.ds(2 * D + g * MC, MC)].rearrange("(k p) n -> p k n", p=P)
                        sp.dma_start(m_ring[:, i % MR], src).then_inc(m_got[i % MR], 16)
            over_blocks(sp, load, first=1)
            sp.wait_ge(turned, 4 * NT)
            sp.wait_ge(col_done, 2 * (NBLK - 1))
            for i in range(4):
                sp.dma_start(m_tiles[i], bcast_rows(b_ada, (2 + i) * D, D, 2)).then_inc(m_bias, 16)
            for i in range(4):
                sp.wait_ge(m_rows, i + 1)
                sp.dma_start(mod_d[:, (2 + i) * D:(3 + i) * D], m_tiles[i]).then_inc(m_out, 16)
            sp.wait_ge(m_out, 64)

        @block.gpsimd
        def _(pool):
            def store(h, half, kind):
                for j in range(2):
                    slot, n = 2 * half + j, 4 * h + 2 * half + j
                    pool.wait_ge(ev_act, n + 1)
                    pool.wait_ge(ev_dve, n + 1)
                    if kind == "z":
                        row = ZROW[h] if isinstance(h, int) and h < H0 else ZR + 4 * (h - H0)
                        pool.dma_start(z_d[bass.ds(row + 2 * half + j, 1)].rearrange("o p n -> p (o n)"),
                                       stage[:, slot, 0:T]).then_inc(out_sem[slot], 16)
                    else:
                        dst = v_d if kind == "v" else vs_d
                        t0, t1 = ((0, 2), (2, 5))[j]
                        pool.dma_start(dst[t0:t1, :, half * WB:(half + 1) * WB].rearrange("t p c -> p t c"),
                                       stage[:, slot, 0:WB * (t1 - t0)].rearrange("p (t c) -> p t c", c=WB)).then_inc(out_sem[slot], 16)
            over_blocks(pool, store)
            for s in range(4):
                pool.wait_ge(out_sem[s], 16 * len([n for n in range(2 * NBLK) if n % 4 == s]))

        @block.scalar
        def _(act):
            for t in range(NT):
                act.wait_ge(x_in[t % 2], 16 * (t // 2 + 1))
                nc.scalar.activation(junk[:], xt[:, t % 2, :], ACT.Square, accum_out=ssq[:, t:t + 1]).then_inc(ss_done, 1)
                act.wait_ge(rs_done, 3 * t + 1)
                nc.scalar.activation(rr[:, t:t + 1], rstd[:, t:t + 1], ACT.Sqrt).then_inc(ss_done, 1)
                for q in (0, 2):
                    act.wait_ge(turned, 4 * t + q + 1)
                    act.wait_ge(mod_ready, 1)
                    for j in range(4):
                        k, cnd = 4 * q + j, min(t, 1)
                        a = nc.scalar.activation(hT[:, k, t * P:(t + 1) * P], ps[:, (4 * t + q) % 4, j * P:(j + 1) * P],
                                                 ACT.Identity, scale=gsc[:, cnd, k:k + 1],
                                                 bias=modt[:, 2 * cnd, k:k + 1])
                    a.then_inc(h_act, 1)

            def evacuate(h, half, kind):
                for j in range(2):
                    n, slot, base = 4 * h + 2 * half + j, 2 * half + j, 4 * half
                    act.wait_ge(col_done, n + 1)
                    if not isinstance(h, int) or h:
                        act.wait_ge(out_sem[slot], 16 * h)
                    if kind == "z":
                        a = nc.scalar.copy(stage[:, slot, TP:T], ps[:, base + 2 * j, :])
                    elif j == 0:
                        a = nc.scalar.copy(stage[:, slot, 0:WB], ps[:, base, 0:WB])
                    else:
                        a = nc.scalar.copy(stage[:, slot, 0:2 * WB], ps[:, base + 2, :])
                    a.then_inc(ev_act, 1)
            over_blocks(act, evacuate)

        @block.vector
        def _(dve):
            ch = Chain(dve, dchain)
            dve.wait_ge(mod_turned, 1)
            ch.link(nc.vector.tensor_copy(modt[:].rearrange("p a k -> p (a k)"), ps[:, 4, 0:5 * KD]))
            for cnd in range(2):
                g2 = nc.vector.scalar_tensor_tensor(gsc[:, cnd, :], modt[:, 2 * cnd + 1, :], 1.0, modt[:, 4, :], ALU.add, ALU.mult)
            g2.then_inc(mod_ready, 1)

            for t in range(NT):
                dve.wait_ge(ss_done, 2 * t + 1)
                nc.vector.tensor_scalar(rstd[:, t:t + 1], ssq[:, t:t + 1], 1.0 / D, NORM_EPS, ALU.mult, ALU.add).then_inc(rs_done, 1)
                dve.wait_ge(ss_done, 2 * t + 2)
                nc.vector.reciprocal(rstd[:, t:t + 1], rr[:, t:t + 1]).then_inc(rs_done, 1)
                dve.wait_ge(rs_done, 3 * t + 2)
                nc.vector.tensor_scalar(xt[:, t % 2, :], xt[:, t % 2, :], rstd[:, t:t + 1], None, ALU.mult).then_inc(rs_done, 1)
                for q in (1, 3):
                    dve.wait_ge(turned, 4 * t + q + 1)
                    if t == 0 and q == 1:
                        dve.wait_ge(mod_ready, 1)
                    for j in range(4):
                        k, cnd = 4 * q + j, min(t, 1)
                        a = nc.vector.tensor_scalar(hT[:, k, t * P:(t + 1) * P], ps[:, (4 * t + q) % 4, j * P:(j + 1) * P],
                                                    gsc[:, cnd, k:k + 1], modt[:, 2 * cnd, k:k + 1], ALU.mult, ALU.add)
                    a.then_inc(h_dve, 1)

            def evacuate(h, half, kind):
                for j in range(2):
                    n, slot, base = 4 * h + 2 * half + j, 2 * half + j, 4 * half
                    g = group_of(h)
                    if g is not None:
                        for k in range(8 * half + 4 * j, 8 * half + 4 * j + 4):
                            accumulate(g, k)
                    dve.wait_ge(col_done, n + 1)
                    if not isinstance(h, int) or h:
                        dve.wait_ge(out_sem[slot], 16 * h)
                    if kind == "z":
                        a = nc.vector.tensor_copy(stage[:, slot, 0:TP], ps[:, base + 2 * j + 1, 0:TP])
                    elif j == 0:
                        a = nc.vector.tensor_copy(stage[:, slot, WB:2 * WB], ps[:, base + 1, 0:WB])
                    else:
                        a = nc.vector.tensor_copy(stage[:, slot, 2 * WB:3 * WB], ps[:, base + 3, 0:WB])
                    a.then_inc(ev_dve, 1)

            def accumulate(g, k):
                w = m_ring[:, (k // 2) % MR, k % 2, :]
                for cnd in range(2):
                    acc = m_acc[:, bass.ds(g, 1), cnd, :].rearrange("p o n -> p (o n)")
                    scalar = cond[:, cnd * KD + k:cnd * KD + k + 1]
                    if k % 2 == 0 and cnd == 0:
                        dve.wait_ge(m_got[(k // 2) % MR], 32 * g + 16 * (k // 8) + 16)
                    if k == 0:
                        a = nc.vector.tensor_scalar(acc, w, scalar, None, ALU.mult)
                    else:
                        dve.wait_ge(mac, 32 * g + 2 * k + cnd - 1)
                        a = nc.vector.scalar_tensor_tensor(acc, w, scalar, acc, ALU.mult, ALU.add)
                    a.then_inc(mac, 1)

            for cnd in range(2):
                nc.vector.memset(pick[:, cnd, cnd:cnd + 1], 1.0)
                last = nc.vector.memset(pick[:, cnd, 1 - cnd:2 - cnd], 0.0)
            last.then_inc(picked, 1)
            over_blocks(dve, evacuate)
            dve.wait_ge(m_bias, 64)
            for i in range(4):
                dve.wait_ge(m_summed, i + 1)
                base = 4 * ((i + 1) % 2)
                nc.vector.tensor_tensor(m_tiles[i], ps[0:2, base:base + 4, :].rearrange("p b n -> p (b n)"), m_tiles[i], ALU.add).then_inc(m_rows, 1)

        @block.tensor
        def _(pe):
            pe.wait_ge(const_in, 16 * 7)
            pe.transpose(ps[:, 4, 0:5 * KD], modr[:], ident[0:5 * KD, 0:5 * KD]).then_inc(mod_turned, 1)
            for t in range(NT):
                pe.wait_ge(rs_done, 3 * t + 3)
                for q in range(4):
                    if t:
                        pe.wait_ge(h_dve if q % 2 else h_act, 2 * (t - 1) + q // 2 + 1)
                    for j in range(4):
                        k = 4 * q + j
                        mm = pe.transpose(ps[:, (4 * t + q) % 4, j * P:(j + 1) * P], xt[:, t % 2, k * P:(k + 1) * P], ident[:])
                    mm.then_inc(turned, 1)
            pe.wait_ge(h_act, 2 * NT)
            pe.wait_ge(h_dve, 2 * NT)

            def multiply(h, half, kind):
                base = 4 * half
                pe.wait_ge(w_got[half], 16 * (h + 1))
                if not isinstance(h, int) or h:
                    pe.wait_ge(ev_act, 4 * h + 2 * half - 2)
                    pe.wait_ge(ev_dve, 4 * h + 2 * half - 2)
                for j in range(2):
                    if kind == "z":
                        for dst, t0, t1 in ((ps[:, base + 2 * j, :], TP, T), (ps[:, base + 2 * j + 1, 0:TP], 0, TP)):
                            for k in range(KD):
                                mm = pe.matmul(dst, ring[:, half, k, j * P:(j + 1) * P], hT[:, k, t0:t1],
                                               start=(k == 0), stop=(k == KD - 1))
                    else:
                        for t, bank, c0 in (((0, 0, 0), (1, 1, 0)), ((2, 2, 0), (3, 2, WB), (4, 3, 0)))[j]:
                            for k in range(KD):
                                mm = pe.matmul(ps[:, base + bank, c0:c0 + WB], hT[:, k, t * P:(t + 1) * P], ring[:, half, k, :],
                                               start=(k == 0), stop=(k == KD - 1))
                    mm.then_inc(col_done, 1)
            over_blocks(pe, multiply)
            pe.wait_ge(picked, 1)
            pe.wait_ge(mac, 32 * NMG)
            for i in range(4):
                if i == 0:
                    pe.wait_ge(ev_act, 2 * (NBLK - 1))
                    pe.wait_ge(ev_dve, 2 * (NBLK - 1))
                elif i == 1:
                    pe.wait_ge(ev_act, 2 * NBLK)
                    pe.wait_ge(ev_dve, 2 * NBLK)
                else:
                    pe.wait_ge(m_rows, i - 1)
                for b in range(4):
                    g, c0 = (i * D + b * 512) // MC, (i * D + b * 512) % MC
                    for cnd in range(2):
                        mm = pe.matmul(ps[0:2, 4 * ((i + 1) % 2) + b, :], pick[:, cnd, :], m_acc[:, g, cnd, c0:c0 + 512],
                                       start=(cnd == 0), stop=(cnd == 1))
                mm.then_inc(m_summed, 1)


def block_gating_and_keys(nc, z_d, vs_d, sg_gain, sg_w, sg_b, vectors, rpb, ident_d, bias_d, par_d, kk_d, o_d):
    NV = sum(v_rows for _, v_rows in vectors)
    with ExitStack() as ctx:
        def sb(name, shape):
            return ctx.enter_context(nc.sbuf_tensor(name, shape, F32))

        def sem(name):
            return nc.alloc_semaphore(name)

        ident = sb("gk_ident", [P, P])
        vs = sb("gk_vs", [P, NT, SGG, P])
        sq = sb("gk_sq", [P, NT, SGG, P])
        gain = sb("gk_gain", [P, SGG, P])
        ws = sb("gk_ws", [P, SGG, P])
        wst = sb("gk_wst", [P, SGG, P])
        brow = sb("gk_brow", [1, SGG, P])
        ones = sb("gk_ones", [1, P])
        ss, sr, rs = sb("gk_ss", [P, NT * SGG]), sb("gk_sr", [P, NT * SGG]), sb("gk_rs", [P, NT * SGG])
        eps = sb("gk_eps", [P, 2])
        ut = sb("gk_ut", [P, SGG, T])
        ob = sb("gk_ob", [P, SGG, T])
        vrow = sb("gk_vrow", [NV, P])
        par = sb("gk_par", [P, NV])
        blk = sb("gk_blk", [P, P])
        kt = sb("gk_kt", [P, NPAIR, T])
        k2 = sb("gk_k2", [P, 2, T])
        nrm = sb("gk_nrm", [P, 2, T])
        ps = ctx.enter_context(nc.psum_tensor("gk_ps", [P, 8, 512], F32))
        small_in, vs_in, ut_in, k_in = sem("gk_small"), sem("gk_vsin"), sem("gk_utin"), sem("gk_kin")
        made, made_eps = sem("gk_made"), sem("gk_mdeps")
        turned, copied, dch = sem("gk_turned"), sem("gk_copied"), sem("gk_dch")
        ssd, srd, vnd, mixd, gated = sem("gk_ssd"), sem("gk_srd"), sem("gk_vnd"), sem("gk_mix"), sem("gk_gated")
        kkd, sqd, sumd, sqrtd, kkn = sem("gk_kkd"), sem("gk_sqd"), sem("gk_sumd"), sem("gk_sqrtd"), sem("gk_kkn")
        out = sem("gk_out")
        table = sb("gk_table", [NAH * NR, W2])
        filled, rpb_in, table_out = sem("gk_filled"), sem("gk_rpbin"), sem("gk_tabout")
        block = ctx.enter_context(nc.Block())

        @block.sync
        def _(sp):
            sp.dma_start(ident[:], ident_d).then_inc(small_in, 16)
            r = 0
            for v, n in vectors:
                sp.dma_start(vrow[r:r + n, :], v).then_inc(small_in, 16)
                r += n
            sp.dma_start(ws[:], sg_w[0].rearrange("g p q -> p g q")).then_inc(small_in, 16)
            sp.dma_start(brow[:], sg_b).then_inc(small_in, 16)
            sp.dma_start(gain[:].rearrange("p g c -> p (g c)"), bcast_rows(sg_gain, 0, 512)).then_inc(small_in, 16)
            sp.dma_start(vs[:].rearrange("p t g c -> p t (g c)"), vs_d.rearrange("t p c -> p t c")).then_inc(vs_in, 16)
            sp.dma_start(ut[:], z_d[ZU:ZU + SGG].rearrange("g p t -> p g t")).then_inc(ut_in, 16)
            sp.dma_start(kt[:], z_d[ZKC:ZKC + NPAIR].rearrange("g p t -> p g t")).then_inc(k_in, 16)
            sp.wait_ge(copied, 1)
            sp.dma_start(par_d, par[:]).then_inc(out, 16)
            sp.wait_ge(gated, 2 * SGG)
            sp.dma_start(o_d[4:4 + SGG].rearrange("g p t -> p g t"), ob[:]).then_inc(out, 16)
            for p in range(NPAIR):
                sp.wait_ge(kkn, p + 1)
                sp.dma_start(kk_d[p], kt[:, p, :]).then_inc(out, 16)
            sp.wait_ge(out, 16 * (2 + NPAIR))

        @block.gpsimd
        def _(pool):
            nc.gpsimd.memset(ones[:], 1.0)
            nc.gpsimd.memset(eps[:, 0:1], NORM_EPS)
            nc.gpsimd.memset(eps[:, 1:2], 1e-12).then_inc(made, 1)
            nc.gpsimd.memset(table[:], NEG).then_inc(filled, 1)
            pool.wait_ge(filled, 1)
            pool.dma_start(table[:, GRID_W - NAW_C:GRID_W + NAW_C - 1], rpb[0].rearrange("h r c -> (h r) c")).then_inc(rpb_in, 16)
            pool.wait_ge(rpb_in, 16)
            pool.dma_start(bias_d.rearrange("r (c w) -> r c w", w=W2),
                           table[:].unsqueeze(1).to_broadcast([NAH * NR, GRID_W, W2])).then_inc(table_out, 16)
            pool.wait_ge(table_out, 16)

        @block.tensor
        def _(pe):
            pe.wait_ge(small_in, 16 * (4 + len(vectors)))
            pe.transpose(ps[:, 0, 0:NV], vrow[:], ident[0:NV, 0:NV]).then_inc(turned, 1)
            for g in range(SGG):
                tr = pe.transpose(ps[:, 1, g * P:(g + 1) * P], ws[:, g, :], ident[:])
            tr.then_inc(turned, 1)
            pe.wait_ge(made, 2)
            for p in range(NPAIR):
                pe.wait_ge(sqd, p + 1)
                b = 2 + 2 * (p % 3)
                if p >= 3:
                    pe.wait_ge(sqrtd, p - 2)
                pe.matmul(ps[:, b, :], blk[:], k2[:, p % 2, TP:T], start=True, stop=True)
                pe.matmul(ps[:, b + 1, 0:TP], blk[:], k2[:, p % 2, 0:TP], start=True, stop=True).then_inc(sumd, 1)
            pe.wait_ge(vnd, 1)
            pe.wait_ge(copied, 2)
            pe.wait_ge(sqrtd, NPAIR)
            for g in range(SGG):
                if g >= 4:
                    pe.wait_ge(gated, 2 * (g - 3))
                for t in range(NT):
                    dst = ps[:, 4 + g, 0:P] if t == 0 else ps[:, g, (t - 1) * P:t * P]
                    pe.matmul(dst, vs[:, t, g, :], wst[:, g, :], start=True, stop=False)
                    mm = pe.matmul(dst, ones[:], brow[:, g, :], start=False, stop=True)
                    if t == 0 or t == NT - 1:
                        mm.then_inc(mixd, 1)

        @block.scalar
        def _(act):
            act.wait_ge(ssd, 1)
            act.wait_ge(made, 2)
            nc.scalar.activation(sr[:], ss[:], ACT.Sqrt, scale=1.0 / P, bias=eps[:, 0:1]).then_inc(srd, 1)
            for p in range(NPAIR):
                act.wait_ge(kkd, p + 1)
                if p >= 2:
                    act.wait_ge(sumd, p - 1)
                nc.scalar.activation(k2[:, p % 2, :], kt[:, p, :], ACT.Square).then_inc(sqd, 1)
                act.wait_ge(sumd, p + 1)
                b = 2 + 2 * (p % 3)
                if p >= 2:
                    act.wait_ge(kkn, p - 1)
                nc.scalar.activation(nrm[:, p % 2, TP:T], ps[:, b, :], ACT.Sqrt, bias=eps[:, 1:2])
                nc.scalar.activation(nrm[:, p % 2, 0:TP], ps[:, b + 1, 0:TP], ACT.Sqrt, bias=eps[:, 1:2]).then_inc(sqrtd, 1)

        @block.vector
        def _(dve):
            ch = Chain(dve, dch)
            nc.vector.memset(blk[0:DH, 0:DH], 1.0)
            nc.vector.memset(blk[0:DH, DH:P], 0.0)
            nc.vector.memset(blk[DH:P, 0:DH], 0.0)
            nc.vector.memset(blk[DH:P, DH:P], 1.0).then_inc(made, 1)
            dve.wait_ge(turned, 1)
            nc.vector.tensor_copy(par[:], ps[:, 0, 0:NV]).then_inc(copied, 1)
            dve.wait_ge(turned, 2)
            nc.vector.tensor_copy(wst[:].rearrange("p g c -> p (g c)"), ps[:, 1, :]).then_inc(copied, 1)
            dve.wait_ge(copied, 1)
            dve.wait_ge(k_in, 16)
            for p in range(NPAIR):
                nc.vector.tensor_scalar(kt[:, p, :], kt[:, p, :], par[:, p:p + 1], None, ALU.mult).then_inc(kkd, 1)
            dve.wait_ge(vs_in, 16)
            ch.link(nc.vector.tensor_tensor(sq[:], vs[:], vs[:], ALU.mult))
            nc.vector.tensor_reduce(ss[:], sq[:].rearrange("p t g c -> p (t g) c"), AX_X, ALU.add).then_inc(ssd, 1)
            for p in range(NPAIR):
                dve.wait_ge(sqrtd, p + 1)
                ch.link(nc.vector.reciprocal(nrm[:, p % 2, :], nrm[:, p % 2, :]))
                dve.wait_ge(kkd, p + 1)
                nc.vector.tensor_tensor(kt[:, p, :], kt[:, p, :], nrm[:, p % 2, :], ALU.mult).then_inc(kkn, 1)
                if p == 1:
                    dve.wait_ge(srd, 1)
                    ch.link(nc.vector.reciprocal(rs[:], sr[:]))
                    v3 = vs[:].rearrange("p t g c -> p (t g) c")
                    ch.link(nc.vector.tensor_tensor(v3, v3, rs[:].unsqueeze(2).to_broadcast([P, NT * SGG, P]), ALU.mult))
                    dve.wait_ge(small_in, 16 * (4 + len(vectors)))
                    for t in range(NT):
                        vn = nc.vector.tensor_tensor(vs[:, t], vs[:, t], gain[:], ALU.mult)
                    vn.then_inc(vnd, 1)
            dve.wait_ge(ut_in, 16)
            for g in range(SGG):
                dve.wait_ge(mixd, 2 * g + 1)
                nc.vector.tensor_tensor(ob[:, g, 0:TP], ps[:, 4 + g, 0:TP], ut[:, g, 0:TP], ALU.mult).then_inc(gated, 1)
                dve.wait_ge(mixd, 2 * g + 2)
                nc.vector.tensor_tensor(ob[:, g, TP:T], ps[:, g, :], ut[:, g, TP:T], ALU.mult).then_inc(gated, 1)


def block_attention(nc, z_d, v_d, cache_k, cache_v, ident_d, bias_d, o_d, new_k, new_v):
    GR = TS // GRID_W
    QS = DH ** -0.5
    U = NT
    NB = 4
    with ExitStack() as ctx:
        def sb(name, shape):
            return ctx.enter_context(nc.sbuf_tensor(name, shape, F32))

        def sem(name):
            return nc.alloc_semaphore(name)

        ident = sb("at_ident", [P, P])
        colmask = sb("at_colmask", [P, GRID_W])
        bias = sb("at_bias", [P, NB, TS + TP])
        qt = sb("at_qt", [P, T])
        ktile = sb("at_kt", [P, T])
        qpad = sb("at_qpad", [P, 2, T])
        vt = sb("at_vt", [P, NT, P])
        ck, cv = sb("at_ck", [P, P]), sb("at_cv", [P, P])
        kct = sb("at_kct", [P, P])
        nk = sb("at_nk", [P, P])
        sc = sb("at_sc", [P, 2, T])
        pr = sb("at_pr", [P, 2, T])
        pt = sb("at_pt", [P, 2, T])
        mx, nmx, sm, rc = (sb(f"at_{n}", [P, 2]) for n in ("mx", "nmx", "sm", "rc"))
        ot = sb("at_ot", [P, T])
        ps_s = ctx.enter_context(nc.psum_tensor("at_ps_s", [P, 2, 1024], F32))
        ps_t = ctx.enter_context(nc.psum_tensor("at_ps_t", [P, 1024], F32))
        ps_o = ctx.enter_context(nc.psum_tensor("at_ps_o", [P, 2, 512], F32))
        pre_in = sem("at_pre_in")
        pair_in, pair_used, bias_ready, bias_used = (sem(f"at_{n}") for n in ("pairin", "pairused", "biasrdy", "biasused"))
        bias_in = [sem(f"at_biasin{i}") for i in range(NB)]
        kct_t, kct_r, q_ready = sem("at_kctt"), sem("at_kctr"), sem("at_qready")
        scored, maxed, negd, expd, rcd, normed, turned, ptd, pvd = (sem(f"at_{n}") for n in
            ("scored", "maxed", "negd", "expd", "rcd", "normed", "turned", "ptd", "pvd"))
        begun = sem("at_begun")
        o_ready, o_out, nk_out, nv_out, ch_s = (sem(f"at_{n}") for n in ("oready", "oout", "nkout", "nvout", "chs"))
        block = ctx.enter_context(nc.Block())
        UP = 2 * U

        toep = dram_ap(bias_d, GRID_W - 1, [[GRID_W * W2, NAH * NR], [W2 - 1, GRID_W], [1, GRID_W]])

        @block.sync
        def _(sp):
            def load_bias(p, n):
                sp.wait_ge(bias_used, p * 8 + n + 1)
                for r2 in range(2):
                    row = (2 * p + n // 4) * NR + (GR - 1) - 2 * (n % 4) - r2
                    sp.dma_start(bias[r2 * GRID_W:(r2 + 1) * GRID_W, n % NB, 0:TS].rearrange("c (r k) -> c r k", k=GRID_W),
                                 toep[bass.ds(row, GR)].rearrange("r c k -> c r k")).then_inc(bias_in[n % NB], 16)

            sp.dma_start(ident[:], ident_d).then_inc(pre_in, 16)
            with sp.Fori(0, NAH // 2) as p:
                for n in range(NB):
                    load_bias(p, n)
                sp.wait_ge(pair_used, p + 1)
                cols = bass.ds(p * P, P)
                sp.dma_start(qt[:], z_d[bass.ds(ZQ + p, 1)].rearrange("o p t -> p (o t)")).then_inc(pair_in, 16)
                sp.dma_start(ktile[:], z_d[bass.ds(ZK + p, 1)].rearrange("o p t -> p (o t)")).then_inc(pair_in, 16)
                sp.dma_start(vt[:], v_d[:, :, cols].rearrange("t p c -> p t c")).then_inc(pair_in, 16)
                sp.dma_start(ck[:], cache_k[:, cols]).then_inc(pair_in, 16)
                sp.dma_start(cv[:], cache_v[:, cols]).then_inc(pair_in, 16)
                for n in range(NB, 8):
                    load_bias(p, n)
            sp.wait_ge(nk_out, 16 * (NAH // 2))
            sp.wait_ge(nv_out, 16 * (NAH // 2))
            sp.wait_ge(o_out, 16 * (NAH // 2))

        @block.gpsimd
        def _(pool):
            nc.gpsimd.memset(bias[:, :, TS:], 0.0)
            pch = Chain(pool, ch_s)
            pch.link(nc.gpsimd.memset(qpad[:], 0.0))
            pch.link(nc.gpsimd.memset(colmask[:], 0.0))
            half = NAW_C // 2
            for r2 in range(2):
                rows = slice(r2 * GRID_W, (r2 + 1) * GRID_W)
                m = colmask[rows, 0:GRID_W - NAW_C]
                pch.link(nc.gpsimd.affine_select(out=m, in_=m, compare_op=ALU.is_ge, fill=NEG, base=half,
                                                 pattern=[[1, GRID_W - NAW_C]], channel_multiplier=-1))
                m = colmask[rows, NAW_C:GRID_W]
                pch.link(nc.gpsimd.affine_select(out=m, in_=m, compare_op=ALU.is_ge, fill=NEG, base=half - 1 - NAW_C,
                                                 pattern=[[-1, GRID_W - NAW_C]], channel_multiplier=1))
            pool.sem_inc(pair_used, 1)
            pool.sem_inc(bias_used, NB)
            with pool.Fori(0, NAH // 2) as p:
                for n in range(8):
                    pool.wait_ge(bias_in[n % NB], p * 64 + (n // NB + 1) * 32)
                    b3 = bias[:, n % NB, 0:TS].rearrange("p (r k) -> p r k", k=GRID_W)
                    nc.gpsimd.tensor_tensor(b3, b3, colmask[:].unsqueeze(1).to_broadcast([P, GR, GRID_W]), ALU.add).then_inc(bias_ready, 1)
                    if n == 3:
                        pool.wait_ge(kct_r, p + 1)
                        pool.dma_start(new_k[:, bass.ds(p * P, P)], nk[:]).then_inc(nk_out, 16)
                        pool.dma_start(new_v[:, bass.ds(p * P, P)], vt[:, 0, :]).then_inc(nv_out, 16)
                        pool.wait_ge(nk_out, p * 16 + 16)
                        pool.wait_ge(nv_out, p * 16 + 16)
                pool.wait_ge(o_ready, 2 * p + 4)
                pool.dma_start(o_d[bass.ds(p, 1)].rearrange("o p t -> p (o t)"), ot[:]).then_inc(o_out, 16)
                pool.wait_ge(o_out, p * 16 + 16)
                pool.sem_inc(pair_used, 1)

        def unit(u):
            return u // U, u % U

        @block.tensor
        def _(pe):
            pe.wait_ge(pre_in, 16)
            with pe.Fori(0, NAH // 2) as p:
                pe.wait_ge(pair_in, p * 80 + 80)
                pe.wait_ge(ptd, p * UP + 1)
                pe.transpose(ps_t[:, 0:P], ck[:], ident[:])
                pe.transpose(ps_t[:, P:2 * P], ktile[:, 0:TP], ident[:]).then_inc(kct_t, 1)
                pe.wait_ge(kct_r, p + 1)
                pe.wait_ge(q_ready, p + 1)

                def scores(u):
                    hh, tile = unit(u)
                    s = u % 2
                    pe.wait_ge(maxed, p * UP + u + 1)
                    if tile == 0:
                        mm = pe.matmul(ps_s[:, s, 512:512 + TP], qpad[:, hh, 0:TP], ktile[:, 0:TP], start=True, stop=True)
                    else:
                        pe.matmul(ps_s[:, s, 0:512], qpad[:, hh, tile * P:(tile + 1) * P], ktile[:, TP:T], start=True, stop=True)
                        mm = pe.matmul(ps_s[:, s, 512:512 + P], qpad[:, hh, tile * P:(tile + 1) * P], kct[:], start=True, stop=True)
                    mm.then_inc(scored, 1)

                def values(u):
                    hh, tile = unit(u)
                    pe.wait_ge(normed, p * UP + u + 1)
                    pe.wait_ge(ptd, p * UP + u + 1)
                    first = 4 if tile == 0 else 0
                    for j in range(first, 5):
                        tr = pe.transpose(ps_t[:, j * P:(j + 1) * P], pr[:, u % 2, j * P:(j + 1) * P], ident[:])
                    tr.then_inc(turned, 1)
                    if u + 2 < UP:
                        scores(u + 2)
                    pe.wait_ge(ptd, p * UP + u + 2)
                    if u == 0:
                        pe.wait_ge(o_ready, 2 * p + 2)
                    dst = ps_o[hh * DH:(hh + 1) * DH, 1, 0:TP] if tile == 0 else ps_o[hh * DH:(hh + 1) * DH, 0, (tile - 1) * P:tile * P]
                    for j in range(first, 5):
                        if tile == 0:
                            vv = vt[:, 0, hh * DH:(hh + 1) * DH]
                        elif j < 4:
                            vv = vt[:, 1 + j, hh * DH:(hh + 1) * DH]
                        else:
                            vv = cv[:, hh * DH:(hh + 1) * DH]
                        mm = pe.matmul(dst, vv, pt[:, u % 2, j * P:(j + 1) * P], start=(j == first), stop=(j == 4))
                    mm.then_inc(pvd, 1)

                scores(0)
                scores(1)
                for u in range(UP):
                    values(u)

        @block.vector
        def _(dve):
            dve.sem_inc(maxed, 2)
            dve.sem_inc(ptd, 1)
            dve.sem_inc(pvd, 1)
            dve.sem_inc(o_ready, 2)
            dve.sem_inc(turned, 2)
            with dve.Fori(0, NAH // 2) as p:
                dve.wait_ge(pair_in, p * 80 + 80)
                dve.wait_ge(kct_t, p + 1)
                nc.vector.tensor_copy(kct[:], ps_t[:, 0:P])
                nc.vector.tensor_copy(nk[:], ps_t[:, P:2 * P]).then_inc(kct_r, 1)
                nc.vector.tensor_scalar(qpad[0:DH, 0, :], qt[0:DH, :], QS, None, ALU.mult)
                nc.vector.tensor_scalar(qpad[DH:P, 1, :], qt[DH:P, :], QS, None, ALU.mult).then_inc(q_ready, 1)

                def maximum(u):
                    hh, tile = unit(u)
                    s = u % 2
                    dve.wait_ge(scored, p * UP + u + 1)
                    if tile == 0:
                        nc.vector.tensor_copy(sc[:, s, 512:T], ps_s[:, s, 512:T])
                        nc.vector.tensor_reduce(mx[:, s:s + 1], ps_s[:, s, 512:T], AX_X, ALU.max).then_inc(maxed, 1)
                    else:
                        n = 4 * hh + tile - 1
                        dve.wait_ge(bias_ready, p * 8 + n + 1)
                        dve.sem_inc(begun, 1)
                        nc.vector.tensor_tensor_reduce(sc[:, s, :], ps_s[:, s, 0:T], bias[:, n % NB, :], 1.0, NEG,
                                                       ALU.add, ALU.max, mx[:, s:s + 1]).then_inc(maxed, 1)
                    dve.wait_ge(maxed, p * UP + u + 3)
                    if tile:
                        dve.sem_inc(bias_used, 1)
                    nc.vector.tensor_scalar(nmx[:, s:s + 1], mx[:, s:s + 1], -1.0, None, ALU.mult).then_inc(negd, 1)

                def normalise(u):
                    _, tile = unit(u)
                    s = u % 2
                    c0 = 512 if tile == 0 else 0
                    dve.wait_ge(expd, p * UP + u + 1)
                    nc.vector.reciprocal(rc[:, s:s + 1], sm[:, s:s + 1]).then_inc(rcd, 1)
                    dve.wait_ge(rcd, p * UP + u + 1)
                    nc.vector.tensor_scalar(pr[:, s, c0:T], pr[:, s, c0:T], rc[:, s:s + 1], None, ALU.mult).then_inc(normed, 1)

                maximum(0)
                maximum(1)
                for u in range(UP):
                    normalise(u)
                    if u + 2 < UP:
                        maximum(u + 2)

        @block.scalar
        def _(act):
            with act.Fori(0, NAH // 2) as p:
                def exponent(u):
                    _, tile = unit(u)
                    s = u % 2
                    c0 = 512 if tile == 0 else 0
                    act.wait_ge(negd, p * UP + u + 1)
                    act.wait_ge(turned, p * UP + u + 1)
                    nc.scalar.activation(pr[:, s, c0:T], sc[:, s, c0:T], ACT.Exp, bias=nmx[:, s:s + 1],
                                         accum_out=sm[:, s:s + 1]).then_inc(expd, 1)

                def copy_turned(u):
                    _, tile = unit(u)
                    c0 = 512 if tile == 0 else 0
                    act.wait_ge(turned, p * UP + u + 3)
                    nc.scalar.copy(pt[:, u % 2, c0:T], ps_t[:, c0:T]).then_inc(ptd, 1)

                exponent(0)
                for u in range(UP):
                    if u + 1 < UP:
                        exponent(u + 1)
                    copy_turned(u)
                act.wait_ge(pvd, p * UP + UP + 1)
                act.wait_ge(pair_used, p + 1)
                nc.scalar.copy(ot[:, TP:T], ps_o[:, 0, :]).then_inc(o_ready, 1)
                nc.scalar.copy(ot[:, 0:TP], ps_o[:, 1, 0:TP]).then_inc(o_ready, 1)


def block_rwkv(nc, z_d, kk_d, par_d, w2, a2, state, ident_d, o_raw_d, state_out):
    LAM = float(np.exp(-0.5))
    LEVELS = [2, 4, 8, 16, 32]
    BATCH = [(0, 4), (4, 8), (8, 10)]
    R = 6
    ORDER = [list(range(NCK)), list(range(NCP))[::-1] + list(range(NCP, NCK))[::-1]]

    plan = [("bk", b) for b in range(5)] + [("sc", c) for c in range(NCK)] + [("vt", b) for b in range(3)]
    plan += [("w", 0), ("a", 0), ("wa", 0)] + [("ti", b) for b in range(3)]
    for level in range(len(LEVELS)):
        plan += [("x", b, level) for b in range(3)]
        for b in range(3):
            plan += [("dt", b, level)] if level < len(LEVELS) - 1 else []
            plan += [("dtt", b, level)]
    NJ = len(plan)
    assert NJ % R == 0, NJ
    on_act = [j[0] in ("w", "a", "wa", "vt", "bk", "ti") for j in plan]
    NA, ND = sum(on_act), NJ - sum(on_act)
    index = {j: n for n, j in enumerate(plan)}
    FRONT = 3

    stages = [(i, s) for i in range(NCK) for s in ("pw", "u", "z")]
    LAST = 56
    timeline = []
    placed = 0
    for n in range(NJ):
        timeline.append(("job", n))
        while placed < len(stages) and placed * LAST < (n + 1) * len(stages):
            timeline.append(("seq", *stages[placed]))
            placed += 1
    PAD_AT = ("job", LAST + 1)
    SCAN_AT, EXP_AT, VPAD_AT = ("job", index[("wa", 0)] + 4), ("job", index[("wa", 0)] + 14), ("job", index[("wa", 0)] + 18)

    with ExitStack() as ctx:
        def sb(name, shape):
            return ctx.enter_context(nc.sbuf_tensor("rw_" + name, shape, F32))

        def sem(name):
            return nc.alloc_semaphore("rw_" + name)

        ident, par, pp = sb("ident", [P, P]), sb("par", [P, 72]), sb("pp", [P, 10])
        mask = sb("mask", [P, 2, 192])
        join = sb("join", [P, 7, P])
        reset = sb("reset", [P, T])
        xwa = sb("xwa", [P, T])
        w2p, a2p = sb("w2p", [P, 2, P]), sb("a2p", [P, 2, P])
        rt, kt, vt, kk = sb("rt", [P, T]), sb("kt", [P, T]), sb("vt", [P, T]), sb("kk", [P, T])
        sg, ar, cs, pq, qq = sb("sg", [P, T]), sb("ar", [P, T]), sb("cs", [P, T]), sb("pq", [P, T]), sb("qq", [P, T])
        e_in, e_ex, e_inv = sb("e_in", [P, T]), sb("e_ex", [P, T]), sb("e_inv", [P, T])
        bb, kd, hc = sb("bb", [P, T]), sb("kd", [P, T]), sb("hc", [P, NCK])
        halves = sb("halves", [P, NCK])
        ec = sb("ec", [P, 2, NCK])
        bkpad = sb("bkpad", [P, 2, NCK, 2, CK])
        vpad = sb("vpad", [P, NCK, 2, CK])
        apad = sb("apad", [P, 2, NCK, 2, CK])
        rbar = sb("rbar", [P, 2, T])
        bktok = sb("bktok", [P, 2, 2 * NCK, P])
        vtok = sb("vtok", [P, 2, NCK, P])
        sc = sb("sc", [P, 2, NCK, 2, 192])
        tm, xm = sb("tm", [P, NCK, P]), sb("xm", [P, NCK, P])
        tt = sb("tt", [P, 2, NCK, P])
        sin, s0, fo = (sb(n, [P, 2, P]) for n in ("sin", "s0", "fo"))
        st, tmp, fs, wsb, usb = (sb(n, [P, P]) for n in ("st", "tmp", "fs", "wsb", "usb"))
        of = sb("of", [P, 2, T])
        osum = sb("osum", [P, T])
        rot = ctx.enter_context(nc.psum_tensor("rw_rot", [P, R, 512], F32))
        wu = ctx.enter_context(nc.psum_tensor("rw_wu", [P, 512], F32))
        zo = ctx.enter_context(nc.psum_tensor("rw_zo", [P, 512], F32))

        once_in, loads, loads_free, made = sem("once"), sem("loads"), sem("loadsfree"), sem("made")
        job, act_ev, dve_ev = sem("job"), sem("actev"), sem("dveev")
        par_ready, xwa_ready = sem("parrdy"), sem("xwardy")
        cs_done, pq_done, bk_done, ex_done, ec_done, rb_done, pad_done, vpad_done = (sem(n) for n in
            ("cs", "pq", "bk", "ex", "ec", "rb", "pad", "vpad"))
        tinit, gch = sem("tinit"), sem("gch")
        w_done, w_ev, u_done, u_ev, z_done, z_ev, o_ev, s_ready = (sem(n) for n in ("wd", "we", "ud", "ue", "zd", "ze", "oe", "sr"))
        fs_done, fo_out, osum_done, o_out = sem("fs"), sem("foout"), sem("osum"), sem("oout")
        block = ctx.enter_context(nc.Block())
        NLOAD = 12 * 16

        def periods(eng, period):
            period(0, 0, first=True, last=False)
            with eng.Fori(0, NPAIR - 1) as q:
                period(q, 1, first=False, last=False)
                period(q + 1, 0, first=False, last=False)
            period(NPAIR - 1, 1, first=False, last=True)

        @block.sync
        def _(sp):
            def load(p):
                for dst, row in ((rt, ZR), (kt, ZKC), (vt, ZV)):
                    sp.dma_start(dst[:], z_d[bass.ds(row + p, 1)].rearrange("o p t -> p (o t)")).then_inc(loads, 16)
                sp.dma_start(kk[:], kk_d[bass.ds(p, 1)].rearrange("o p t -> p (o t)")).then_inc(loads, 16)
                for d in range(2):
                    sp.dma_start(w2p[0:64, d, :], w2[0, d, :, bass.ds(p * P, P)]).then_inc(loads, 16)
                    sp.dma_start(a2p[64:P, d, :], a2[0, d, :, bass.ds(p * P, P)]).then_inc(loads, 16)
                    for hh in range(2):
                        sp.dma_start(sin[hh * DH:(hh + 1) * DH, d, hh * DH:(hh + 1) * DH],
                                     state[d, bass.ds(2 * p + hh, 1)].rearrange("o v k -> (o v) k")).then_inc(loads, 16)

            def store(p):
                for d in range(2):
                    sp.wait_ge(w_ev, (2 * p + d) * NCK + NCP + 1)
                    for hh in range(2):
                        sp.dma_start(state_out[d, bass.ds(2 * p + hh, 1)].rearrange("o v k -> (o v) k"),
                                     fo[hh * DH:(hh + 1) * DH, d, hh * DH:(hh + 1) * DH]).then_inc(fo_out, 16)
                sp.wait_ge(osum_done, p + 2)
                sp.dma_start(o_raw_d[bass.ds(p, 1)].rearrange("o p t -> p (o t)"), osum[:]).then_inc(o_out, 16)

            sp.dma_start(ident[:], ident_d).then_inc(once_in, 16)
            sp.dma_start(par[:], par_d).then_inc(once_in, 16)
            sp.dma_start(xwa[:], z_d[ZX]).then_inc(once_in, 16)
            sp.wait_ge(made, 1)
            load(0)
            with sp.Fori(0, NPAIR - 1) as q:
                sp.wait_ge(loads_free, q + 1)
                load(q + 1)
                store(q)
            store(NPAIR - 1)
            sp.wait_ge(o_out, 16 * NPAIR + 1)
            sp.wait_ge(fo_out, 16 * 4 * NPAIR + 1)

        @block.gpsimd
        def _(pool):
            ch = Chain(pool, gch)
            for t in (w2p, a2p, sin, bkpad, vpad, apad):
                last = nc.gpsimd.memset(t[:], 0.0)
            last.then_inc(made, 1)
            ch.link(nc.gpsimd.memset(mask[:], 1.0))
            for d in range(2):
                sgn = 1 if d == 0 else -1
                m = mask[:, d, 0:P]
                ch.link(nc.gpsimd.affine_select(out=m, in_=m, compare_op=ALU.is_gt, fill=0.0, base=0,
                                                pattern=[[sgn, P]], channel_multiplier=-sgn))
                for hh in range(2):
                    m = mask[hh * CK:(hh + 1) * CK, d, P:P + CK]
                    ch.link(nc.gpsimd.affine_select(out=m, in_=m, compare_op=ALU.is_ge, fill=0.0, base=0,
                                                    pattern=[[sgn, CK]], channel_multiplier=-sgn))
            ch.link(nc.gpsimd.memset(join[:], 1.0))
            for i in range(7):
                n = 2 ** i
                m = join[:, i, :].rearrange("p (b n) -> p b n", n=n)
                ch.link(nc.gpsimd.affine_select(out=m, in_=m, compare_op=ALU.is_ge, fill=0.0, base=0,
                                                pattern=[[-n, P // n], [0, n]], channel_multiplier=1))
                ch.link(nc.gpsimd.affine_select(out=m, in_=m, compare_op=ALU.is_ge, fill=0.0, base=n - 1,
                                                pattern=[[n, P // n], [0, n]], channel_multiplier=-1))
            for i in range(6):
                ch.link(nc.gpsimd.tensor_tensor(join[:, i, :], join[:, i + 1, :], join[:, i, :], ALU.subtract))
            ch.link(nc.gpsimd.memset(halves[:], 0.5))
            ch.link(nc.gpsimd.memset(reset[:], 1.0))
            ch.link(nc.gpsimd.memset(reset[:].rearrange("p (c t) -> p c t", t=CK)[:, :, 0:1], 0.0))
            pool.sem_inc(made, 1)
            for s in (o_ev, z_ev, u_ev, osum_done, o_out, fo_out):
                pool.sem_inc(s, 1)

            def c3(t):
                return t.rearrange("p (c t) -> p c t", t=CK)

            def front(u, first=False):
                pool.wait_ge(cs_done, u + 1)
                if not first:
                    pool.wait_ge(ec_done, u)
                    pool.wait_ge(pad_done, u)
                nc.gpsimd.tensor_tensor(hc[:], c3(cs[:])[:, :, CK - 1], halves[:], ALU.mult).then_inc(pq_done, 1)
                pool.wait_ge(pq_done, 3 * u + 1)
                nc.gpsimd.tensor_tensor(c3(pq[:]), c3(cs[:]), hc[:].unsqueeze(2).to_broadcast([P, NCK, CK]), ALU.subtract).then_inc(pq_done, 1)
                pool.wait_ge(pq_done, 3 * u + 2)
                nc.gpsimd.tensor_tensor(qq[:], pq[:], sg[:], ALU.subtract).then_inc(pq_done, 1)
                nc.gpsimd.tensor_tensor(bb[:], kk[:], ar[:], ALU.mult)
                nc.gpsimd.tensor_scalar(kd[:], ar[:], pp[:, 1:2], pp[:, 9:10], ALU.mult, ALU.add).then_inc(bk_done, 1)
                pool.wait_ge(bk_done, 2 * u + 1)
                nc.gpsimd.tensor_tensor(kd[:], kd[:], kt[:], ALU.mult).then_inc(bk_done, 1)

            def period(p, d, first, last):
                u = 2 * p + d
                if d and not last:
                    pool.wait_ge(rb_done, u + 1)
                    pool.wait_ge(pad_done, u + 1)
                    pool.wait_ge(vpad_done, p + 1)
                    pool.sem_inc(loads_free, 1)
                for b, (c0, c1) in enumerate(BATCH):
                    pool.wait_ge(dve_ev, u * ND + c1)
                    nc.gpsimd.tensor_tensor(tt[:, d, c0:c1], sc[:, d, c0:c1, 0, 0:P], join[:, 0:1, :].to_broadcast([P, c1 - c0, P]), ALU.mult).then_inc(tinit, 1)
                    pool.wait_ge(tinit, 6 * u + 2 * b + 1)
                    nc.gpsimd.tensor_tensor(tt[:, d, c0:c1], tt[:, d, c0:c1], ident[:].unsqueeze(1).to_broadcast([P, c1 - c0, P]), ALU.add).then_inc(tinit, 1)
                if not last:
                    front(u + 1)
                    pool.wait_ge(ex_done, u + 2)
                    if not first:
                        pool.wait_ge(z_done, NCK * u)
                    nc.gpsimd.tensor_tensor(rbar[:, 1 - d, :], rt[:], e_in[:], ALU.mult).then_inc(rb_done, 1)
                if d == 0 and not first:
                    add_directions(p - 1)

            def add_directions(p):
                pool.wait_ge(o_ev, (2 * p + 2) * NCK + 1)
                pool.wait_ge(o_out, 16 * p + 1)
                nc.gpsimd.tensor_tensor(osum[:], of[:, 0, :], of[:, 1, :], ALU.add).then_inc(osum_done, 1)

            front(0, first=True)
            pool.wait_ge(ex_done, 1)
            nc.gpsimd.tensor_tensor(rbar[:, 0, :], rt[:], e_in[:], ALU.mult).then_inc(rb_done, 1)
            periods(pool, period)
            add_directions(NPAIR - 1)

        def evacuated(n):
            return sum(on_act[m] == on_act[n] for m in range(n))

        @block.tensor
        def _(pe):
            pe.wait_ge(once_in, 48)
            pe.wait_ge(made, 2)
            pe.wait_ge(xwa_ready, 1)

            def front_job(kind, d, bank):
                if kind in ("w", "a"):
                    return pe.matmul(bank, (w2p if kind == "w" else a2p)[:, d, :], xwa[:, TP:T], start=True, stop=True)
                pe.matmul(bank[:, 0:TP], w2p[:, d, :], xwa[:, 0:TP], start=True, stop=True)
                pe.matmul(bank[:, TP:2 * TP], a2p[:, d, :], xwa[:, 0:TP], start=True, stop=True)
                return pe.transpose(bank[:, 2 * P:3 * P], sin[:, d, :], ident[:])

            def run_job(n, p, d, first, last):
                u = 2 * p + d
                kind, b = plan[n][0:2]
                bank = rot[:, n % R]
                reads = []
                if kind in ("x", "dt", "dtt"):
                    lv = plan[n][2]
                    if kind == "x":
                        reads = [("ti", b) if lv == 0 else ("dt", b, lv - 1)]
                    elif kind == "dt" or lv == len(LEVELS) - 1:
                        reads = [("x", b, lv)]
                for a, sem_, per, more in ((True, act_ev, NA, FRONT), (False, dve_ev, ND, 0)):
                    counts = [evacuated(m) + 1 for m in [index[r] for r in reads] + ([n - R] if n >= R else []) if on_act[m] == a]
                    if counts:
                        pe.wait_ge(sem_, u * per + more + max(counts))
                    elif n < R and first and a:
                        pe.wait_ge(act_ev, FRONT)
                    elif n < R and not first and on_act[n - R + NJ] == a:
                        pe.wait_ge(sem_, (u - 1) * per + more + evacuated(n - R + NJ) + 1)
                if kind in ("w", "a", "wa"):
                    if kind == "w" and d and not last:
                        pe.wait_ge(loads, (p + 2) * NLOAD)
                    mm = front_job(kind, 1 - d, bank)
                elif kind == "vt":
                    pe.wait_ge(vpad_done, p + 1)
                    for i, c in enumerate(range(*BATCH[b])):
                        mm = pe.transpose(bank[:, i * P:(i + 1) * P], vpad[:, c].rearrange("p h t -> p (h t)"), ident[:])
                elif kind == "bk":
                    pe.wait_ge(pad_done, u + 1)
                    for i in range(4):
                        m = 4 * b + i
                        mm = pe.transpose(bank[:, i * P:(i + 1) * P], bkpad[:, m // NCK, m % NCK].rearrange("p h t -> p (h t)"), ident[:])
                elif kind == "sc":
                    pe.wait_ge(rb_done, u + 1)
                    for i in range(2):
                        lhs = bkpad[:, i, b].rearrange("p h t -> p (h t)")
                        pe.matmul(bank[:, i * 192:i * 192 + P], lhs, apad[:, d, b].rearrange("p h t -> p (h t)"), start=True, stop=True)
                        mm = pe.matmul(bank[:, i * 192 + P:(i + 1) * 192], lhs, rbar[:, d, b * CK:(b + 1) * CK], start=True, stop=True)
                elif kind == "ti":
                    pe.wait_ge(tinit, 6 * u + 2 * b + 2)
                    for i, c in enumerate(range(*BATCH[b])):
                        mm = pe.transpose(bank[:, i * P:(i + 1) * P], tt[:, d, c, :], ident[:])
                else:
                    for i, c in enumerate(range(*BATCH[b])):
                        lhs, rhs = {"x": (sc[:, d, c, 0, 0:P], tm[:, c, :]), "dt": (tt[:, d, c, :], xm[:, c, :]),
                                    "dtt": (xm[:, c, :], tt[:, d, c, :])}[kind]
                        mm = pe.matmul(bank[:, i * P:(i + 1) * P], lhs, rhs, start=True, stop=True)
                mm.then_inc(job, 1)

            def stage(i, s, u, d):
                c = ORDER[d][i]
                q = u * NCK + i
                if s == "pw":
                    if i == 0:
                        pe.wait_ge(dve_ev, (u + 1) * ND)
                    pe.wait_ge(z_ev, q + 1)
                    pe.wait_ge(o_ev, q + 1)
                    pe.wait_ge(u_ev, q + 1)
                    if i == NCP:
                        pe.wait_ge(fs_done, u + 1)
                        pe.transpose(wu[:, 2 * P:3 * P], fs[:], ident[:])
                    pe.matmul(zo[:, 0:P], bktok[:, d, NCK + c, :], vtok[:, d, c, :], start=True, stop=False, skip_group_check=True)
                    pe.matmul(zo[:, P:P + CK], vtok[:, d, c, :], sc[:, d, c, 1, P:192], start=False, stop=False, skip_group_check=True)
                    pe.matmul(wu[:, 0:P], sc[:, d, c, 1, 0:P], vtok[:, d, c, :], start=True, stop=False)
                    pe.wait_ge(s_ready, q + 1)
                    pe.matmul(wu[:, 0:P], apad[:, d, c].rearrange("p h t -> p (h t)"), st[:], start=False, stop=True).then_inc(w_done, 1)
                    pe.matmul(zo[:, P:P + CK], st[:], rbar[:, d, c * CK:(c + 1) * CK], start=False, stop=False, skip_group_check=True)
                elif s == "u":
                    pe.wait_ge(w_ev, q + 1)
                    pe.matmul(wu[:, P:2 * P], tt[:, d, c, :], wsb[:], start=True, stop=True).then_inc(u_done, 1)
                else:
                    pe.wait_ge(u_ev, q + 2)
                    pe.matmul(zo[:, 0:P], bktok[:, d, c, :], usb[:], start=False, stop=True, skip_group_check=True)
                    pe.matmul(zo[:, P:P + CK], usb[:], sc[:, d, c, 0, P:192], start=False, stop=True, skip_group_check=True).then_inc(z_done, 1)

            def period(p, d, first, last):
                for item in timeline:
                    if item[0] == "job":
                        run_job(item[1], p, d, first, last)
                    elif not first:
                        stage(item[1], item[2], 2 * p + d - 1, 1 - d)

            pe.wait_ge(loads, NLOAD)
            for n, kind in enumerate(("w", "a", "wa")):
                front_job(kind, 0, rot[:, n]).then_inc(job, 1)
            periods(pe, period)
            for i, s in stages:
                stage(i, s, 2 * NPAIR - 1, 1)

        @block.scalar
        def _(act):
            act.wait_ge(once_in, 48)
            nc.scalar.activation(xwa[0:64, :], xwa[0:64, :], ACT.Tanh).then_inc(xwa_ready, 1)

            def take_front(kind, d, bank):
                if kind == "w":
                    return nc.scalar.activation(sg[:, TP:T], bank, ACT.Sigmoid, bias=pp[:, 5 + d:6 + d])
                if kind == "a":
                    return nc.scalar.activation(ar[:, TP:T], bank, ACT.Sigmoid, bias=pp[:, 7 + d:8 + d])
                nc.scalar.activation(sg[:, 0:TP], bank[:, 0:TP], ACT.Sigmoid, bias=pp[:, 5 + d:6 + d])
                nc.scalar.activation(ar[:, 0:TP], bank[:, TP:2 * TP], ACT.Sigmoid, bias=pp[:, 7 + d:8 + d])
                return nc.scalar.copy(s0[:, d, :], bank[:, 2 * P:3 * P])

            def empty(n, p, d, first, last):
                u = 2 * p + d
                kind, b = plan[n][0:2]
                bank = rot[:, n % R]
                act.wait_ge(job, FRONT + u * NJ + n + 1)
                if kind in ("w", "a", "wa"):
                    if kind == "w":
                        act.wait_ge(pq_done, 3 * u + 3)
                        act.wait_ge(bk_done, 2 * u + 2)
                        act.wait_ge(par_ready, 2 * p + (2 if last else 2 * d + 2))
                    if kind == "wa" and not first:
                        act.wait_ge(s_ready, (u - 1) * NCK + NCP + 1)
                    a = take_front(kind, 1 - d, bank)
                elif kind == "vt":
                    c0, c1 = BATCH[b]
                    a = nc.scalar.copy(vtok[:, d, c0:c1, :].rearrange("p c k -> p (c k)"), bank[:, 0:(c1 - c0) * P])
                elif kind == "bk":
                    a = nc.scalar.copy(bktok[:, d, 4 * b:4 * b + 4, :].rearrange("p c k -> p (c k)"), bank)
                elif kind == "ti":
                    c0, c1 = BATCH[b]
                    a = nc.scalar.copy(tm[:, c0:c1, :].rearrange("p c k -> p (c k)"), bank[:, 0:(c1 - c0) * P])
                a.then_inc(act_ev, 1)

            def exponentials(u, d, first=False):
                act.wait_ge(pq_done, 3 * u + 3)
                if not first:
                    act.wait_ge(pad_done, u)
                    act.wait_ge(rb_done, u)
                s = LAM if d else -LAM
                nc.scalar.activation(e_in[:], (qq if d else pq)[:], ACT.Exp, scale=s)
                nc.scalar.activation(e_ex[:], (pq if d else qq)[:], ACT.Exp, scale=s)
                nc.scalar.activation(e_inv[:], (qq if d else pq)[:], ACT.Exp, scale=-s).then_inc(ex_done, 1)

            def chunk_decays(d):
                nc.scalar.activation(ec[:, d, :], hc[:], ACT.Exp, scale=-LAM).then_inc(ec_done, 1)

            def pad_values(p):
                act.wait_ge(loads, (p + 1) * NLOAD)
                nc.scalar.copy(vpad[0:64, :, 0, :], vt[0:64, :].rearrange("p (c t) -> p c t", t=CK))
                nc.scalar.copy(vpad[64:P, :, 1, :], vt[64:P, :].rearrange("p (c t) -> p c t", t=CK)).then_inc(vpad_done, 1)

            def stage(i, s, u, d, p):
                c = ORDER[d][i]
                q = u * NCK + i
                if s == "pw":
                    act.wait_ge(w_done, q + 1)
                    a = nc.scalar.copy(wsb[:], wu[:, 0:P])
                    if i == NCP:
                        act.wait_ge(fo_out, 64 * p + 1)
                        a = nc.scalar.copy(fo[:, d, :], wu[:, 2 * P:3 * P])
                    a.then_inc(w_ev, 1)
                elif s == "u":
                    act.wait_ge(u_done, q + 1)
                    nc.scalar.copy(usb[:], wu[:, P:2 * P]).then_inc(u_ev, 1)
                else:
                    act.wait_ge(z_done, q + 1)
                    act.wait_ge(z_ev, q + 2)
                    if i == 0 and d == 0:
                        act.wait_ge(osum_done, p + 1)
                    nc.scalar.copy(of[:, d, c * CK:(c + 1) * CK], zo[:, P:P + CK]).then_inc(o_ev, 1)

            def period(p, d, first, last):
                if first:
                    chunk_decays(d)
                for item in timeline:
                    if item[0] == "job":
                        if on_act[item[1]]:
                            empty(item[1], p, d, first, last)
                        if item == EXP_AT and not last:
                            exponentials(2 * p + d + 1, 1 - d)
                        if item == VPAD_AT and d and not last:
                            pad_values(p + 1)
                    elif not first:
                        stage(item[1], item[2], 2 * p + d - 1, 1 - d, p if d else p - 1)
                        if item[1:] == (0, "pw"):
                            chunk_decays(d)

            pad_values(0)
            act.wait_ge(par_ready, 2)
            for n, kind in enumerate(("w", "a", "wa")):
                act.wait_ge(job, n + 1)
                take_front(kind, 0, rot[:, n]).then_inc(act_ev, 1)
            exponentials(0, 0, first=True)
            periods(act, period)
            for i, s in stages:
                stage(i, s, 2 * NPAIR - 1, 1, NPAIR - 1)

        @block.vector
        def _(dve):
            dve.wait_ge(once_in, 48)
            dve.wait_ge(made, 2)
            p9 = par[:].rearrange("p (v k) -> p v k", k=NPAIR)

            def empty(n, p, d):
                u = 2 * p + d
                kind, b = plan[n][0:2]
                bank = rot[:, n % R]
                dve.wait_ge(job, FRONT + u * NJ + n + 1)
                if kind == "sc":
                    a = nc.vector.tensor_tensor(sc[:, d, b], bank[:, 0:384].rearrange("p (i n) -> p i n", i=2),
                                                mask[:, d:d + 1, :].to_broadcast([P, 2, 192]), ALU.mult)
                else:
                    lv = plan[n][2]
                    c0, c1 = BATCH[b]
                    src = bank[:, 0:(c1 - c0) * P].rearrange("p (c k) -> p c k", k=P)
                    if kind == "x":
                        a = nc.vector.tensor_tensor(xm[:, c0:c1, :], src, join[:, lv + 1:lv + 2, :].to_broadcast([P, c1 - c0, P]), ALU.mult)
                    else:
                        t = tm[:, c0:c1, :] if kind == "dt" else tt[:, d, c0:c1, :]
                        a = nc.vector.tensor_tensor(t, src, t, ALU.add)
                a.then_inc(dve_ev, 1)

            def scan(act_count):
                dve.wait_ge(act_ev, act_count)
                nc.vector.tensor_tensor_scan(cs[:], reset[:], sg[:], 0.0, ALU.mult, ALU.add).then_inc(cs_done, 1)

            def padded(u, d, first=False, second=False):
                dve.wait_ge(ex_done, u + 1)
                dve.wait_ge(bk_done, 2 * u + 2)
                if not first:
                    dve.wait_ge(job, FRONT + (u - 1) * NJ + index[("sc", NCK - 1)] + 1)
                    if not second:
                        dve.wait_ge(z_done, NCK * (u - 1))
                for hh in range(2):
                    rows = slice(hh * DH, (hh + 1) * DH)

                    def c3(t):
                        return t[rows, :].rearrange("p (c t) -> p c t", t=CK)
                    nc.vector.scalar_tensor_tensor(apad[rows, d, :, hh, :], c3(kk), -1.0, c3(e_ex), ALU.mult, ALU.mult)
                    nc.vector.tensor_tensor(bkpad[rows, 0, :, hh, :], c3(bb), c3(e_inv), ALU.mult)
                    a = nc.vector.tensor_tensor(bkpad[rows, 1, :, hh, :], c3(kd), c3(e_inv), ALU.mult)
                a.then_inc(pad_done, 1)

            def vectors(p):
                nc.vector.tensor_copy(pp[:, 0:9], p9[:, :, bass.ds(p, 1)].rearrange("p v o -> p (v o)")).then_inc(par_ready, 1)
                dve.wait_ge(par_ready, 2 * p + 1)
                nc.vector.tensor_scalar(pp[:, 9:10], pp[:, 1:2], -1.0, 1.0, ALU.mult, ALU.add).then_inc(par_ready, 1)

            def stage(i, s, u, d):
                c = ORDER[d][i]
                q = u * NCK + i
                nx = ORDER[d][i + 1] if i + 1 < NCK else None
                if i == 0 and s == "pw":
                    nc.vector.memset(st[:], 0.0).then_inc(s_ready, 1)
                    dve.wait_ge(ec_done, u + 1)
                if s != "z":
                    return
                dve.wait_ge(z_done, q + 1)
                nc.vector.tensor_tensor(tmp[:], zo[:, 0:P], st[:], ALU.add).then_inc(z_ev, 1)
                dve.wait_ge(z_ev, q + 2)
                if i == NCP - 1:
                    nc.vector.tensor_scalar(st[:], s0[:, d, :], ec[:, d, nx:nx + 1], None, ALU.mult).then_inc(s_ready, 1)
                    nc.vector.tensor_scalar(fs[:], tmp[:], ec[:, d, c:c + 1], None, ALU.mult).then_inc(fs_done, 1)
                elif nx is not None:
                    nc.vector.tensor_scalar(st[:], tmp[:], ec[:, d, c:c + 1], ec[:, d, nx:nx + 1],
                                            ALU.mult, ALU.mult).then_inc(s_ready, 1)

            def period(p, d, first, last):
                u = 2 * p + d
                if d and not last:
                    dve.wait_ge(bk_done, 2 * u + 2)
                    vectors(p + 1)
                for item in timeline:
                    if item[0] == "job":
                        if not on_act[item[1]]:
                            empty(item[1], p, d)
                        if item == SCAN_AT and not last:
                            scan(FRONT + u * NA + evacuated(index[("wa", 0)]) + 1)
                        if item == PAD_AT and not last:
                            padded(u + 1, 1 - d, second=first)
                    elif not first:
                        stage(item[1], item[2], u - 1, 1 - d)

            vectors(0)
            scan(FRONT)
            padded(0, 0, first=True)
            periods(dve, period)
            for i, s in stages:
                stage(i, s, 2 * NPAIR - 1, 1)


def load_w_out(sp, w_out, ring, w_got, b):
    WB = ring.shape[3]
    sp.dma_start(ring[:, b % 2], w_out[0, :, b * WB:(b + 1) * WB].rearrange("(k p) n -> p k n", p=P)).then_inc(w_got[b % 2], 16)


def block_rwkv_output(nc, z_d, o_raw_d, par_d, g2, w_out, w_ring, w_got, o_d):
    with ExitStack() as ctx:
        def sb(name, shape):
            return ctx.enter_context(nc.sbuf_tensor("ro_" + name, shape, F32))

        def sem(name):
            return nc.alloc_semaphore("ro_" + name)

        par, g2s, sx = sb("par", [P, 72]), sb("g2s", [P, RW]), sb("sx", [P, T])
        mean_w, sum_w, eps = sb("mean_w", [P, P]), sb("sum_w", [P, P]), sb("eps", [P, 1])
        o, rt, kt, vt = (sb(n, [P, 2, T]) for n in ("o", "r", "k", "v"))
        sq, rs, bo = (sb(n, [P, 2, T]) for n in ("sq", "rs", "bo"))
        ps = [ctx.enter_context(nc.psum_tensor(f"ro_{n}", [P, 1024], F32)) for n in ("mean", "var", "bonus", "gate")]
        once, made, sx_done, ch = sem("once"), sem("made"), sem("sx"), sem("ch")
        loads = (sem("load0"), sem("load1"))
        meaned, centred, squared, vard, rsd, rk_done, bonused, done, out = (sem(n) for n in
            ("meaned", "centred", "squared", "vard", "rsd", "rk", "bonused", "done", "out"))
        block = ctx.enter_context(nc.Block())

        @block.sync
        def _(sp):
            sp.dma_start(par[:], par_d).then_inc(once, 16)
            sp.dma_start(g2s[:], g2[0]).then_inc(once, 16)
            sp.dma_start(sx[:], z_d[ZX + 1]).then_inc(once, 16)
            for p in range(NPAIR):
                if p in (2, 3):
                    load_w_out(sp, w_out, w_ring, w_got, p - 2)
                if p >= 2:
                    sp.wait_ge(out, 16 * (p - 1))
                sp.dma_start(o[:, p % 2, :], o_raw_d[p]).then_inc(loads[p % 2], 16)
                for dst, row in ((rt, ZR), (kt, ZKC), (vt, ZV)):
                    sp.dma_start(dst[:, p % 2, :], z_d[row + p]).then_inc(loads[p % 2], 16)
                if p >= 1:
                    sp.wait_ge(done, p)
                    sp.dma_start(o_d[8 + p - 1], o[:, (p - 1) % 2, :]).then_inc(out, 16)
            sp.wait_ge(done, NPAIR)
            sp.dma_start(o_d[8 + NPAIR - 1], o[:, (NPAIR - 1) % 2, :]).then_inc(out, 16)
            sp.wait_ge(out, 16 * NPAIR)

        @block.tensor
        def _(pe):
            pe.wait_ge(made, 1)
            pe.wait_ge(sx_done, 1)

            def both(dst, lhs, rhs):
                pe.matmul(dst[:, 0:512], lhs, rhs[:, 0:512], start=True, stop=True)
                return pe.matmul(dst[:, 512:T], lhs, rhs[:, 512:T], start=True, stop=True)

            for p in range(NPAIR):
                s = p % 2
                pe.wait_ge(loads[s], 64 * (p // 2 + 1))
                if p:
                    pe.wait_ge(done, p)
                both(ps[0], mean_w[:], o[:, s, :]).then_inc(meaned, 1)
                pe.wait_ge(rk_done, p + 1)
                both(ps[2], sum_w[:], bo[:, s, :])
                both(ps[3], g2s[:, p * P:(p + 1) * P], sx[:]).then_inc(bonused, 1)
                pe.wait_ge(squared, p + 1)
                both(ps[1], mean_w[:], sq[:, s, :]).then_inc(vard, 1)

        @block.scalar
        def _(act):
            act.wait_ge(once, 48)
            nc.scalar.activation(sx[:], sx[:], ACT.Sigmoid).then_inc(sx_done, 1)
            act.wait_ge(made, 1)
            for p in range(NPAIR):
                s = p % 2
                act.wait_ge(centred, p + 1)
                nc.scalar.activation(sq[:, s, :], o[:, s, :], ACT.Square).then_inc(squared, 1)
                act.wait_ge(vard, p + 1)
                nc.scalar.activation(rs[:, s, :], ps[1][:, 0:T], ACT.Ln, bias=eps[:]).then_inc(ch, 1)
                act.wait_ge(ch, p + 1)
                nc.scalar.activation(rs[:, s, :], rs[:, s, :], ACT.Exp, scale=-0.5).then_inc(rsd, 1)

        @block.vector
        def _(dve):
            nc.vector.memset(eps[:], GN_EPS)
            for w, v in ((mean_w, 1.0 / DH), (sum_w, 1.0)):
                nc.vector.memset(w[0:DH, DH:P], 0.0)
                nc.vector.memset(w[DH:P, 0:DH], 0.0)
                nc.vector.memset(w[0:DH, 0:DH], v)
                last = nc.vector.memset(w[DH:P, DH:P], v)
            last.then_inc(made, 1)
            dve.wait_ge(once, 48)
            link = Chain(dve, nc.alloc_semaphore("ro_dch")).link
            for p in range(NPAIR):
                s = p % 2
                dve.wait_ge(loads[s], 64 * (p // 2 + 1))
                nc.vector.scalar_tensor_tensor(bo[:, s, :], rt[:, s, :], par[:, 16 + p:17 + p], kt[:, s, :], ALU.mult, ALU.mult).then_inc(rk_done, 1)
                dve.wait_ge(meaned, p + 1)
                nc.vector.tensor_tensor(o[:, s, :], o[:, s, :], ps[0][:, 0:T], ALU.subtract).then_inc(centred, 1)
                dve.wait_ge(bonused, p + 1)
                link(nc.vector.tensor_tensor(vt[:, s, :], ps[2][:, 0:T], vt[:, s, :], ALU.mult))
                dve.wait_ge(rsd, p + 1)
                link(nc.vector.tensor_tensor(o[:, s, :], o[:, s, :], rs[:, s, :], ALU.mult))
                link(nc.vector.tensor_scalar(o[:, s, :], o[:, s, :], par[:, 24 + p:25 + p], par[:, 32 + p:33 + p], ALU.mult, ALU.add))
                link(nc.vector.tensor_tensor(o[:, s, :], o[:, s, :], vt[:, s, :], ALU.add))
                nc.vector.tensor_tensor(o[:, s, :], o[:, s, :], ps[3][:, 0:T], ALU.mult).then_inc(done, 1)


def block_output_projection(nc, o_d, w_out, ring, w_got, mod_d, g_post_mix, g_pre_ffn, consts, mixed_d):
    WB = ring.shape[3]
    with ExitStack() as ctx:
        def sb(name, shape):
            return ctx.enter_context(nc.sbuf_tensor("op_" + name, shape, F32))

        def sem(name):
            return nc.alloc_semaphore("op_" + name)

        ot, stage = sb("ot", [P, KD, T]), sb("stage", [P, 2, NT, WB])
        gains = sb("gains", [P, D])
        ps = ctx.enter_context(nc.psum_tensor("op_ps", [P, 8, 512], F32))
        o_in, mm_done, evd, used = sem("oin"), sem("mm"), sem("ev"), sem("used")
        out = (sem("out0"), sem("out1"))
        rows_in = [sem(f"rowsin{i}") for i in range(3)]
        gain_in, gained = sem("gainin"), sem("gained")
        block = ctx.enter_context(nc.Block())

        @block.sync
        def _(sp):
            sp.dma_start(ot[:], o_d.rearrange("k p t -> p k t")).then_inc(o_in, 16)
            for b in range(2, D // WB):
                sp.wait_ge(mm_done, NT * (b - 1))
                load_w_out(sp, w_out, ring, w_got, b)
            for b in range(D // WB):
                sp.wait_ge(evd, NT * (b + 1))
                sp.dma_start(mixed_d[:, :, b * WB:(b + 1) * WB].rearrange("t p n -> p t n"), stage[:, b % 2]).then_inc(out[b % 2], 16)
            sp.wait_ge(out[0], 32)
            sp.wait_ge(out[1], 32)

        @block.tensor
        def _(pe):
            pe.wait_ge(o_in, 16)
            for b in range(D // WB):
                pe.wait_ge(w_got[b % 2], 16 * (b // 2 + 1))
                for t in range(NT):
                    n = b * NT + t
                    if n >= 8:
                        pe.wait_ge(evd, n - 7)
                    for k in range(KD):
                        mm = pe.matmul(ps[:, n % 8, :], ot[:, k, t * P:(t + 1) * P], ring[:, b % 2, k, :], start=(k == 0), stop=(k == KD - 1))
                    mm.then_inc(mm_done, 1)

        @block.gpsimd
        def _(pool):
            for i, (g, part) in enumerate(((g_post_mix, 2), (g_pre_ffn, 4), (None, 3))):
                for cnd in range(2):
                    pool.dma_start(consts[:, cnd, i, :], bcast_rows(mod_d, cnd * 6 * D + part * D, D)).then_inc(rows_in[i], 16)
                if g is not None:
                    if i:
                        pool.wait_ge(gained, 2 * i)
                    pool.dma_start(gains[:], bcast_rows(g, 0, D)).then_inc(gain_in, 16)
            pool.wait_ge(rows_in[2], 32)

        @block.vector
        def _(dve):
            for i in range(2):
                dve.wait_ge(gain_in, 16 * (i + 1))
                dve.wait_ge(rows_in[i], 32)
                for cnd in range(2):
                    c = consts[:, cnd, i, :]
                    if i == 0:
                        nc.vector.tensor_tensor(c, c, gains[:], ALU.mult).then_inc(gained, 1)
                    else:
                        nc.vector.scalar_tensor_tensor(c, c, 1.0, gains[:], ALU.add, ALU.mult).then_inc(gained, 1)

        @block.scalar
        def _(act):
            for b in range(D // WB):
                for t in range(NT):
                    n = b * NT + t
                    act.wait_ge(mm_done, n + 1)
                    if b >= 2 and t == 0:
                        act.wait_ge(out[b % 2], 16)
                    nc.scalar.copy(stage[:, b % 2, t, :], ps[:, n % 8, :]).then_inc(evd, 1)


def block_middle(nc, x_prompt, x_sample, mixed_d, consts, w_router, ident_d, x1_d, h2_d, aff_d, afft_d):
    with ExitStack() as ctx:
        def sb(name, shape):
            return ctx.enter_context(nc.sbuf_tensor("mi_" + name, shape, F32))

        def sem(name):
            return nc.alloc_semaphore("mi_" + name)

        ident, wr, eps = sb("ident", [P, P]), sb("wr", [P, KD, NE]), sb("eps", [P, 1])
        g1, a2, sh2 = (consts[:, :, i, :] for i in range(3))
        x, mx = sb("x", [P, 2, D]), sb("mx", [P, 2, D])
        junk, h2t = sb("junk", [P, D]), sb("h2t", [P, KD, P])
        st = sb("st", [P, NT, 6])
        af, afs = sb("af", [P, NT, NE]), sb("afs", [P, NT, 4])
        aft = sb("aft", [NE, T])
        ps = ctx.enter_context(nc.psum_tensor("mi_ps", [P, 8, 512], F32))
        once, made, rows_ready = sem("once"), sem("made"), sem("rows")
        loads = (sem("load0"), sem("load1"))
        ss1, sd1, x1r, ss2, sd2, h2r, turned, h2te, routed, mxd, expd, affd, atd, ate = (sem(n) for n in
            ("ss1", "sd1", "x1", "ss2", "sd2", "h2", "turned", "h2te", "routed", "mxd", "expd", "affd", "atd", "ate"))
        x1_out, h2_out, out = sem("x1out"), sem("h2out"), sem("out")
        block = ctx.enter_context(nc.Block())

        def store(sp, t):
            sp.wait_ge(x1r, t + 1)
            sp.dma_start(x1_d[t], x[:, t % 2, :]).then_inc(x1_out, 16)
            sp.wait_ge(h2r, t + 1)
            sp.dma_start(h2_d[t], mx[:, t % 2, :]).then_inc(h2_out, 16)

        @block.sync
        def _(sp):
            sp.dma_start(ident[:], ident_d).then_inc(once, 16)
            sp.dma_start(wr[:], w_router[0].rearrange("(k p) e -> p k e", p=P)).then_inc(once, 16)
            for t in range(NT):
                s = t % 2
                if t >= 2:
                    sp.wait_ge(x1_out, 16 * (t - 1))
                    sp.wait_ge(h2_out, 16 * (t - 1))
                    sp.wait_ge(turned, 4 * (t - 1))
                sp.dma_start(x[:, s, :], x_prompt[0] if t == 0 else x_sample[0, (t - 1) * P:t * P, :]).then_inc(loads[s], 16)
                sp.dma_start(mx[:, s, :], mixed_d[t]).then_inc(loads[s], 16)
                if t >= 1:
                    store(sp, t - 1)
            store(sp, NT - 1)
            sp.wait_ge(affd, NT)
            sp.dma_start(aff_d, af[:]).then_inc(out, 16)
            sp.wait_ge(ate, 2)
            sp.dma_start(afft_d, aft[:]).then_inc(out, 16)
            sp.wait_ge(x1_out, 16 * NT)
            sp.wait_ge(h2_out, 16 * NT)
            sp.wait_ge(out, 32)

        @block.tensor
        def _(pe):
            pe.wait_ge(once, 32)
            for t in range(NT):
                pe.wait_ge(h2r, t + 1)
                for q in range(4):
                    if t:
                        pe.wait_ge(h2te, 4 * (t - 1) + q + 1)
                    for j in range(4):
                        k = 4 * q + j
                        tr = pe.transpose(ps[:, q, j * P:(j + 1) * P], mx[:, t % 2, k * P:(k + 1) * P], ident[:])
                    tr.then_inc(turned, 1)
                pe.wait_ge(h2te, 4 * t + 4)
                if t >= 2:
                    pe.wait_ge(expd, t - 1)
                for k in range(KD):
                    mm = pe.matmul(ps[:, 4 + t % 2, 0:NE], h2t[:, k, :], wr[:, k, :], start=(k == 0), stop=(k == KD - 1))
                mm.then_inc(routed, 1)
            for t in range(NT):
                pe.wait_ge(affd, t + 1)
                dst = ps[0:NE, 6, (t - 1) * P:t * P] if t else ps[0:NE, 7, 0:P]
                pe.transpose(dst, af[:, t, :], ident[:]).then_inc(atd, 1)

        @block.scalar
        def _(act):
            act.wait_ge(made, 1)
            for t in range(NT):
                s = t % 2
                act.wait_ge(loads[s], 32 * (t // 2 + 1))
                nc.scalar.activation(junk[:], mx[:, s, :], ACT.Square, accum_out=st[:, t, 0:1]).then_inc(ss1, 1)
                act.wait_ge(ss1, 2 * t + 1)
                nc.scalar.activation(st[:, t, 1:2], st[:, t, 0:1], ACT.Sqrt, scale=1.0 / D, bias=eps[:]).then_inc(ss1, 1)
                act.wait_ge(x1r, t + 1)
                nc.scalar.activation(junk[:], x[:, s, :], ACT.Square, accum_out=st[:, t, 3:4]).then_inc(ss2, 1)
                act.wait_ge(ss2, 2 * t + 1)
                nc.scalar.activation(st[:, t, 4:5], st[:, t, 3:4], ACT.Sqrt, scale=1.0 / D, bias=eps[:]).then_inc(ss2, 1)
                for q in range(4):
                    act.wait_ge(turned, 4 * t + q + 1)
                    if t:
                        act.wait_ge(routed, t)
                    nc.scalar.copy(h2t[:, 4 * q:4 * q + 4, :].rearrange("p k t -> p (k t)"), ps[:, q, :]).then_inc(h2te, 1)
                act.wait_ge(mxd, t + 1)
                nc.scalar.activation(af[:, t, :], ps[:, 4 + t % 2, 0:NE], ACT.Exp, bias=afs[:, t, 1:2], accum_out=afs[:, t, 2:3]).then_inc(expd, 1)

        @block.vector
        def _(dve):
            link = Chain(dve, nc.alloc_semaphore("mi_dch")).link
            nc.vector.memset(eps[:], NORM_EPS).then_inc(made, 1)
            def router(t):
                dve.wait_ge(routed, t + 1)
                link(nc.vector.tensor_reduce(afs[:, t, 0:1], ps[:, 4 + t % 2, 0:NE], AX_X, ALU.max))
                nc.vector.tensor_scalar(afs[:, t, 1:2], afs[:, t, 0:1], -1.0, None, ALU.mult).then_inc(mxd, 1)
                dve.wait_ge(expd, t + 1)
                link(nc.vector.reciprocal(afs[:, t, 3:4], afs[:, t, 2:3]))
                nc.vector.tensor_scalar(af[:, t, :], af[:, t, :], afs[:, t, 3:4], None, ALU.mult).then_inc(affd, 1)

            for t in range(NT):
                s, cnd = t % 2, min(t, 1)
                dve.wait_ge(ss1, 2 * t + 2)
                link(nc.vector.reciprocal(st[:, t, 2:3], st[:, t, 1:2]))
                link(nc.vector.scalar_tensor_tensor(mx[:, s, :], mx[:, s, :], st[:, t, 2:3], g1[:, cnd, :], ALU.mult, ALU.mult))
                nc.vector.tensor_tensor(x[:, s, :], x[:, s, :], mx[:, s, :], ALU.add).then_inc(x1r, 1)
                dve.wait_ge(ss2, 2 * t + 2)
                link(nc.vector.reciprocal(st[:, t, 5:6], st[:, t, 4:5]))
                link(nc.vector.scalar_tensor_tensor(mx[:, s, :], x[:, s, :], st[:, t, 5:6], a2[:, cnd, :], ALU.mult, ALU.mult))
                nc.vector.tensor_tensor(mx[:, s, :], mx[:, s, :], sh2[:, cnd, :], ALU.add).then_inc(h2r, 1)
                router(t)
            dve.wait_ge(atd, 1)
            nc.vector.tensor_copy(aft[:, 0:TP], ps[0:NE, 7, 0:P]).then_inc(ate, 1)
            dve.wait_ge(atd, NT)
            nc.vector.tensor_copy(aft[:, TP:T], ps[0:NE, 6, :]).then_inc(ate, 1)


def load_expert(sp, weights, ring, slot_in, e, r, n, used=None):
    w_gate, w_up, w_down = weights
    slot = n % len(slot_in)
    e = bass.ds(e, 1)
    if r < 16:
        w = w_gate if r % 2 == 0 else w_up
        src = w[0, e, (r // 2) * 256:(r // 2 + 1) * 256, :].rearrange("o (k p) f -> p (o k) f", p=P)
        dst = ring[:, slot, :].rearrange("p (k f) -> p k f", k=2)
    else:
        src = w_down[0, e, (r - 16) * P:(r - 15) * P, :].rearrange("o p f -> p (o f)")
        dst = ring[:, slot, :]
    if used:
        sp.wait_ge(*used)
    sp.dma_start(dst, src).then_inc(slot_in[slot], 16)


def block_select(nc, afft_d, ident_d, h2_d, h2, h2_in, weights, ring, slot_in, slot_d):
    with ExitStack() as ctx:
        def sb(name, shape):
            return ctx.enter_context(nc.sbuf_tensor("se_" + name, shape, F32))

        ident, wk, sel, cum = sb("ident", [P, P]), sb("wk", [NE, T]), sb("sel", [NE, T]), sb("cum", [NE, T])
        zero, top = sb("zero", [NE, T]), sb("top", [NE, 8])
        slot = sb("slot", [P, NT, NE])
        ps = ctx.enter_context(nc.psum_tensor("se_ps", [P, 512], F32))
        once, cumd, turned, done, out = (nc.alloc_semaphore("se_" + n) for n in ("once", "cumd", "turned", "done", "out"))
        block = ctx.enter_context(nc.Block())

        @block.sync
        def _(sp):
            sp.dma_start(ident[:], ident_d).then_inc(once, 16)
            sp.dma_start(wk[:], afft_d).then_inc(once, 16)
            sp.dma_start(h2[:], h2_d.rearrange("t p d -> p t d")).then_inc(h2_in, 16)
            for n in range(len(slot_in)):
                load_expert(sp, weights, ring, slot_in, 0, n, n)
            sp.wait_ge(done, 1)
            sp.dma_start(slot_d, slot[:]).then_inc(out, 16)
            sp.wait_ge(out, 16)

        @block.vector
        def _(dve):
            link = Chain(dve, nc.alloc_semaphore("se_ch")).link
            link(nc.vector.memset(zero[:], 1.0))
            dve.wait_ge(once, 32)
            for t0, t1, cap in ((0, TP, CAPP), (TP, T, CAPS)):
                for _ in range(cap // 8):
                    link(nc.vector.max(top[:], wk[:, t0:t1]))
                    link(nc.vector.match_replace(wk[:, t0:t1], top[:], wk[:, t0:t1], -1.0))
                link(nc.vector.tensor_scalar(sel[:, t0:t1], wk[:, t0:t1], 0.0, None, ALU.is_lt))
                link(nc.vector.tensor_tensor_scan(cum[:, t0:t1], zero[:, t0:t1], sel[:, t0:t1], 0.0, ALU.mult, ALU.add))
            nc.vector.tensor_tensor(cum[:], cum[:], sel[:], ALU.mult).then_inc(cumd, 1)
            dve.wait_ge(turned, 1)
            nc.vector.tensor_copy(slot[:].rearrange("p t e -> p (t e)"), ps[:, 0:NT * NE]).then_inc(done, 1)

        @block.tensor
        def _(pe):
            pe.wait_ge(once, 32)
            pe.wait_ge(cumd, 1)
            for t in range(NT):
                tr = pe.transpose(ps[:, t * NE:(t + 1) * NE], cum[:, t * P:(t + 1) * P], ident[0:NE, 0:NE])
            tr.then_inc(turned, 1)


def block_experts(nc, h2, h2_in, aff_d, slot_d, ident_d, weights, ring, slot_in, ffn_d):
    NG, EG = NE // 4, 4
    RING = len(slot_in)
    PER = 24
    NL = EG * PER
    with ExitStack() as ctx:
        def sb(name, shape):
            return ctx.enter_context(nc.sbuf_tensor("ex_" + name, shape, F32))

        def sem(name):
            return nc.alloc_semaphore("ex_" + name)

        ident = sb("ident", [P, P])
        aff, slot, iota = sb("aff", [P, NT, NE]), sb("slot", [P, NT, NE]), sb("iota", [P, 64])
        xsp = sb("xsp", [P, KD, NE * CAPP])
        xe0, xe1 = sb("xe0", [P, KD, 80]), sb("xe1", [P, KD, P])
        oh = sb("oh", [P, 4, 2, CAPS])
        cg, cgp = sb("cg", [P, 4, EG, CAPS]), sb("cgp", [P, EG, 32])
        cc, ccp = sb("cc", [P, 2, 4, P]), sb("ccp", [P, P])
        hid = sb("hid", [P, DE])
        hidt = sb("hidt", [P, 8, P])
        y, yp = sb("y", [P, 2, D]), sb("yp", [P, D])
        f = sb("f", [P, NT, D])
        ps = ctx.enter_context(nc.psum_tensor("ex_ps", [P, 8, 512], F32))

        once, made, ohp_ready, pg, pg_ev = sem("once"), sem("made"), sem("ohp"), sem("pg"), sem("pgev")
        slot_used = sem("used")
        oh_ready, gathered, xe_act, xe_dve, xe_pool = (sem(n) for n in ("oh", "gath", "xea", "xev", "xep"))
        silu_done, hid_done, turned, ht_act, ht_dve, y_act, y_dve = (sem(n) for n in
            ("silu", "hid", "turned", "hta", "htv", "ya", "yv"))
        cg_ready, cc_turned, cc_ready, comb, added, out = (sem(n) for n in ("cg", "cct", "cc", "comb", "added", "out"))
        block = ctx.enter_context(nc.Block())
        rows = [80, P]

        @block.sync
        def _(sp):
            sp.dma_start(ident[:], ident_d).then_inc(once, 16)
            sp.dma_start(aff[:], aff_d).then_inc(once, 16)
            sp.dma_start(slot[:], slot_d).then_inc(once, 16)

            def load(g, n):
                load_expert(sp, weights, ring, slot_in, 4 * g + n // PER, n % PER, n, used=(slot_used, g * NL + n - RING + 1))

            for n in range(RING, NL):
                load(0, n)
            with sp.Fori(1, NG) as g:
                for n in range(NL):
                    load(g, n)
            sp.wait_ge(added, 36 * NG)
            sp.dma_start(ffn_d.rearrange("t p d -> p t d"), f[:]).then_inc(out, 16)
            sp.wait_ge(out, 16)

        @block.gpsimd
        def _(pool):
            nc.gpsimd.memset(xe1[:], 0.0)
            nc.gpsimd.memset(yp[:], 0.0)
            nc.gpsimd.memset(f[:], 0.0)
            nc.gpsimd.iota(iota[:], pattern=[[1, 64]], base=1, channel_multiplier=0, allow_small_or_imprecise_dtypes=True).then_inc(made, 1)
            pool.wait_ge(made, 1)
            pool.wait_ge(pg_ev, 16)
            with pool.Fori(0, NG) as g:
                for q in range(2):
                    pool.wait_ge(gathered, g * 8 + 4 * q + 4)
                    nc.gpsimd.tensor_copy(xe0[:, :, 64:80], xsp[:, :, bass.ds(g * 64 + 32 * q, CAPP)])
                    nc.gpsimd.tensor_copy(xe1[:, :, 0:16], xsp[:, :, bass.ds(g * 64 + 32 * q + 16, CAPP)]).then_inc(xe_pool, 1)

        @block.tensor
        def _(pe):
            pe.wait_ge(once, 48)
            pe.wait_ge(h2_in, 16)
            pe.wait_ge(ohp_ready, 1)
            for k in range(KD):
                if k >= 8:
                    pe.wait_ge(pg_ev, k - 7)
                pe.matmul(ps[:, k % 8, 0:256], h2[:, 0, k * P:(k + 1) * P], cg[:, 0].rearrange("p e c -> p (e c)"), start=True, stop=True).then_inc(pg, 1)
            pe.wait_ge(pg_ev, 16)
            with pe.Fori(0, NG) as g:
                def slot_ready(n):
                    pe.wait_ge(slot_in[n % RING], g * (16 * NL // RING) + 16 * (n // RING + 1))

                def gather(q):
                    pe.wait_ge(oh_ready, 2 * g + q + 1)
                    for b in range(4):
                        for i in range(4):
                            k = 4 * b + i
                            for t in range(4):
                                mm = pe.matmul(ps[:, 4 + b, i * P:(i + 1) * P], h2[:, 1 + t, k * P:(k + 1) * P],
                                               oh[:, t].rearrange("p e c -> p (e c)"), start=(t == 0), stop=(t == 3))
                        mm.then_inc(gathered, 1)

                def gate_up(j):
                    m = rows[j % 2]
                    xe = (xe0, xe1)[j % 2]
                    if j % 2 == 0:
                        pe.wait_ge(xe_act, 4 * g + j + 2)
                        pe.wait_ge(xe_dve, 4 * g + j + 2)
                        pe.wait_ge(xe_pool, 2 * g + j // 2 + 1)
                    for r in range(16):
                        n = j * PER + r
                        slot_ready(n)
                        for kk in range(2):
                            k = 2 * (r // 2) + kk
                            for h in range(2):
                                mm = pe.matmul(ps[0:m, 2 * (r % 2) + h, :], xe[:, k, 0:m],
                                               ring[:, n % RING, kk * DE + h * 512:kk * DE + (h + 1) * 512],
                                               start=(k == 0), stop=(k == KD - 1))
                        mm.then_inc(slot_used, 1)

                def turn_hidden(j):
                    m = rows[j % 2]
                    for h in range(2):
                        pe.wait_ge(hid_done, 8 * g + 2 * j + h + 1)
                        for i in range(4):
                            tr = pe.transpose(ps[:, h, i * P:i * P + m], hid[0:m, (4 * h + i) * P:(4 * h + i + 1) * P], ident[0:m, 0:m])
                        tr.then_inc(turned, 1)

                def down(j):
                    m = rows[j % 2]
                    for k in range(8):
                        n = j * PER + 16 + k
                        slot_ready(n)
                        if k == 0:
                            pe.wait_ge(ht_act, 4 * g + j + 1)
                        if k == 4:
                            pe.wait_ge(ht_dve, 4 * g + j + 1)
                        for h in range(4):
                            mm = pe.matmul(ps[0:m, 4 + h, :], hidt[:, k, 0:m], ring[:, n % RING, h * 512:(h + 1) * 512],
                                           start=(k == 0), stop=(k == 7))
                        mm.then_inc(slot_used, 1)

                def combine(q):
                    outs = [(1 + t, h) for t in range(4) for h in range(4)] + ([(0, h) for h in range(4)] if q else [])
                    pe.wait_ge(y_act, 4 * g + 2 * q + 2)
                    pe.wait_ge(y_dve, 4 * g + 2 * q + 2)
                    for o, (t, h) in enumerate(outs):
                        if o >= 4:
                            pe.wait_ge(added, 36 * g + 16 * q + o - 3)
                        lhs, rhs = (cc[:, q, t - 1, :], y[:, q, h * 512:(h + 1) * 512]) if t else (ccp[:], yp[:, h * 512:(h + 1) * 512])
                        pe.matmul(ps[:, 4 + o % 4, :], lhs, rhs, start=True, stop=True).then_inc(comb, 1)
                    pe.wait_ge(added, 36 * g + 16 + 20 * q)

                gather(0)
                gate_up(0)
                pe.wait_ge(cg_ready, 2 * g + 2)
                for q in range(2):
                    for t in range(4):
                        pe.transpose(ps[:, 4 + q, t * P:(t + 1) * P], cg[:, t, 2 * q:2 * q + 2].rearrange("p e c -> p (e c)"), ident[:])
                pe.transpose(ps[:, 6, 0:P], cgp[:].rearrange("p e c -> p (e c)"), ident[:]).then_inc(cc_turned, 1)
                turn_hidden(0)
                pe.wait_ge(cc_ready, g + 1)
                down(0)
                gate_up(1)
                pe.wait_ge(y_act, 4 * g + 1)
                pe.wait_ge(y_dve, 4 * g + 1)
                gather(1)
                turn_hidden(1)
                pe.wait_ge(xe_act, 4 * g + 4)
                pe.wait_ge(xe_dve, 4 * g + 4)
                down(1)
                gate_up(2)
                combine(0)
                turn_hidden(2)
                down(2)
                gate_up(3)
                turn_hidden(3)
                pe.wait_ge(y_act, 4 * g + 3)
                pe.wait_ge(y_dve, 4 * g + 3)
                down(3)
                combine(1)

        def rows_of(j):
            if j % 2 == 0:
                return slice(0, 64), slice(64, 80), slice(32 * j, 32 * j + CAPP)
            return slice(64, P), slice(0, 16), slice(32 * j, 32 * j + CAPP)

        def store_rows(copy, j, banks):
            s, pr, dst = rows_of(j)
            for h in banks:
                copy(y[s, j // 2, h * 512:(h + 1) * 512], ps[s, 4 + h, :])
                last = copy(yp[dst, h * 512:(h + 1) * 512], ps[pr, 4 + h, :])
            return last

        @block.scalar
        def _(act):
            act.wait_ge(made, 1)
            for k in range(0, KD, 2):
                act.wait_ge(pg, k + 1)
                if k:
                    act.wait_ge(pg_ev, k)
                nc.scalar.copy(xsp[:, k, :], ps[:, k % 8, 0:256]).then_inc(pg_ev, 1)
            with act.Fori(0, NG) as g:
                def take_gathered(q):
                    for b in (0, 2):
                        act.wait_ge(gathered, 8 * g + 4 * q + b + 1)
                        src = ps[:, 4 + b, :].rearrange("p (k c) -> p k c", c=P)
                        nc.scalar.copy(xe0[:, 4 * b:4 * b + 4, 0:64], src[:, :, 0:64])
                        nc.scalar.copy(xe1[:, 4 * b:4 * b + 4, 64:P], src[:, :, 64:P]).then_inc(xe_act, 1)

                def expert(j):
                    m = rows[j % 2]
                    act.wait_ge(slot_used, g * NL + j * PER + 16)
                    for h in range(2):
                        nc.scalar.activation(hid[0:m, h * 512:(h + 1) * 512], ps[0:m, h, :], ACT.Silu).then_inc(silu_done, 1)
                    if j == 0:
                        act.wait_ge(cc_turned, g + 1)
                        for q in range(2):
                            nc.scalar.copy(cc[:, q].rearrange("p t c -> p (t c)"), ps[:, 4 + q, :])
                        nc.scalar.copy(ccp[:], ps[:, 6, 0:P]).then_inc(cc_ready, 1)
                    if j == 1:
                        take_gathered(1)
                    act.wait_ge(turned, 8 * g + 2 * j + 1)
                    nc.scalar.copy(hidt[:, 0:4, 0:m], ps[:, 0, :].rearrange("p (i c) -> p i c", c=P)[:, :, 0:m]).then_inc(ht_act, 1)
                    act.wait_ge(slot_used, g * NL + (j + 1) * PER)
                    store_rows(nc.scalar.copy, j, (0, 1)).then_inc(y_act, 1)

                take_gathered(0)
                for j in range(EG):
                    expert(j)

        @block.vector
        def _(dve):
            link = Chain(dve, nc.alloc_semaphore("ex_dch")).link
            dve.wait_ge(made, 1)
            dve.wait_ge(once, 48)

            def one_hot(dst, tiles, experts, n):
                nt, ne = dst.shape[1], dst.shape[2]
                for t in range(nt):
                    last = nc.vector.tensor_tensor(dst[:, t], iota[:, 0:n].unsqueeze(1).to_broadcast([P, ne, n]),
                                                   slot[:, tiles + t, experts].unsqueeze(2).to_broadcast([P, ne, n]), ALU.is_equal)
                return last

            one_hot(cg[:, 0].rearrange("p e c -> p (e c)").rearrange("p (o e c) -> p o e c", o=1, c=CAPP), 0, slice(0, NE), CAPP).then_inc(ohp_ready, 1)
            for k in range(1, KD, 2):
                dve.wait_ge(pg, k + 1)
                dve.wait_ge(pg_ev, k)
                nc.vector.tensor_copy(xsp[:, k, :], ps[:, k % 8, 0:256]).then_inc(pg_ev, 1)
            with dve.Fori(0, NG) as g:
                def pair(q):
                    one_hot(oh[:], 1, bass.ds(4 * g + 2 * q, 2), CAPS).then_inc(oh_ready, 1)

                def take_gathered(q):
                    for b in (1, 3):
                        dve.wait_ge(gathered, 8 * g + 4 * q + b + 1)
                        src = ps[:, 4 + b, :].rearrange("p (k c) -> p k c", c=P)
                        nc.vector.tensor_copy(xe0[:, 4 * b:4 * b + 4, 0:64], src[:, :, 0:64])
                        nc.vector.tensor_copy(xe1[:, 4 * b:4 * b + 4, 64:P], src[:, :, 64:P]).then_inc(xe_dve, 1)

                def scatter_matrices():
                    for t in range(4):
                        nc.vector.tensor_tensor(cg[:, t], iota[:].unsqueeze(1).to_broadcast([P, EG, CAPS]),
                                                slot[:, 1 + t, bass.ds(4 * g, EG)].unsqueeze(2).to_broadcast([P, EG, CAPS]), ALU.is_equal)
                    nc.vector.tensor_tensor(cgp[:], iota[:, 0:32].unsqueeze(1).to_broadcast([P, EG, 32]),
                                            slot[:, 0, bass.ds(4 * g, EG)].unsqueeze(2).to_broadcast([P, EG, 32]), ALU.is_equal).then_inc(cg_ready, 1)
                    dve.wait_ge(cg_ready, 2 * g + 1)
                    for t in range(4):
                        nc.vector.tensor_tensor(cg[:, t], cg[:, t], aff[:, 1 + t, bass.ds(4 * g, EG)].unsqueeze(2).to_broadcast([P, EG, CAPS]), ALU.mult)
                    nc.vector.tensor_tensor(cgp[:], cgp[:], aff[:, 0, bass.ds(4 * g, EG)].unsqueeze(2).to_broadcast([P, EG, 32]), ALU.mult).then_inc(cg_ready, 1)

                def hidden(j):
                    m = rows[j % 2]
                    for h in range(2):
                        dve.wait_ge(silu_done, 8 * g + 2 * j + h + 1)
                        cols = slice(h * 512, (h + 1) * 512)
                        nc.vector.tensor_tensor(hid[0:m, cols], ps[0:m, 2 + h, :], hid[0:m, cols], ALU.mult).then_inc(hid_done, 1)

                def outputs(j):
                    m = rows[j % 2]
                    dve.wait_ge(turned, 8 * g + 2 * j + 2)
                    nc.vector.tensor_copy(hidt[:, 4:8, 0:m], ps[:, 1, :].rearrange("p (i c) -> p i c", c=P)[:, :, 0:m]).then_inc(ht_dve, 1)
                    dve.wait_ge(slot_used, g * NL + (j + 1) * PER)
                    store_rows(nc.vector.tensor_copy, j, (2, 3)).then_inc(y_dve, 1)

                def add(q):
                    outs = [(1 + t, h) for t in range(4) for h in range(4)] + ([(0, h) for h in range(4)] if q else [])
                    for o, (t, h) in enumerate(outs):
                        dve.wait_ge(comb, 36 * g + 16 * q + o + 1)
                        cols = slice(h * 512, (h + 1) * 512)
                        nc.vector.tensor_tensor(f[:, t, cols], ps[:, 4 + o % 4, :], f[:, t, cols], ALU.add).then_inc(added, 1)

                pair(0)
                take_gathered(0)
                scatter_matrices()
                hidden(0)
                outputs(0)
                pair(1)
                hidden(1)
                take_gathered(1)
                outputs(1)
                hidden(2)
                add(0)
                outputs(2)
                hidden(3)
                outputs(3)
                add(1)


def block_final(nc, x1_d, ffn_d, mod_d, g_post_ffn, y_prompt, y_sample):
    with ExitStack() as ctx:
        def sb(name, shape):
            return ctx.enter_context(nc.sbuf_tensor("fi_" + name, shape, F32))

        def sem(name):
            return nc.alloc_semaphore("fi_" + name)

        g2, gp = sb("g2", [P, 2, D]), sb("gp", [P, D])
        x, f, junk, st, eps = sb("x", [P, NT, D]), sb("f", [P, NT, D]), sb("junk", [P, D]), sb("st", [P, NT, 3]), sb("eps", [P, 1])
        once, made, ss, done, out = (sem(n) for n in ("once", "made", "ss", "done", "out"))
        loads = [sem(f"load{t}") for t in range(NT)]
        block = ctx.enter_context(nc.Block())

        @block.sync
        def _(sp):
            for t in range(NT):
                sp.dma_start(f[:, t, :], ffn_d[t]).then_inc(loads[t], 16)
                sp.dma_start(x[:, t, :], x1_d[t]).then_inc(loads[t], 16)
            for t in range(NT):
                sp.wait_ge(done, t + 1)
                sp.dma_start(y_prompt[0] if t == 0 else y_sample[0, (t - 1) * P:t * P, :], x[:, t, :]).then_inc(out, 16)
            sp.wait_ge(out, 16 * NT)

        @block.gpsimd
        def _(pool):
            pool.dma_start(gp[:], bcast_rows(g_post_ffn, 0, D)).then_inc(once, 16)
            for cnd in range(2):
                pool.dma_start(g2[:, cnd, :], bcast_rows(mod_d, cnd * 6 * D + 5 * D, D)).then_inc(once, 16)

        @block.scalar
        def _(act):
            act.wait_ge(made, 1)
            for t in range(NT):
                act.wait_ge(loads[t], 32)
                nc.scalar.activation(junk[:], f[:, t, :], ACT.Square, accum_out=st[:, t, 0:1]).then_inc(ss, 1)
                act.wait_ge(ss, 2 * t + 1)
                nc.scalar.activation(st[:, t, 1:2], st[:, t, 0:1], ACT.Sqrt, scale=1.0 / D, bias=eps[:]).then_inc(ss, 1)

        @block.vector
        def _(dve):
            link = Chain(dve, nc.alloc_semaphore("fi_ch")).link
            nc.vector.memset(eps[:], NORM_EPS).then_inc(made, 1)
            dve.wait_ge(once, 48)
            for cnd in range(2):
                last = nc.vector.tensor_tensor(g2[:, cnd, :], g2[:, cnd, :], gp[:], ALU.mult)
            link(last)
            for t in range(NT):
                dve.wait_ge(ss, 2 * t + 2)
                link(nc.vector.reciprocal(st[:, t, 2:3], st[:, t, 1:2]))
                link(nc.vector.scalar_tensor_tensor(f[:, t, :], f[:, t, :], st[:, t, 2:3], g2[:, min(t, 1), :], ALU.mult, ALU.mult))
                nc.vector.tensor_tensor(x[:, t, :], x[:, t, :], f[:, t, :], ALU.add).then_inc(done, 1)


def trunk(nc, a, s):
    with nc.cleanup_on_exit():
        trunk_mixers(nc, a, s)
    trunk_experts(nc, a, s)


def trunk_mixers(nc, a, s):
    block_modulation(nc, a["c"], a["c_ctx"], a["w_ada"], a["b_ada"], s["mod"], s["cond"], s["ident"])
    block_projection(nc, a["x_prompt"], a["x_sample"], a["g_pre_mix"], a["w_in"], a["w_ada"], a["b_ada"], s["cond"], s["mod"], s["ident"],
                     s["z"], s["v"], s["vs"])

    def channel_rows(ap):
        if ap.shape[-1] == DH:
            return ap.rearrange("a (k two) d -> (a k) (two d)", two=2)
        return ap.rearrange("a (k p) -> (a k) p" if len(ap.shape) == 2 else "a b (k p) -> (a b k) p", p=P)

    vectors = [(channel_rows(a[n]), NPAIR * (2 if n in ("rw_w0", "rw_a0") else 1))
               for n in ("rw_kk", "rw_ka", "rw_rk", "rw_ln_w", "rw_ln_b", "rw_w0", "rw_a0")]
    block_gating_and_keys(nc, s["z"], s["vs"], a["sg_gain"], a["sg_w"], a["sg_b"], vectors, a["na_rpb"], s["ident"], s["bias"], s["par"],
                          s["kk"], s["o"])
    flat = "a b c h d -> (a b c) (h d)"
    block_attention(nc, s["z"], s["v"], a["cache_k"].rearrange(flat), a["cache_v"].rearrange(flat), s["ident"],
                    s["bias"], s["o"], a["new_cache_k"].rearrange(flat), a["new_cache_v"].rearrange(flat))
    states = "a b d h v k -> (a b d) h v k"
    block_rwkv(nc, s["z"], s["kk"], s["par"], a["rw_w2"], a["rw_a2"], a["state_wkv"].rearrange(states), s["ident"],
               s["o_raw"], a["new_state_wkv"].rearrange(states))


def trunk_experts(nc, a, s):
    with ExitStack() as ctx:
        consts = ctx.enter_context(nc.sbuf_tensor("mix_consts", [P, 2, 3, D], F32))
        with nc.sbuf_tensor("w_out_ring", [P, 2, KD, 512], F32) as w_ring:
            w_got = [nc.alloc_semaphore(f"w_out_got{i}") for i in range(2)]
            block_rwkv_output(nc, s["z"], s["o_raw"], s["par"], a["rw_g2"], a["w_out"], w_ring, w_got, s["o"])
            block_output_projection(nc, s["o"], a["w_out"], w_ring, w_got, s["mod"], a["g_post_mix"], a["g_pre_ffn"], consts, s["mixed"])
        block_middle(nc, a["x_prompt"], a["x_sample"], s["mixed"], consts, a["w_router"],
                     s["ident"], s["x1"], s["h2"], s["aff"], s["afft"])
    with ExitStack() as ctx:
        h2 = ctx.enter_context(nc.sbuf_tensor("experts_h2", [P, NT, D], F32))
        ring = ctx.enter_context(nc.sbuf_tensor("experts_ring", [P, 6, 2048], F32))
        h2_in, slot_in = nc.alloc_semaphore("experts_h2_in"), [nc.alloc_semaphore(f"experts_slot{i}") for i in range(6)]
        weights = (a["w_gate"], a["w_up"], a["w_down"])
        block_select(nc, s["afft"], s["ident"], s["h2"], h2, h2_in, weights, ring, slot_in, s["slot"])
        block_experts(nc, h2, h2_in, s["aff"], s["slot"], s["ident"], weights, ring, slot_in, s["ffn"])
    block_final(nc, s["x1"], s["ffn"], s["mod"], a["g_post_ffn"], a["y_prompt"], a["y_sample"])


_INS = ["x_prompt", "x_sample", "cache_k", "cache_v", "state_wkv", "c", "c_ctx", "w_ada", "b_ada", "g_pre_mix", "g_post_mix",
        "g_pre_ffn", "g_post_ffn", "w_in", "na_rpb", "sg_gain", "sg_w", "sg_b", "rw_w0", "rw_w2", "rw_a0", "rw_a2", "rw_g2",
        "rw_kk", "rw_ka", "rw_rk", "rw_ln_w", "rw_ln_b", "w_out", "w_router", "w_gate", "w_up", "w_down"]
_OUTS = [("y_prompt", (1, TP, D)), ("y_sample", (1, TS, D)), ("new_cache_k", (1, 1, TP, NAH, DH)),
         ("new_cache_v", (1, 1, TP, NAH, DH)), ("new_state_wkv", (1, 1, 2, 16, DH, DH))]
_SCRATCH = [("mod", (2, 6 * D)), ("cond", (P, 2 * KD)), ("ident", (P, P)), ("z", (NZ, P, T)), ("v", (NT, P, NAW)), ("vs", (NT, P, 512)),
            ("bias", (NAH * 15, GRID_W * (2 * GRID_W - 1))), ("par", (P, 72)), ("kk", (NPAIR, P, T)), ("o", (KD, P, T)),
            ("o_raw", (NPAIR, P, T)), ("mixed", (NT, P, D)), ("x1", (NT, P, D)), ("h2", (NT, P, D)), ("aff", (P, NT, NE)),
            ("afft", (NE, T)), ("slot", (P, NT, NE)), ("ffn", (NT, P, D))]


def kernel(**inputs):
    import concourse.bacc as bacc
    from concourse.bass_utils import run_bass_kernel_spmd

    nc = bacc.Bacc("TRN2", target_bir_lowering=False, num_devices=1)
    arrays, aps = {}, {}
    for name in _INS:
        x = np.ascontiguousarray(inputs[name])
        arrays[f"in_{name}"] = x
        aps[name] = nc.dram_tensor(f"in_{name}", x.shape, mybir.dt.from_np(x.dtype), kind="ExternalInput").ap()
    for name, shape in _OUTS:
        aps[name] = nc.dram_tensor(f"out_{name}", shape, F32, kind="ExternalOutput").ap()
    scratch = {name: nc.dram_tensor(f"scratch_{name}", shape, F32).ap() for name, shape in _SCRATCH}
    trunk(nc, aps, scratch)
    r = run_bass_kernel_spmd(nc, [arrays], core_ids=[0])
    return tuple(r.results[0][f"out_{name}"] for name, _ in _OUTS)
```
